# Optimizing a Trainium2 kernel written in Bass

```python
import jax, jax.numpy as jnp
from jax import lax
import numpy as np

D_MODEL = 1024
BATCH = 1
SEQ = 1024
DEPTH = 1

GRID_W = 64
CTX_LEN = 256
D_RNN = D_MODEL
LRU_BLOCKS = 8
LRU_BLOCK_W = D_RNN // LRU_BLOCKS
LRU_CONV_W = 4
LRU_CONV_LEFT = 2
LRU_C = 8.0
NA_HEADS = 16
HEAD_DIM = 64
D_ATT = NA_HEADS * HEAD_DIM
NA_ROWS = 8
NA_COLS = 16
ROPE_BASE = 10000.0
D_FF = ((8 * D_MODEL // 3 + 127) // 128) * 128
FFN_CONV_W = 3
FFN_CONV_LEFT = 1
N_MOD = 6
EPS = 1e-6
NEG_INF = -1e30
IN_SPLITS = (D_RNN, D_RNN + D_ATT, D_RNN + 2 * D_ATT, 2 * D_RNN + 2 * D_ATT, 2 * D_RNN + 3 * D_ATT, 2 * D_RNN + 3 * D_ATT + D_MODEL)
IN_COLS = 2 * D_RNN + 3 * D_ATT + 2 * D_MODEL
CTX_KV_COLS = D_RNN + 2 * D_ATT

kernel_name = 'hybrid_rglru_natten_dit_block'

def rms_norm(x, g):
    xf = x.astype(jnp.float32)
    y = xf * lax.rsqrt(jnp.mean(xf * xf, axis=-1, keepdims=True) + EPS)
    return (y * g).astype(x.dtype)

def modulate(x, g, shift, scale):
    return rms_norm(x, g) * (1 + scale) + shift

def split_heads(t):
    b, n, _ = t.shape
    return t.reshape(b, n, NA_HEADS, HEAD_DIM)

def head_rms(t, g):
    return rms_norm(split_heads(t), g)

def dwconv(x, w, b, left):
    k_w, ch = w.shape
    y = lax.conv_general_dilated(x, w[:, None, :], window_strides=(1,), padding=[(left, k_w - 1 - left)],
                                 dimension_numbers=('NWC', 'WIO', 'NWC'), feature_group_count=ch)
    return y + b

def _rotate(x, pos):
    n = x.shape[-1] // 2
    freq = ROPE_BASE ** (-jnp.arange(n, dtype=jnp.float32) / n)
    ang = pos.astype(jnp.float32)[:, None] * freq
    cos = jnp.cos(ang)[None, :, None, :]
    sin = jnp.sin(ang)[None, :, None, :]
    x1 = x[..., :n].astype(jnp.float32)
    x2 = x[..., n:].astype(jnp.float32)
    return jnp.concatenate([x1 * cos - x2 * sin, x2 * cos + x1 * sin], axis=-1).astype(x.dtype)

def rope_2d(x, row_pos, col_pos):
    h = x.shape[-1] // 2
    return jnp.concatenate([_rotate(x[..., :h], row_pos), _rotate(x[..., h:], col_pos)], axis=-1)

def rglru_coeffs(xc, wa, ba, wx, bx, lam):
    b_, t_, ch = xc.shape
    xb = xc.reshape(b_, t_, LRU_BLOCKS, LRU_BLOCK_W)
    r = jax.nn.sigmoid((jnp.einsum('btnk,nkj->btnj', xb, wa).reshape(b_, t_, ch) + ba).astype(jnp.float32))
    i = jax.nn.sigmoid((jnp.einsum('btnk,nkj->btnj', xb, wx).reshape(b_, t_, ch) + bx).astype(jnp.float32))
    log_a = -LRU_C * r * jax.nn.softplus(-lam.astype(jnp.float32))
    a = jnp.exp(log_a)
    b = jnp.sqrt(-jnp.expm1(2.0 * log_a)) * i * xc.astype(jnp.float32)
    return a, b

def _lin_combine(left, right):
    a_l, b_l = left
    a_r, b_r = right
    return a_l * a_r, a_r * b_l + b_r

def linear_scan(a, b, h0=None):
    a_cum, h = lax.associative_scan(_lin_combine, (a, b), axis=1)
    if h0 is None:
        return h
    return h + a_cum * h0[:, None, :]

def rglru_bidirectional(x_lat, x_ctx, wa, ba, wx, bx, lam, need_ctx_out):
    lat_seqs, ctx_seqs = [], []
    for d in range(2):
        a_c, b_c = rglru_coeffs(x_ctx, wa[d], ba[d], wx[d], bx[d], lam[d])
        a_x, b_x = rglru_coeffs(x_lat, wa[d], ba[d], wx[d], bx[d], lam[d])
        if d == 1:
            a_c, b_c, a_x, b_x = [jnp.flip(t, axis=1) for t in (a_c, b_c, a_x, b_x)]
        h_c = linear_scan(a_c, b_c)
        h_x = linear_scan(a_x, b_x, h_c[:, -1])
        if d == 1:
            h_x = jnp.flip(h_x, axis=1)
        lat_seqs.append(h_x)
        if need_ctx_out:
            ctx_seqs.append(jnp.flip(h_c, axis=1) if d == 1 else h_c)
    h_lat = (lat_seqs[0] + lat_seqs[1]).astype(x_lat.dtype)
    h_ctx = (ctx_seqs[0] + ctx_seqs[1]).astype(x_ctx.dtype) if need_ctx_out else None
    return h_lat, h_ctx

def neighborhood_attention(q_rot, q_plain, k_rot, v, k_ctx, v_ctx, rpb):
    b_, t_, h_, dh = q_rot.shape
    rows = t_ // GRID_W
    kh = min(NA_ROWS, rows)
    r = jnp.arange(rows)
    row_start = jnp.clip(r - kh // 2, 0, rows - kh)
    row_idx = row_start[:, None] + jnp.arange(kh)[None, :]
    cidx = jnp.arange(GRID_W)
    col_start = jnp.clip(cidx - NA_COLS // 2, 0, GRID_W - NA_COLS)
    in_win = (cidx[None, :] >= col_start[:, None]) & (cidx[None, :] < col_start[:, None] + NA_COLS)
    dr = row_idx - r[:, None] + (NA_ROWS - 1)
    dc = jnp.clip(cidx[None, :] - cidx[:, None], -(NA_COLS - 1), NA_COLS - 1) + (NA_COLS - 1)
    bias = rpb[:, dr[:, None, :, None], dc[None, :, None, :]]
    bias = jnp.where(in_win[None, None, :, None, :], bias, NEG_INF)
    qg = q_rot.reshape(b_, rows, GRID_W, h_, dh)
    kb = k_rot.reshape(b_, rows, GRID_W, h_, dh)[:, row_idx]
    vb = v.reshape(b_, rows, GRID_W, h_, dh)[:, row_idx]
    scale = dh ** -0.5
    s_lat = jnp.einsum('brchd,brikhd->bhrcik', qg, kb).astype(jnp.float32) * scale + bias[None]
    s_ctx = jnp.einsum('brchd,bnhd->bhrcn', q_plain.reshape(b_, rows, GRID_W, h_, dh), k_ctx).astype(jnp.float32) * scale
    n_lat = kh * GRID_W
    s = jnp.concatenate([s_lat.reshape(b_, h_, rows, GRID_W, n_lat), s_ctx], axis=-1)
    p = jax.nn.softmax(s, axis=-1)
    p_lat = p[..., :n_lat].reshape(b_, h_, rows, GRID_W, kh, GRID_W).astype(v.dtype)
    p_ctx = p[..., n_lat:].astype(v.dtype)
    o = jnp.einsum('bhrcik,brikhd->brchd', p_lat, vb) + jnp.einsum('bhrcn,bnhd->brchd', p_ctx, v_ctx)
    return o.reshape(b_, t_, h_ * dh)

def context_attention(q, k, v):
    b_, n_, h_, dh = q.shape
    s = jnp.einsum('bnhd,bmhd->bhnm', q, k).astype(jnp.float32) * (dh ** -0.5)
    p = jax.nn.softmax(s, axis=-1).astype(v.dtype)
    return jnp.einsum('bhnm,bmhd->bnhd', p, v).reshape(b_, n_, h_ * dh)

def merge_branches(y_rnn, y_na, g_rnn, g_na, w_rnn_out, w_na_out, w_out):
    merged = jax.nn.sigmoid(g_rnn) * (y_rnn @ w_rnn_out) + jax.nn.sigmoid(g_na) * (y_na @ w_na_out)
    return merged @ w_out

def conv_ffn(xn, w_up, conv_w, conv_b, w_down):
    h = dwconv(xn @ w_up, conv_w, conv_b, FFN_CONV_LEFT)
    a, g = jnp.split(h, 2, axis=-1)
    return (jax.nn.silu(a) * g) @ w_down

def setup_inputs(seed: int = 0) -> dict:
    key = jax.random.key(seed)
    ks = jax.random.split(key, 32)
    L = DEPTH

    def nrm(k, shape, scale):
        return jax.random.normal(k, shape, jnp.float32) * scale

    a0 = jax.random.uniform(ks[15], (L, 2, D_RNN), jnp.float32, 0.9, 0.999)
    return {
        'x': nrm(ks[0], (BATCH, SEQ, D_MODEL), 1.0),
        'c': nrm(ks[1], (BATCH, D_MODEL), 1.0),
        'ctx': nrm(ks[2], (BATCH, CTX_LEN, D_MODEL), 1.0),
        'c_ctx': nrm(ks[3], (D_MODEL,), 1.0),
        'w_mod': nrm(ks[4], (L, D_MODEL, N_MOD * D_MODEL), 0.5 * D_MODEL ** -0.5),
        'b_mod': nrm(ks[5], (L, N_MOD * D_MODEL), 0.02),
        'norm_mix_g': 1.0 + nrm(ks[6], (L, D_MODEL), 0.02),
        'norm_ffn_g': 1.0 + nrm(ks[7], (L, D_MODEL), 0.02),
        'w_in': nrm(ks[8], (L, D_MODEL, IN_COLS), D_MODEL ** -0.5),
        'lru_conv_w': nrm(ks[9], (L, LRU_CONV_W, D_RNN), LRU_CONV_W ** -0.5),
        'lru_conv_b': nrm(ks[10], (L, D_RNN), 0.02),
        'lru_wa': nrm(ks[11], (L, 2, LRU_BLOCKS, LRU_BLOCK_W, LRU_BLOCK_W), LRU_BLOCK_W ** -0.5),
        'lru_ba': nrm(ks[12], (L, 2, D_RNN), 0.02),
        'lru_wx': nrm(ks[13], (L, 2, LRU_BLOCKS, LRU_BLOCK_W, LRU_BLOCK_W), LRU_BLOCK_W ** -0.5),
        'lru_bx': nrm(ks[14], (L, 2, D_RNN), 0.02),
        'lru_lambda': jnp.log(a0) - jnp.log1p(-a0),
        'q_norm_g': 1.0 + nrm(ks[16], (L, HEAD_DIM), 0.02),
        'k_norm_g': 1.0 + nrm(ks[17], (L, HEAD_DIM), 0.02),
        'na_rpb': nrm(ks[18], (L, NA_HEADS, 2 * NA_ROWS - 1, 2 * NA_COLS - 1), 0.1),
        'w_rnn_out': nrm(ks[19], (L, D_RNN, D_MODEL), D_RNN ** -0.5),
        'w_na_out': nrm(ks[20], (L, D_ATT, D_MODEL), D_ATT ** -0.5),
        'w_out': nrm(ks[21], (L, D_MODEL, D_MODEL), D_MODEL ** -0.5),
        'w_up': nrm(ks[22], (L, D_MODEL, 2 * D_FF), D_MODEL ** -0.5),
        'ffn_conv_w': nrm(ks[23], (L, FFN_CONV_W, 2 * D_FF), FFN_CONV_W ** -0.5),
        'ffn_conv_b': nrm(ks[24], (L, 2 * D_FF), 0.02),
        'w_down': nrm(ks[25], (L, D_FF, D_MODEL), D_FF ** -0.5),
    }

def reference(x, c, ctx, c_ctx, w_mod, b_mod, norm_mix_g, norm_ffn_g, w_in, lru_conv_w, lru_conv_b,
              lru_wa, lru_ba, lru_wx, lru_bx, lru_lambda, q_norm_g, k_norm_g, na_rpb,
              w_rnn_out, w_na_out, w_out, w_up, ffn_conv_w, ffn_conv_b, w_down):
    seq = x.shape[1]
    t = jnp.arange(seq)
    row_pos = t // GRID_W
    col_pos = t % GRID_W
    s_c = jax.nn.silu(c)
    s_ctx = jax.nn.silu(c_ctx)
    for l in range(DEPTH):
        last = l == DEPTH - 1
        mx = jnp.split((s_c @ w_mod[l] + b_mod[l])[:, None, :], N_MOD, axis=-1)
        mc = jnp.split((s_ctx @ w_mod[l] + b_mod[l])[None, None, :], N_MOD, axis=-1)
        xn = modulate(x, norm_mix_g[l], mx[0], mx[1])
        cn = modulate(ctx, norm_mix_g[l], mc[0], mc[1])
        xr, kx, vx, gx, qx, mrx, mnx = jnp.split(xn @ w_in[l], list(IN_SPLITS), axis=-1)
        if last:
            cr, kc, vc = jnp.split(cn @ w_in[l][:, :CTX_KV_COLS], [D_RNN, D_RNN + D_ATT], axis=-1)
        else:
            cr, kc, vc, gc, qc, mrc, mnc = jnp.split(cn @ w_in[l], list(IN_SPLITS), axis=-1)
        xr = dwconv(xr, lru_conv_w[l], lru_conv_b[l], LRU_CONV_LEFT)
        cr = dwconv(cr, lru_conv_w[l], lru_conv_b[l], LRU_CONV_LEFT)
        h_x, h_c = rglru_bidirectional(xr, cr, lru_wa[l], lru_ba[l], lru_wx[l], lru_bx[l], lru_lambda[l], not last)
        y_rnn_x = h_x * jax.nn.gelu(gx)
        qx = head_rms(qx, q_norm_g[l])
        kx = head_rms(kx, k_norm_g[l])
        kc = head_rms(kc, k_norm_g[l])
        vx = split_heads(vx)
        vc = split_heads(vc)
        y_na_x = neighborhood_attention(rope_2d(qx, row_pos, col_pos), qx, rope_2d(kx, row_pos, col_pos),
                                        vx, kc, vc, na_rpb[l])
        x = x + mx[2] * merge_branches(y_rnn_x, y_na_x, mrx, mnx, w_rnn_out[l], w_na_out[l], w_out[l])
        x = x + mx[5] * conv_ffn(modulate(x, norm_ffn_g[l], mx[3], mx[4]), w_up[l], ffn_conv_w[l], ffn_conv_b[l], w_down[l])
        if not last:
            y_rnn_c = h_c * jax.nn.gelu(gc)
            y_na_c = context_attention(head_rms(qc, q_norm_g[l]), kc, vc)
            ctx = ctx + mc[2] * merge_branches(y_rnn_c, y_na_c, mrc, mnc, w_rnn_out[l], w_na_out[l], w_out[l])
            ctx = ctx + mc[5] * conv_ffn(modulate(ctx, norm_ffn_g[l], mc[3], mc[4]), w_up[l], ffn_conv_w[l], ffn_conv_b[l], w_down[l])
    return x


_drawn_inputs = setup_inputs


def setup_inputs(seed=0):
    import zlib

    import numpy as np

    out = dict(_drawn_inputs(seed))
    spreads = {}
    factors = {'ctx': 4.167,
     'norm_mix_g': 8.0,
     'norm_ffn_g': 8.0,
     'lru_conv_b': 5.432,
     'lru_ba': 8.0,
     'lru_bx': 8.0,
     'q_norm_g': 8.0,
     'k_norm_g': 8.0,
     'na_rpb': 39.143,
     'ffn_conv_b': 8.0}
    for name, (base, spread) in spreads.items():
        noise = np.random.default_rng([zlib.crc32(name.encode()), seed]).standard_normal(out[name].shape)
        drawn = base * np.exp(spread * noise) if base else spread * noise
        out[name] = __import__('jax').numpy.asarray(drawn.astype(out[name].dtype))
    for name, factor in factors.items():
        out[name] = (out[name] * factor).astype(out[name].dtype)
    return out
```

```python
from contextlib import ExitStack

import numpy as np

import concourse.bass as bass
from concourse import mybir

F32 = mybir.dt.float32
F32R = mybir.dt.float32r
ALU = mybir.AluOpType
ACT = mybir.ActivationFunctionType
AX_X = mybir.AxisListType.X

P = 128
D = 1024
KC = D // P
T = 1024
C = 256
N = C + T
GW = 64
HD = 64
PAIRS = KC
NT = T // P
NCT = C // P
WIN = 8
FF = 2816
FC = FF // P
GROUPS = (8, 7, 7)
UP_UNITS = 2 * FC
FF_UNITS = UP_UNITS + KC * len(GROUPS)
EPS = 1e-6
NEG = -1e30
HALF = 512
assert sum(GROUPS) == FC

KEY_ROW0 = [min(max(2 * t - WIN // 2, 0), 2 * NT - WIN) for t in range(NT)]
KEY_ROWS = [9 if 2 <= t <= 5 else 8 for t in range(NT)]
BIAS_ROW0 = [KEY_ROW0[t] - 2 * t + WIN - 1 for t in range(NT)]
BIAS_ROWS = 14


def three_passes(pe, out, w_hi, w_lo, x_hi, x_lo, chunks):
    last = None
    for k in range(chunks):
        pe.matmul(out, w_hi(k), x_hi(k), start=(k == 0), stop=False)
        pe.matmul(out, w_hi(k), x_lo(k), start=False, stop=False)
        last = pe.matmul(out, w_lo(k), x_hi(k), start=False, stop=(k == chunks - 1))
    return last


def build(nc, xT, ctxT, svec, w_mod, b_mod, gains, w_fm, w_qkv, lru_w, lru_p, qk_g, rpb,
          w_mix, w_ff, ffn_p, consts, neg_row, outT, yr_d, yn_d, smr_d, smn_d, bias_d):
    with ExitStack() as top:
        def sem(name):
            return top.enter_context(nc.semaphore(name))

        def sbuf(stack, name, shape, dt=F32):
            return stack.enter_context(nc.sbuf_tensor(name, shape, dt))

        def psum(stack, name, shape):
            return stack.enter_context(nc.psum_tensor(name, shape, F32))

        mod = sbuf(top, "mod", [P, 6 * KC, 2])
        gain = sbuf(top, "gain", [P, 2, KC])
        ones = sbuf(top, "ones", [P, P])
        eps = sbuf(top, "eps", [P, 1])
        lrup = sbuf(top, "lrup", [P, 11, KC])
        decay = sbuf(top, "decay", [P, 2, 2, KC])
        ab = ExitStack()
        xnh = sbuf(ab, "xnh", [P, KC, N], F32R)
        xnl = sbuf(ab, "xnl", [P, KC, N], F32R)
        setup_block(nc, sem, sbuf, psum, xT, ctxT, svec, w_mod, b_mod, gains, lru_p,
                    mod, gain, ones, eps, lrup, decay, xnh, xnl, rpb, bias_d)
        mixer_block(nc, sem, sbuf, psum, w_fm, w_qkv, lru_w, qk_g, bias_d, consts, neg_row,
                    eps, lrup, decay, xnh, xnl, yr_d, yn_d, smr_d, smn_d)
        ab.close()
        with ExitStack() as cd:
            x1 = sbuf(cd, "x1", [P, KC, T])
            merge_block(nc, sem, sbuf, psum, xT, w_mix, mod, x1, yr_d, yn_d, smr_d, smn_d)
            ffn_block(nc, sem, sbuf, psum, w_ff, ffn_p, mod, gain, ones, eps, x1, outT)


def setup_block(nc, sem, sbuf, psum, xT, ctxT, svec, w_mod, b_mod, gains, lru_p,
                mod, gain, ones, eps, lrup, decay, xnh, xnl, rpb, bias_d):
    SL = 8
    with ExitStack() as st:
        xs = sbuf(st, "xs", [P, KC, N])
        sq = sbuf(st, "sq", [P, 2, N])
        rs = sbuf(st, "rs", [P, N])
        tmp = sbuf(st, "tmp_norm", [P, N])
        wm = sbuf(st, "wm", [P, SL, KC, P])
        sv = sbuf(st, "sv", [P, KC, 2])
        bm = sbuf(st, "bm", [P, 6 * KC])
        gm = sbuf(st, "gm", [P, 2, KC])
        la = sbuf(st, "la", [P, 6, 2, KC])
        ss = psum(st, "ss", [P, 3, HALF])
        mp = psum(st, "mp", [P, SL, 2])

        small_in = sem("a_small_in")
        x_in = [sem(f"a_x_in{k}") for k in range(KC)]
        wm_in = [sem(f"a_wm_in{s}") for s in range(SL)]
        memset_done = sem("a_memset")
        silu_done = sem("a_silu")
        squared = sem("a_squared")
        sq_used = sem("a_sq_used")
        mod_ready = sem("a_mod_ready")
        mod_out = sem("a_mod_out")
        root = sem("a_root")
        scaled = sem("a_scaled")
        hi_done = sem("a_hi")
        dve_step = sem("a_dve_step")
        bias_set = [sem(f"a_bias_set{n}") for n in range(2)]
        lam_abs = sem("a_lam_abs")
        lam_exp = sem("a_lam_exp")
        groups = 6 * KC // SL

        with nc.Block() as block:
            @block.sync
            def _(sp):
                sp.dma_start(sv[:, :, :], svec).then_inc(small_in, 16)
                sp.dma_start(bm[:, :], b_mod).then_inc(small_in, 16)
                sp.dma_start(gain[:, :, :], gains).then_inc(small_in, 16)
                sp.dma_start(lrup[:, :, :], lru_p).then_inc(small_in, 16)
                for k in range(KC):
                    sp.dma_start(xs[:, k, 0:C], ctxT[k]).then_inc(x_in[k], 16)
                    sp.dma_start(xs[:, k, C:N], xT[k]).then_inc(x_in[k], 16)
                for s in range(SL):
                    sp.dma_start(wm[:, s, :, :], w_mod[s]).then_inc(wm_in[s], 16)
                for lower in range(2):
                    src = bass.AP(tensor=rpb.tensor, offset=(1 - lower) * P + GW - 1,
                                  ap=[[P, 2 * PAIRS * 16], [-1, GW], [1, GW]])
                    sp.dma_start(bias_d[GW * lower:GW * lower + GW].rearrange("p h e c -> (h e) p c"), src)\
                      .then_inc(bias_set[lower], 16)
                with sp.Fori(1, groups) as g:
                    sp.wait_ge(mod_ready, g)
                    for s in range(SL):
                        sp.dma_start(wm[:, s, :, :], w_mod[bass.ds(g * SL + s, 1)]).then_inc(wm_in[s], 16)
                for lower in range(2):
                    sp.wait_ge(bias_set[lower], 16)

            @block.gpsimd
            def _(pool):
                pool.memset(ones[:, :], 1.0).then_inc(memset_done, 1)
                pool.memset(eps[:, :], EPS).then_inc(memset_done, 1)

            @block.tensor
            def _(pe):
                pe.wait_ge(memset_done, 2)
                for k in range(KC):
                    pe.wait_ge(squared, k + 1)
                    for b, (c0, c1) in enumerate(((0, 512), (512, 1024), (1024, N))):
                        last = pe.matmul(ss[:, b, 0:c1 - c0], ones[:, :], sq[:, k % 2, c0:c1],
                                         start=(k == 0), stop=(k == KC - 1))
                    last.then_inc(sq_used, 1)
                pe.wait_ge(silu_done, 1)
                with pe.Fori(0, groups) as g:
                    pe.wait_ge(mod_out, g)
                    for s in range(SL):
                        pe.wait_ge(wm_in[s], g * 16 + 16)
                        for k in range(KC):
                            last = pe.matmul(mp[:, s, :], wm[:, s, k, :], sv[:, k, :],
                                             start=(k == 0), stop=(k == KC - 1))
                    last.then_inc(mod_ready, 1)

            @block.scalar
            def _(act):
                act.wait_ge(small_in, 64)
                act.activation(sv[:, :, :], sv[:, :, :], ACT.Silu).then_inc(silu_done, 1)
                act.wait_ge(lam_abs, 1)
                act.activation(la[:, 1], la[:, 0], ACT.Exp).then_inc(lam_exp, 1)
                for k in range(KC):
                    act.wait_ge(x_in[k], 32)
                    if k >= 2:
                        act.wait_ge(sq_used, k - 1)
                    act.activation(sq[:, k % 2, :], xs[:, k, :], ACT.Square).then_inc(squared, 1)
                act.wait_ge(sq_used, KC)
                act.activation(tmp[:, :], ss[:, :, :].rearrange("p a b -> p (a b)")[:, 0:N], ACT.Sqrt,
                               bias=eps[:, :], scale=1.0 / D).then_inc(root, 1)
                for k in range(KC):
                    act.wait_ge(scaled, k + 1)
                    act.activation(xnh[:, k, 0:C], xs[:, k, 0:C], ACT.Identity, bias=mod[:, k, 1:2])
                    act.activation(xnh[:, k, C:N], xs[:, k, C:N], ACT.Identity, bias=mod[:, k, 0:1])\
                       .then_inc(hi_done, 1)

            @block.vector
            def _(dve):
                steps = [0]

                def then(ins):
                    steps[0] += 1
                    ins.then_inc(dve_step, 1)
                    dve.wait_ge(dve_step, steps[0])

                dve.wait_ge(small_in, 64)
                lam = lrup[:, 9:11, :]
                dve.scalar_tensor_tensor(la[:, 0], lam, -1.0, lam, ALU.mult, ALU.min).then_inc(lam_abs, 1)
                dve.wait_ge(lam_exp, 1)
                then(dve.tensor_scalar(la[:, 2], la[:, 1], 2.0, None, ALU.add))
                then(dve.reciprocal(la[:, 2], la[:, 2]))
                then(dve.tensor_tensor(la[:, 2], la[:, 1], la[:, 2], ALU.mult))
                then(dve.tensor_tensor(la[:, 3], la[:, 2], la[:, 2], ALU.mult))
                then(dve.tensor_scalar(la[:, 4], la[:, 3], 1.0 / 15, None, ALU.mult))
                for odd in (13, 11, 9, 7, 5, 3):
                    then(dve.scalar_tensor_tensor(la[:, 4], la[:, 4], 1.0 / odd, la[:, 3], ALU.add, ALU.mult))
                then(dve.scalar_tensor_tensor(la[:, 4], la[:, 4], 1.0, la[:, 2], ALU.add, ALU.mult))
                then(dve.tensor_scalar(la[:, 5], lam, -1.0, 0.0, ALU.mult, ALU.max))
                then(dve.scalar_tensor_tensor(la[:, 5], la[:, 4], 2.0, la[:, 5], ALU.mult, ALU.add))
                then(dve.tensor_scalar(decay[:, 0], la[:, 5], -8.0, None, ALU.mult))
                then(dve.tensor_scalar(decay[:, 1], la[:, 5], 8.0, None, ALU.mult))

                def mod_group(g):
                    dve.wait_ge(mod_ready, g + 1)
                    return dve.tensor_tensor(mod[:, bass.ds(g * SL, SL), :], mp[:, :, :],
                                             bm[:, bass.ds(g * SL, SL)].unsqueeze(2).broadcast_to([P, SL, 2]),
                                             ALU.add).then_inc(mod_out, 1)

                mod_group(0)
                mod_group(1)
                dve.wait_ge(mod_out, 2)
                for w in range(2):
                    then(dve.scalar_tensor_tensor(gm[:, w, :], mod[:, KC:2 * KC, w], 1.0, gain[:, 0, :],
                                                  ALU.add, ALU.mult))
                dve.wait_ge(root, 1)
                then(dve.reciprocal(rs[:, :], tmp[:, :]))
                then(dve.tensor_scalar(tmp[:, :], ss[:, :, :].rearrange("p a b -> p (a b)")[:, 0:N],
                                       -0.5 / D, -0.5 * EPS, ALU.mult, ALU.add))
                then(dve.tensor_tensor(tmp[:, :], tmp[:, :], rs[:, :], ALU.mult))
                then(dve.tensor_tensor(tmp[:, :], tmp[:, :], rs[:, :], ALU.mult))
                then(dve.scalar_tensor_tensor(rs[:, :], tmp[:, :], 1.5, rs[:, :], ALU.add, ALU.mult))
                for k in range(KC + 1):
                    if k < KC:
                        dve.scalar_tensor_tensor(xs[:, k, 0:C], xs[:, k, 0:C], gm[:, 1, k:k + 1], rs[:, 0:C],
                                                 ALU.mult, ALU.mult)
                        dve.scalar_tensor_tensor(xs[:, k, C:N], xs[:, k, C:N], gm[:, 0, k:k + 1], rs[:, C:N],
                                                 ALU.mult, ALU.mult).then_inc(scaled, 1)
                    if k >= 1:
                        j = k - 1
                        dve.wait_ge(scaled, k)
                        dve.wait_ge(hi_done, k)
                        dve.scalar_tensor_tensor(xnl[:, j, 0:C], xs[:, j, 0:C], mod[:, j, 1:2],
                                                 xnh[:, j, 0:C].bitcast(F32), ALU.add, ALU.subtract)
                        dve.scalar_tensor_tensor(xnl[:, j, C:N], xs[:, j, C:N], mod[:, j, 0:1],
                                                 xnh[:, j, C:N].bitcast(F32), ALU.add, ALU.subtract)
                with dve.Fori(2, groups) as g:
                    mod_group(g)


XR, Q0, Q1, Q2, G, MR, MN = range(7)
RAW_SLOT = [0, 1, 2, 0, 1, 2, 1]
RAW_USE = [(0, 2), (0, 3), (0, 2), (1, 2), (1, 3), (1, 2), (2, 3)]
UNITS = 7
F_USES = 21
Q_TILES = NT + NCT
ATT = 2 * NT


def mixer_block(nc, sem, sbuf, psum, w_fm, w_qkv, lru_w, qk_g, bias_d, consts, neg_row,
                eps, lrup, decay, xnh, xnl, yr_d, yn_d, smr_d, smn_d):
    with ExitStack() as st:
        raw = sbuf(st, "raw", [P, 3, 1024])
        fh = sbuf(st, "fh", [P, 2, KC, P], F32R)
        fl = sbuf(st, "fl", [P, 2, KC, P], F32R)
        qh = sbuf(st, "qh", [P, KC, 384], F32R)
        ql = sbuf(st, "ql", [P, KC, 384], F32R)
        qkv = sbuf(st, "qkv", [P, Q_TILES, 384])
        pad = sbuf(st, "pad", [P, 1288])
        xc = sbuf(st, "xc", [P, N])
        gR = sbuf(st, "gR", [P, N])
        gI = sbuf(st, "gI", [P, N])
        gA = sbuf(st, "gA", [P, N])
        gD = sbuf(st, "gD", [P, N])
        h0 = sbuf(st, "h0", [P, N])
        gel = sbuf(st, "gel", [P, T])
        stage = sbuf(st, "stage", [P, HALF])
        kcT = sbuf(st, "kcT", [P, C])
        bias = sbuf(st, "bias", [P, 2, BIAS_ROWS, GW])
        cst = sbuf(st, "cst", [P, P + GW + 2 * NT * HD])
        negr = sbuf(st, "negr", [1, 2 * P + GW])
        gqk = sbuf(st, "gqk", [P, 2, HD])
        sqs = sbuf(st, "sqs", [P, 2, 256])
        ssq = sbuf(st, "ssq", [P, Q_TILES, 4])
        rstd = sbuf(st, "rstd", [P, 2, Q_TILES, 4])
        lw = sbuf(st, "lw", [P, 4, P])
        lp = sbuf(st, "lp", [P, 15])
        stat = sbuf(st, "stat", [P, ATT, 5])
        ysc = sbuf(st, "ysc", [P, ATT, 2])
        qrot, krot, swp = gR[:, 0:T], gI[:, 0:T], gA[:, 0:T]
        qrotT, krotT, qplT = pad[:, 261:261 + T], xc[:, 0:T], h0[:, 0:T]
        prob = [gA[:, 0:832], gR[:, 0:832]]
        probT1 = sbuf(st, "probT1", [P, 7 * P])
        probT = [x[:, 0:7 * P].rearrange("p (a b) -> p a b", b=P) for x in (gI, probT1)]
        ytok = gD[:, HALF:2 * HALF].rearrange("p (a b) -> p a b", b=P)
        yT = gD[:, 0:HALF]
        ident = cst[:, 0:P]
        colmask = cst[:, P:P + GW]
        cosT = cst[:, P + GW:P + GW + NT * HD].rearrange("p (t f) -> p t f", f=HD)
        sinT = cst[:, P + GW + NT * HD:].rearrange("p (t f) -> p t f", f=HD)

        f_ps = [psum(st, f"f_ps{b}", [P, HALF]) for b in range(2)]
        q_ps = [psum(st, f"q_ps{b}", [P, HALF]) for b in range(2)]
        t_ps = [psum(st, f"t_ps{b}", [P, HALF]) for b in range(2)]
        o_ps = [psum(st, f"o_ps{b}", [P, HALF]) for b in range(2)]

        raw_in = [sem(f"b_raw_in{s}") for s in range(3)]
        w_hi = sem("b_w_hi")
        w_lo = sem("b_w_lo")
        f_full = sem("b_f_full")
        f_free = sem("b_f_free")
        q_full = sem("b_q_full")
        q_free = sem("b_q_free")
        sq_used = sem("b_sq_used")
        conv_done = sem("b_conv_done")
        lw_in = sem("b_lw_in")
        decayed = sem("b_decayed")
        one_minus = sem("b_one_minus")
        rooted = sem("b_rooted")
        gates_free = sem("b_gates_free")
        dve_step = sem("b_dve_step")
        rms_root = sem("b_rms_root")
        yr_ready = sem("b_yr_ready")
        yr_out = sem("b_yr_out")
        stage_out = sem("b_stage_out")
        rope_q = sem("b_rope_q")
        rope_k = sem("b_rope_k")
        tr_full = sem("b_tr_full")
        tr_act = sem("b_tr_act")
        tr_dve = sem("b_tr_dve")
        bias_in = sem("b_bias_in")
        bias_done = sem("b_bias_done")
        const_in = sem("b_const_in")
        set_done = sem("b_set_done")
        qk_done = sem("b_qk_done")
        bound_done = sem("b_bound_done")
        bound_step = sem("b_bound_step")
        exp_done = sem("b_exp_done")
        pt_full = sem("b_pt_full")
        pt_dve = sem("b_pt_dve")
        pt_act = sem("b_pt_act")
        pv_done = sem("b_pv_done")
        y_step = sem("b_y_step")
        y_done = sem("b_y_done")
        yt_full = sem("b_yt_full")
        yt_ready = sem("b_yt_ready")
        yt_out = sem("b_yt_out")

        def hi_parts(u):
            if u in (Q0, Q1, Q2):
                j = u - Q0
                return (qh[:, :, :].rearrange("p k c -> p (k c)")[:, 1024 * j:1024 * j + 1024],
                        ql[:, :, :].rearrange("p k c -> p (k c)")[:, 1024 * j:1024 * j + 1024])
            s = 0 if u in (XR, MR) else 1
            return (fh[:, s, :, :].rearrange("p k c -> p (k c)"), fl[:, s, :, :].rearrange("p k c -> p (k c)"))

        def raw_wait(eng, u, i):
            use, uses = RAW_USE[u]
            eng.wait_ge(raw_in[RAW_SLOT[u]], (i * uses + use + 1) * 16)

        SEGS = ((0, C), (C, C + HALF), (C + HALF, N))

        with nc.Block() as block:
            @block.sync
            def _(sp):
                sp.dma_start(cst[:, :], consts).then_inc(const_in, 16)
                sp.dma_start(negr[:, :], neg_row).then_inc(const_in, 16)
                sp.dma_start(gqk[:, :, :], bass.AP(tensor=qk_g.tensor, offset=0, ap=[[0, P], [HD, 2], [1, HD]]))\
                  .then_inc(const_in, 16)

                def load(u, i):
                    if u in (Q0, Q1, Q2):
                        src = w_qkv[bass.ds(i, 1), :, 1024 * (u - Q0):1024 * (u - Q0) + 1024]
                    else:
                        src = w_fm[bass.ds(i * 4 + (u - 3 if u else 0), 1), :, :]
                    sp.dma_start(raw[:, RAW_SLOT[u], :], src.rearrange("a p c -> (a p) c"))\
                      .then_inc(raw_in[RAW_SLOT[u]], 16)

                for u in (XR, Q0, Q1):
                    load(u, 0)
                sp.wait_ge(w_lo, XR + 1)
                load(Q2, 0)

                def store(dst, i, half, src, done):
                    rows = dst[bass.ds(i, 1), :, :] if half is None else \
                        dst[bass.ds(i, 1), :, HALF * half:HALF * half + HALF]
                    sp.dma_start(rows.rearrange("a p t -> (a p) t"), src).then_inc(done, 16)

                def turn(i, last):
                    sp.wait_ge(bound_done, i * ATT)
                    sp.dma_start(bias[:, :, :, :].rearrange("p h e c -> p h (e c)"),
                                 bias_d[:, bass.ds(i * 2, 2), 1:1 + BIAS_ROWS, :].rearrange("p h e c -> p h (e c)"))\
                      .then_inc(bias_in, 16)
                    sp.wait_ge(f_full, i * F_USES)
                    sp.dma_start(lw[:, :, :].rearrange("p a b -> p (a b)"),
                                 lru_w[bass.ds(i, 1)].rearrange("a p c -> (a p) c")).then_inc(lw_in, 16)
                    def next_block(u, before, n):
                        sp.wait_ge(w_lo, i * UNITS + before + 1)
                        load(u, n)

                    next_block(G, Q0, i)
                    next_block(MR, Q1, i)
                    next_block(MN, G, i)
                    if not last:
                        next_block(XR, Q2, i + 1)
                    sp.wait_ge(yr_ready, i + 1)
                    store(yr_d, i, None, gel[:, :], yr_out)
                    for j, dst in enumerate((smr_d, smr_d, smn_d, smn_d)):
                        sp.wait_ge(f_free, i * F_USES + (17 + j + 1))
                        store(dst, i, j % 2, stage[:, :], stage_out)
                        if not last and j in (1, 3):
                            next_block(*((Q0, MN), (Q1, MR))[j // 2], i + 1)
                    if not last:
                        sp.wait_ge(w_lo, i * UNITS + (UNITS + XR + 1))
                        load(Q2, i + 1)
                    for j in range(2):
                        sp.wait_ge(yt_ready, i * 2 + (j + 1))
                        store(yn_d, i, j, yT, yt_out)

                with sp.Fori(0, PAIRS - 1) as i:
                    turn(i, False)
                turn(PAIRS - 1, True)
                sp.wait_ge(yr_out, PAIRS * 16)
                sp.wait_ge(stage_out, PAIRS * 64)
                sp.wait_ge(yt_out, PAIRS * 32)

            @block.gpsimd
            def _(pool):
                pool.memset(pad[:, :], 0.0).then_inc(set_done, 1)
                pool.memset(ssq[:, :, :], 1.0).then_inc(set_done, 1)
                pool.wait_ge(const_in, 48)
                with pool.Fori(0, PAIRS) as i:
                    pool.wait_ge(bias_in, i * 16 + 16)
                    for h in range(2):
                        pool.tensor_tensor(bias[:, h, :, :], bias[:, h, :, :],
                                           colmask.unsqueeze(1).broadcast_to([P, BIAS_ROWS, GW]), ALU.add)\
                            .then_inc(bias_done, 1)

            @block.tensor
            def _(pe):
                def f_bank(i, j):
                    pe.wait_ge(f_free, i * F_USES + max(j - 1, 0))
                    return f_ps[j % 2]

                def fm(i, j, u, slot, c0, c1):
                    bank = f_bank(i, j)
                    return three_passes(pe, bank[:, 0:c1 - c0], lambda k: fh[:, slot, k, :],
                                        lambda k: fl[:, slot, k, :], lambda k: xnh[:, k, c0:c1],
                                        lambda k: xnl[:, k, c0:c1], KC).then_inc(f_full, 1)

                def fm_block(i, j, u, segs):
                    pe.wait_ge(w_lo, i * UNITS + u + 1)
                    for n, (c0, c1) in enumerate(segs):
                        fm(i, j + n, u, 0 if u in (XR, MR) else 1, c0, c1)

                def q_tile(i, t):
                    c0 = C + P * t if t < NT else P * (t - NT)
                    w0 = 0 if t < NT else P
                    pe.wait_ge(q_free, i * Q_TILES + max(t - 1, 0))
                    last = three_passes(pe, q_ps[t % 2][:, w0:384], lambda k: xnh[:, k, c0:c0 + P],
                                        lambda k: xnl[:, k, c0:c0 + P], lambda k: qh[:, k, w0:384],
                                        lambda k: ql[:, k, w0:384], KC)
                    last.then_inc(q_full, 1)

                def gates(i, d):
                    if d == 0:
                        pe.wait_ge(lw_in, i * 16 + 16)
                        pe.wait_ge(conv_done, i + 1)
                    j = 3 + 6 * d
                    for g in range(2):
                        for c0, c1 in SEGS:
                            bank = f_bank(i, j)
                            pe.matmul(bank[:, 0:c1 - c0], lw[:, 2 * g + d, :], xc[:, c0:c1],
                                             start=True, stop=True).then_inc(f_full, 1)
                            j += 1

                def transposes(i):
                    jobs = [("qp", 0), ("qp", 4), ("qr", 0), ("qr", 4), ("kr", 0), ("kr", 4), ("kc", 0)]
                    for n, (what, t0) in enumerate(jobs):
                        if n == 0:
                            pe.wait_ge(rope_q, i + 1)
                            pe.wait_ge(yr_ready, i + 1)
                            pe.wait_ge(pt_dve, i * ATT)
                            pe.wait_ge(yt_ready, i * 2)
                        if what == "kr" and t0 == 0:
                            pe.wait_ge(rope_k, i + 1)
                        if n % 2 == 0:
                            pe.wait_ge(tr_act, i * 4 + n // 2)
                        else:
                            pe.wait_ge(tr_dve, i * 3 + n // 2)
                        for t in range(t0, t0 + (2 if what == "kc" else 4)):
                            src = {"qp": lambda: qkv[:, t, 0:P], "qr": lambda: qrot[:, P * t:P * t + P],
                                   "kr": lambda: krot[:, P * t:P * t + P],
                                   "kc": lambda: qkv[:, NT + t, P:2 * P]}[what]()
                            last = pe.transpose(t_ps[n % 2][:, P * (t - t0):P * (t - t0) + P], src, ident)
                        last.then_inc(tr_full, 1)

                def scores(i, u):
                    t, h = u // 2, u % 2
                    rows = slice(HD * h, HD * h + HD)
                    a, b = (f_ps if u % 2 == 0 else q_ps)
                    if u >= 2:
                        pe.wait_ge(exp_done, i * ATT + u - 1)
                    k0 = KEY_ROW0[t] * GW
                    inner = KEY_ROWS[t] == 9
                    pe.matmul(a[:, 0:HALF], qrotT[rows, P * t:P * t + P], krotT[rows, k0:k0 + HALF],
                              start=True, stop=not inner)
                    if inner:
                        pe.matmul(a[:, 0:GW], negr[0:1, 0:P], negr[0:1, 2 * P:], start=False, stop=True)
                        pe.matmul(b[:, 0:GW], qrotT[rows, P * t:P * t + P],
                                  krotT[rows, k0 + HALF:k0 + HALF + GW], start=True, stop=False)
                        pe.matmul(b[:, 0:GW], negr[0:1, P:2 * P], negr[0:1, 2 * P:], start=False, stop=True)
                    pe.matmul(b[:, GW:GW + C], qplT[rows, P * t:P * t + P], kcT[rows, :],
                              start=True, stop=True).then_inc(qk_done, 1)

                def prob_transposes(i, u):
                    t = u // 2
                    pe.wait_ge(exp_done, i * ATT + u + 1)
                    pe.wait_ge(pt_dve, i * ATT + u)
                    pe.wait_ge(pt_act, i * ATT + u)
                    for b in range(4):
                        pe.transpose(t_ps[0][:, P * b:P * b + P], prob[u % 2][:, P * b:P * b + P], ident)
                    if KEY_ROWS[t] == 9:
                        pe.transpose(t_ps[1][0:GW, 0:P], prob[u % 2][:, HALF:HALF + GW], ident)
                    for b in range(2):
                        last = pe.transpose(t_ps[1][:, P + P * b:2 * P + P * b],
                                            prob[u % 2][:, 576 + P * b:576 + P * b + P], ident)
                    last.then_inc(pt_full, 1)

                def weighted_values(i, u):
                    t, h = u // 2, u % 2
                    v0 = 2 * P + HD * h
                    out = o_ps[u % 2][:, 0:HD]
                    pe.wait_ge(pt_dve, i * ATT + u + 1)
                    pe.wait_ge(pt_act, i * ATT + u + 1)
                    pe.wait_ge(y_done, i * ATT + max(u - 1, 0))
                    s = probT[u % 2]
                    for b in range(4):
                        pe.matmul(out, s[:, b, :], qkv[:, KEY_ROW0[t] // 2 + b, v0:v0 + HD],
                                  start=(b == 0), stop=False)
                    if KEY_ROWS[t] == 9:
                        pe.matmul(out, s[0:GW, 4, :], qkv[0:GW, KEY_ROW0[t] // 2 + 4, v0:v0 + HD],
                                  start=False, stop=False)
                    for b in range(2):
                        last = pe.matmul(out, s[:, 5 + b, :], qkv[:, NT + b, v0:v0 + HD],
                                         start=False, stop=(b == 1))
                    last.then_inc(pv_done, 1)

                def y_transposes(i, j):
                    pe.wait_ge(y_done, i * ATT + 8 * j + 8)
                    for b in range(4):
                        last = pe.transpose(t_ps[0][:, P * b:P * b + P], ytok[:, b, :], ident)
                    last.then_inc(yt_full, 1)

                pe.wait_ge(const_in, 48)
                with pe.Fori(0, PAIRS) as i:
                    pe.wait_ge(exp_done, i * ATT)
                    fm_block(i, 0, XR, SEGS)
                    pe.wait_ge(w_lo, i * UNITS + Q2 + 1)
                    for t in range(4):
                        q_tile(i, t)
                    gates(i, 0)
                    for t in range(4, 7):
                        q_tile(i, t)
                    gates(i, 1)
                    for t in range(7, Q_TILES):
                        q_tile(i, t)
                    fm_block(i, 15, G, SEGS[1:])
                    fm_block(i, 17, MR, SEGS[1:])
                    transposes(i)
                    fm_block(i, 19, MN, SEGS[1:])
                    pe.wait_ge(f_free, i * F_USES + F_USES)
                    pe.wait_ge(q_free, i * Q_TILES + Q_TILES)
                    pe.wait_ge(tr_act, i * 4 + 4)
                    pe.wait_ge(tr_dve, i * 3 + 3)
                    scores(i, 0)
                    scores(i, 1)
                    for u in range(ATT):
                        if u == 8:
                            pe.wait_ge(yt_ready, i * 2 + 1)
                        prob_transposes(i, u)
                        if u + 2 < ATT:
                            scores(i, u + 2)
                        weighted_values(i, u)
                        if u % 8 == 7:
                            y_transposes(i, u // 8)

            @block.scalar
            def _(act):
                def split_hi(u, i):
                    raw_wait(act, u, i)
                    if u in (Q0, Q1, Q2):
                        act.wait_ge(q_full, i * Q_TILES)
                    act.copy(hi_parts(u)[0], raw[:, RAW_SLOT[u], :]).then_inc(w_hi, 1)

                def f_evac(i, j, out, func, **kw):
                    act.wait_ge(f_full, i * F_USES + j + 1)
                    return act.activation(out, f_ps[j % 2][:, 0:out.shape[1]], func, **kw).then_inc(f_free, 1)

                def q_evac(i, t):
                    w0 = 0 if t < NT else P
                    act.wait_ge(q_full, i * Q_TILES + t + 1)
                    act.copy(qkv[:, t, w0:384], q_ps[t % 2][:, w0:384])
                    act.wait_ge(sq_used, i * Q_TILES + max(t - 1, 0))
                    act.activation(sqs[:, t % 2, w0:256], q_ps[t % 2][:, w0:256], ACT.Square).then_inc(q_free, 1)

                def gates(i, d):
                    if d == 1:
                        act.wait_ge(gates_free, i + 1)
                    for g, out in enumerate((gR, gI)):
                        for n, (c0, c1) in enumerate(SEGS):
                            f_evac(i, 3 + 6 * d + 3 * g + n, out[:, c0:c1], ACT.Sigmoid,
                                   bias=lp[:, 5 + 2 * g + d:6 + 2 * g + d])

                def decays(i, d):
                    act.wait_ge(f_free, i * F_USES + 9 + 6 * d)
                    act.activation(gA[:, :], gR[:, :], ACT.Exp, scale=lp[:, 11 + d:12 + d])\
                       .then_inc(decayed, 1)
                    act.activation(gR[:, :], gR[:, :], ACT.Tanh, scale=lp[:, 13 + d:14 + d])
                    act.wait_ge(decayed, 4 * i + 2 * d + 1)
                    act.activation(gD[:, :], gA[:, :], ACT.Square).then_inc(decayed, 1)

                def root(i, d):
                    act.wait_ge(one_minus, 2 * i + d + 1)
                    act.activation(gD[:, :], gD[:, :], ACT.Sqrt).then_inc(rooted, 1)

                def tr_evac(i, n):
                    act.wait_ge(tr_full, i * 7 + n + 1)
                    dst = {0: qplT[:, 0:HALF], 2: qrotT[:, 0:HALF], 4: krotT[:, 0:HALF], 6: kcT[:, :]}[n]
                    act.copy(dst, t_ps[0][:, 0:dst.shape[1]]).then_inc(tr_act, 1)

                def soft(i, u):
                    rows = KEY_ROWS[u // 2] * GW
                    b = (f_ps if u % 2 == 0 else q_ps)[1]
                    act.wait_ge(bound_done, i * ATT + u + 1)
                    act.activation(prob[u % 2][:, 0:rows], prob[u % 2][:, 0:rows], ACT.Exp,
                                   bias=stat[:, u, 2:3], accum_out=stat[:, u, 3:4])
                    act.activation(prob[u % 2][:, 576:832], b[:, GW:GW + C], ACT.Exp,
                                   bias=stat[:, u, 2:3], accum_out=stat[:, u, 4:5]).then_inc(exp_done, 1)

                def probT_evac(i, u):
                    act.wait_ge(pt_full, i * ATT + u + 1)
                    if u >= 2:
                        act.wait_ge(pv_done, i * ATT + u - 1)
                    if KEY_ROWS[u // 2] == 9:
                        act.copy(probT[u % 2][0:GW, 4, :], t_ps[1][0:GW, 0:P])
                    act.copy(probT[u % 2][:, 5:7, :], t_ps[1][:, P:3 * P].rearrange("p (a b) -> p a b", b=P))\
                       .then_inc(pt_act, 1)

                def y_evac(i, j):
                    act.wait_ge(yt_full, i * 2 + j + 1)
                    act.wait_ge(yt_out, i * 32 + j * 16)
                    act.copy(yT, t_ps[0][:, :]).then_inc(yt_ready, 1)

                act.wait_ge(set_done, 2)
                for u in (XR, Q0, Q1, Q2):
                    split_hi(u, 0)

                def turn(i, last):
                    f_evac(i, 0, pad[:, 2:2 + C], ACT.Copy)
                    f_evac(i, 1, pad[:, 261:261 + HALF], ACT.Copy)
                    f_evac(i, 2, pad[:, 261 + HALF:261 + T], ACT.Copy)
                    for t in range(4):
                        q_evac(i, t)
                    act.wait_ge(f_full, i * F_USES)
                    split_hi(G, i)
                    act.wait_ge(yt_out, i * 32)
                    gates(i, 0)
                    q_evac(i, 4)
                    decays(i, 0)
                    q_evac(i, 5)
                    root(i, 0)
                    q_evac(i, 6)
                    gates(i, 1)
                    q_evac(i, 7)
                    decays(i, 1)
                    split_hi(MR, i)
                    q_evac(i, 8)
                    q_evac(i, 9)
                    root(i, 1)
                    act.wait_ge(sq_used, i * Q_TILES + Q_TILES)
                    act.activation(rstd[:, 0, :, :], ssq[:, :, :], ACT.Sqrt, bias=eps[:, :], scale=1.0 / HD)\
                       .then_inc(rms_root, 1)
                    act.wait_ge(yr_out, i * 16)
                    f_evac(i, 15, gel[:, 0:HALF], ACT.Gelu_apprx_tanh)
                    f_evac(i, 16, gel[:, HALF:T], ACT.Gelu_apprx_tanh)
                    act.wait_ge(f_full, i * F_USES + 17)
                    split_hi(MN, i)
                    for j in range(4):
                        act.wait_ge(stage_out, i * 64 + j * 16)
                        act.wait_ge(f_full, i * F_USES + 17 + j + 1)
                        act.activation(stage[:, :], f_ps[(17 + j) % 2][:, :], ACT.Sigmoid)\
                           .then_inc(f_free, 1)
                        if j == 1:
                            for n in (0, 2, 4, 6):
                                tr_evac(i, n)
                            if not last:
                                split_hi(XR, i + 1)
                    soft(i, 0)
                    soft(i, 1)
                    for u in range(ATT):
                        probT_evac(i, u)
                        if u + 2 < ATT:
                            soft(i, u + 2)
                        if not last and u in (1, 3, 5):
                            split_hi((Q0, Q1, Q2)[u // 2], i + 1)
                        if u % 8 == 7:
                            y_evac(i, u // 8)

                with act.Fori(0, PAIRS - 1) as i:
                    turn(i, False)
                turn(PAIRS - 1, True)

            @block.vector
            def _(dve):
                def split_lo(u, i, n):
                    raw_wait(dve, u, i)
                    dve.wait_ge(w_hi, i * UNITS + u + 1)
                    hi, lo = hi_parts(u)
                    dve.tensor_tensor(lo, raw[:, RAW_SLOT[u], :], hi.bitcast(F32), ALU.subtract).then_inc(w_lo, 1)

                steps = [0]

                def then(ins):
                    steps[0] += 1
                    ins.then_inc(dve_step, 1)
                    dve.wait_ge(dve_step, base[0] + steps[0])

                base = [0]

                def conv(i):
                    dve.wait_ge(decayed, i * 4)
                    dve.tensor_scalar(lp[:, 0:11], lrup[:, :, bass.ds(i, 1)].rearrange("p a b -> p (a b)"),
                                      1.0, None, ALU.mult)
                    then(dve.tensor_scalar(lp[:, 11:15], decay[:, :, :, bass.ds(i, 1)].rearrange("p a b c -> p (a b c)"),
                                           1.0, None, ALU.mult))
                    dve.wait_ge(f_free, i * F_USES + 3)
                    for o, p0, n in ((0, 0, C), (C, 259, T)):
                        then(dve.tensor_scalar(xc[:, o:o + n], pad[:, p0:p0 + n], lp[:, 0:1],
                                               lp[:, 4:5], ALU.mult, ALU.add))
                        for k in range(1, 4):
                            last = dve.scalar_tensor_tensor(xc[:, o:o + n], pad[:, p0 + k:p0 + k + n],
                                                            lp[:, k:k + 1], xc[:, o:o + n],
                                                            ALU.mult, ALU.add)
                            if k < 3:
                                then(last)
                    last.then_inc(conv_done, 1)

                def head_squares(i, t):
                    g0 = 0 if t < NT else 2
                    dve.wait_ge(q_free, i * Q_TILES + t + 1)
                    dve.tensor_reduce(ssq[:, t, g0:4], sqs[:, t % 2, HD * g0:256].rearrange("p (g f) -> p g f", f=HD),
                                      AX_X, ALU.add).then_inc(sq_used, 1)

                def gated_input(i, d):
                    dve.wait_ge(f_free, i * F_USES + 9 + 6 * d)
                    then(dve.tensor_tensor(gI[:, :], gI[:, :], xc[:, :], ALU.mult))

                def complement(i, d):
                    dve.wait_ge(decayed, 4 * i + 2 * d + 2)
                    dve.scalar_tensor_tensor(gD[:, :], gD[:, :], 1.0, gR[:, :], ALU.add, ALU.mult)\
                       .then_inc(one_minus, 1)

                def scan(i, d):
                    dve.wait_ge(rooted, 2 * i + d + 1)
                    then(dve.tensor_tensor(gI[:, :], gI[:, :], gD[:, :], ALU.mult))
                    if d == 0:
                        dve.tensor_tensor_scan(h0[:, :], gA[:, :], gI[:, :], 0.0, ALU.mult, ALU.add)\
                           .then_inc(gates_free, 1)
                    else:
                        then(dve.tensor_tensor_scan(gI[:, C - 1::-1], gA[:, C - 1::-1], gI[:, C - 1::-1], 0.0,
                                                    ALU.mult, ALU.add))
                        then(dve.tensor_tensor_scan(gI[:, N - 1:C - 1:-1], gA[:, N - 1:C - 1:-1],
                                                    gI[:, N - 1:C - 1:-1], gI[:, 0:1], ALU.mult, ALU.add))
                        last = dve.tensor_tensor(h0[:, C:N], h0[:, C:N], gI[:, C:N], ALU.add)
                        then(last)

                def rnn_out(i):
                    dve.wait_ge(f_free, i * F_USES + 17)
                    dve.tensor_tensor(gel[:, :], gel[:, :], h0[:, C:N], ALU.mult).then_inc(yr_ready, 1)

                def head_norm(i, col, tiles, g):
                    x = qkv[:, 0:tiles, P * col:P * col + P].rearrange("p t (h f) -> p t h f", f=HD)
                    then(dve.tensor_tensor(x, x, ssq[:, 0:tiles, 2 * col:2 * col + 2].unsqueeze(3)
                                           .broadcast_to([P, tiles, 2, HD]), ALU.mult))
                    gb = g.unsqueeze(1).unsqueeze(1).broadcast_to([P, tiles, 2, HD])
                    then(dve.tensor_tensor(x, x, gb, ALU.mult))

                def rotate(i, col, out, done):
                    o4 = out.rearrange("p (t h f) -> p t h f", h=2, f=HD)
                    s4 = swp.rearrange("p (t h f) -> p t h f", h=2, f=HD)
                    x = qkv[:, 0:NT, P * col:P * col + P].rearrange("p t (h f) -> p t h f", f=HD)
                    dve.tensor_tensor(o4, x, cosT.unsqueeze(2).broadcast_to([P, NT, 2, HD]), ALU.mult)
                    for h in range(2):
                        for b in range(2):
                            xs = x[:, :, h, :].rearrange("p t (a b f) -> p t a b f", a=2, b=2)[:, :, :, 1 - b, :]
                            sn = sinT.rearrange("p t (a b f) -> p t a b f", a=2, b=2)[:, :, :, b, :]
                            so = s4[:, :, h, :].rearrange("p t (a b f) -> p t a b f", a=2, b=2)[:, :, :, b, :]
                            last = dve.tensor_tensor(so, xs, sn, ALU.mult)
                    then(last)
                    dve.tensor_tensor(out, out, swp, ALU.add).then_inc(done, 1)

                def tr_evac(i, n):
                    dve.wait_ge(tr_full, i * 7 + n + 1)
                    dst = {1: qplT, 3: qrotT, 5: krotT}[n][:, HALF:T]
                    dve.tensor_copy(dst, t_ps[1][:, :]).then_inc(tr_dve, 1)

                def bound(i, u):
                    t, h = u // 2, u % 2
                    a, b = (f_ps if u % 2 == 0 else q_ps)
                    rows = KEY_ROWS[t]
                    e = BIAS_ROW0[t] - 1
                    dve.wait_ge(qk_done, i * ATT + u + 1)
                    dve.tensor_reduce(stat[:, u, 1:2], b[:, GW:GW + C], AX_X, ALU.max)
                    if rows == 9:
                        dve.tensor_tensor(prob[u % 2][:, HALF:HALF + GW], b[:, 0:GW], bias[:, h, e + 8, :],
                                          ALU.add).then_inc(bound_step, 1)
                    last = dve.tensor_tensor_reduce(out=prob[u % 2][:, 0:HALF], in0=a[:, :],
                                                    in1=bias[:, h, e:e + 8, :].rearrange("p a b -> p (a b)"),
                                                    scale=1.0, scalar=-3.0e38, op0=ALU.add, op1=ALU.max,
                                                    accum_out=stat[:, u, 0:1])
                    if rows == 9:
                        dve.wait_ge(bound_step, 8 * i + (u - 3))
                        last = dve.tensor_reduce(ysc[:, u, 0:1], prob[u % 2][:, HALF:HALF + GW], AX_X, ALU.max)
                    then(last)
                    if rows == 9:
                        then(dve.tensor_tensor(stat[:, u, 0:1], stat[:, u, 0:1], ysc[:, u, 0:1], ALU.max))
                    then(dve.tensor_tensor(stat[:, u, 1:2], stat[:, u, 0:1], stat[:, u, 1:2], ALU.max))
                    dve.tensor_scalar(stat[:, u, 2:3], stat[:, u, 1:2], -1.0, None, ALU.mult)\
                       .then_inc(bound_done, 1)

                def probT_evac(i, u):
                    dve.wait_ge(pt_full, i * ATT + u + 1)
                    if u >= 2:
                        dve.wait_ge(pv_done, i * ATT + u - 1)
                    dve.tensor_copy(probT[u % 2][:, 0:4, :].rearrange("p a b -> p (a b)"), t_ps[0][:, :])\
                       .then_inc(pt_dve, 1)

                def y_out(i, u):
                    t, h = u // 2, u % 2
                    dve.wait_ge(exp_done, i * ATT + u + 1)
                    then(dve.tensor_tensor(ysc[:, u, 0:1], stat[:, u, 3:4], stat[:, u, 4:5], ALU.add))
                    then(dve.reciprocal(ysc[:, u, 1:2], ysc[:, u, 0:1]))
                    dve.wait_ge(pv_done, i * ATT + u + 1)
                    if u % 8 == 0:
                        dve.wait_ge(yt_full, i * 2 + u // 8)
                    dve.tensor_scalar(ytok[:, t % 4, HD * h:HD * h + HD], o_ps[u % 2][:, 0:HD], ysc[:, u, 1:2],
                                      None, ALU.mult).then_inc(y_done, 1)

                dve.wait_ge(const_in, 48)
                then(dve.tensor_scalar(gqk[:, 0, :], gqk[:, 0, :], HD ** -0.5, None, ALU.mult))
                for u in (XR, Q0, Q1, Q2):
                    split_lo(u, 0, u)

                per_turn = [None]

                def turn(i, last):
                    base[0] = 1 + i * STEPS
                    steps[0] = 0
                    conv(i)
                    for t in range(4):
                        head_squares(i, t)
                    split_lo(G, i, 4)
                    gated_input(i, 0)
                    head_squares(i, 4)
                    complement(i, 0)
                    head_squares(i, 5)
                    scan(i, 0)
                    head_squares(i, 6)
                    gated_input(i, 1)
                    head_squares(i, 7)
                    complement(i, 1)
                    split_lo(MR, i, 5)
                    head_squares(i, 8)
                    head_squares(i, 9)
                    scan(i, 1)
                    dve.wait_ge(rms_root, i + 1)
                    rt, v = rstd[:, 0, :, :], ssq[:, :, :]
                    then(dve.reciprocal(rt, rt))
                    dve.tensor_scalar(v, v, -0.5 / HD, -0.5 * EPS, ALU.mult, ALU.add)
                    then(dve.tensor_tensor(rstd[:, 1, :, :], rt, rt, ALU.mult))
                    then(dve.tensor_tensor(v, v, rstd[:, 1, :, :], ALU.mult))
                    then(dve.scalar_tensor_tensor(v, v, 1.5, rt, ALU.add, ALU.mult))
                    head_norm(i, 0, NT, gqk[:, 0, :])
                    rotate(i, 0, qrot, rope_q)
                    rnn_out(i)
                    split_lo(MN, i, 6)
                    head_norm(i, 1, Q_TILES, gqk[:, 1, :])
                    dve.wait_ge(rope_q, i + 1)
                    rotate(i, 1, krot, rope_k)
                    for n in (1, 3, 5):
                        tr_evac(i, n)
                    if not last:
                        split_lo(XR, i + 1, 0)
                    dve.wait_ge(bias_done, 2 * i + 2)
                    bound(i, 0)
                    bound(i, 1)
                    for u in range(ATT):
                        probT_evac(i, u)
                        if u + 2 < ATT:
                            bound(i, u + 2)
                        y_out(i, u)
                        if not last and u in (1, 3, 5):
                            split_lo((Q0, Q1, Q2)[u // 2], i + 1, 0)
                    assert steps[0] == STEPS, steps[0]

                with dve.Fori(0, PAIRS - 1) as i:
                    turn(i, False)
                turn(PAIRS - 1, True)


STEPS = 3 + 1 + 6 + 1 + 1 + 1 + 4 + 1 + 3 + 3 + ATT * 4 + 8


def merge_block(nc, sem, sbuf, psum, xT, w_mix, mod, x1, yr_d, yn_d, smr_d, smn_d):
    with ExitStack() as st:
        raw = sbuf(st, "raw_c", [P, 2, 1024])
        wh = sbuf(st, "wh_c", [P, 2, KC, P], F32R)
        wl = sbuf(st, "wl_c", [P, 2, KC, P], F32R)
        ah = [sbuf(st, f"ah{n}", [P, KC, T], F32R) for n in range(2)]
        al = [sbuf(st, f"al{n}", [P, KC, T], F32R) for n in range(2)]
        aux = sbuf(st, "aux", [P, 2, T])
        ys = sbuf(st, "ys", [P, 2, T])
        ps = psum(st, "ps_c", [P, 4, HALF])
        raw_in = [sem(f"c_raw_in{s}") for s in range(2)]
        aux_in = [sem(f"c_aux_in{s}") for s in range(2)]
        ys_in = [sem(f"c_ys_in{s}") for s in range(2)]
        w_hi, w_lo = sem("c_w_hi"), sem("c_w_lo")
        y_hi, y_lo = sem("c_y_hi"), sem("c_y_lo")
        full, free = sem("c_full"), sem("c_free")
        part = sem("c_part")
        merged_hi, merged_lo = sem("c_merged_hi"), sem("c_merged_lo")
        units = 3 * KC
        flat = lambda a, s: a[:, s, :, :].rearrange("p k c -> p (k c)")

        with nc.Block() as block:
            @block.sync
            def _(sp):
                for n in range(2):
                    sp.dma_start(raw[:, n, :], w_mix[n]).then_inc(raw_in[n], 16)
                with sp.Fori(0, units // 2 - 1) as r:
                    for b in range(2):
                        sp.wait_ge(w_lo, r * 2 + b + 1)
                        sp.dma_start(raw[:, b, :], w_mix[bass.ds(r * 2 + b + 2, 1)].rearrange("a p c -> (a p) c"))\
                          .then_inc(raw_in[b], 16)

            @block.gpsimd
            def _(pool):
                for n in range(2 * KC):
                    if n >= 2:
                        pool.wait_ge(y_lo, n - 1)
                    pool.dma_start(ys[:, n % 2, :], (yr_d if n < KC else yn_d)[n % KC]).then_inc(ys_in[n % 2], 16)
                    if n in (8, 9):
                        pool.dma_start(aux[:, n % 2, :], smr_d[n % 2]).then_inc(aux_in[n % 2], 16)
                for n in range(2, units):
                    src = (smr_d, smn_d, xT)[n // KC]
                    pool.wait_ge(free, 2 * n - 2)
                    pool.dma_start(aux[:, n % 2, :], src[n % KC]).then_inc(aux_in[n % 2], 16)

            @block.tensor
            def _(pe):
                for ph in range(3):
                    if ph < 2:
                        pe.wait_ge(y_lo, KC * (ph + 1))
                    else:
                        pe.wait_ge(merged_lo, 2 * KC)
                    s = ph % 2
                    with pe.Fori(0, KC // 2) as r:
                        for b in range(2):
                            n = r * 2 + (KC * ph + b)
                            pe.wait_ge(w_lo, n + 1)
                            for half in range(2):
                                if ph > 0:
                                    pe.wait_ge(free, n * 2 + half - 3)
                                else:
                                    pe.wait_ge(free, r * 4 if b == 0 else r * 4 + half)
                                cols = slice(HALF * half, HALF * half + HALF)
                                three_passes(pe, ps[:, 2 * b + half, :], lambda k: wh[:, b, k, :],
                                                    lambda k: wl[:, b, k, :], lambda k: ah[s][:, k, cols],
                                                    lambda k: al[s][:, k, cols], KC).then_inc(full, 1)

            @block.scalar
            def _(act):
                def w_split(n, b):
                    act.wait_ge(raw_in[b], (n // 2) * 16 + 16 if isinstance(n, int) else (n - b) * 8 + 16)
                    act.copy(flat(wh, b), raw[:, b, :]).then_inc(w_hi, 1)

                def y_split(n):
                    act.wait_ge(ys_in[n % 2], (n // 2) * 16 + 16)
                    act.copy(ah[n // KC][:, n % KC, :], ys[:, n % 2, :]).then_inc(y_hi, 1)

                w_split(0, 0)
                for n in range(KC):
                    y_split(n)
                w_split(1, 1)
                for n in range(KC, 2 * KC):
                    y_split(n)
                with act.Fori(0, units // 2 - 1) as r:
                    for b in range(2):
                        act.wait_ge(full, r * 4 + (2 * b + 2))
                        w_split(r * 2 + (b + 2), b)

            @block.vector
            def _(dve):
                def w_split(n, b):
                    dve.wait_ge(w_hi, n + 1)
                    dve.wait_ge(raw_in[b], (n // 2) * 16 + 16 if isinstance(n, int) else (n - b) * 8 + 16)
                    dve.tensor_tensor(flat(wl, b), raw[:, b, :], flat(wh, b).bitcast(F32), ALU.subtract)\
                       .then_inc(w_lo, 1)

                def y_split(n):
                    dve.wait_ge(y_hi, n + 1)
                    dve.wait_ge(ys_in[n % 2], (n // 2) * 16 + 16)
                    dve.tensor_tensor(al[n // KC][:, n % KC, :], ys[:, n % 2, :],
                                      ah[n // KC][:, n % KC, :].bitcast(F32), ALU.subtract).then_inc(y_lo, 1)

                w_split(0, 0)
                for n in range(KC):
                    y_split(n)
                w_split(1, 1)
                for n in range(KC, 2 * KC):
                    y_split(n)
                for ph in range(3):
                    def step(n, m, b, more):
                        dve.wait_ge(aux_in[b], (n - b) * 8 + 16)
                        for half in range(2):
                            cols = slice(HALF * half, HALF * half + HALF)
                            out = x1[:, bass.ds(m, 1), cols].rearrange("p a c -> p (a c)")
                            dve.wait_ge(full, n * 2 + half + 1)
                            if ph == 0:
                                dve.tensor_tensor(out, ps[:, 2 * b + half, :], aux[:, b, cols], ALU.mult)\
                                   .then_inc(free, 1)
                            elif ph == 1:
                                dve.tensor_tensor(aux[:, b, cols], ps[:, 2 * b + half, :], aux[:, b, cols],
                                                  ALU.mult).then_inc(part, 1)
                                dve.wait_ge(part, m * 2 + half + 1)
                                dve.tensor_tensor(out, out, aux[:, b, cols], ALU.add)\
                                   .then_inc(free, 1)
                                dve.wait_ge(free, n * 2 + half + 1)
                            else:
                                dve.scalar_tensor_tensor(out, ps[:, 2 * b + half, :],
                                                         mod[:, bass.ds(m + 2 * KC, 1), 0:1].rearrange("p a b -> p (a b)"),
                                                         aux[:, b, cols], ALU.mult, ALU.add).then_inc(free, 1)
                            if ph == 0 or ph == 2:
                                pass
                        if more:
                            w_split(n + 2, b)
                        if ph == 1:
                            for half in range(2):
                                cols = slice(HALF * half, HALF * half + HALF)
                                out = x1[:, bass.ds(m, 1), cols]
                                dve.tensor_scalar(ah[0][:, bass.ds(m, 1), cols], out, 1.0, None, ALU.mult)\
                                   .then_inc(merged_hi, 1)
                                dve.wait_ge(merged_hi, m * 2 + half + 1)
                                dve.tensor_tensor(al[0][:, bass.ds(m, 1), cols], out,
                                                  ah[0][:, bass.ds(m, 1), cols].bitcast(F32), ALU.subtract)\
                                   .then_inc(merged_lo, 1)

                    turns = KC // 2 - (ph == 2)
                    with dve.Fori(0, turns) as r:
                        for b in range(2):
                            step(r * 2 + (KC * ph + b), r * 2 + b, b, True)
                    if ph == 2:
                        for b in range(2):
                            step(units - 2 + b, KC - 2 + b, b, False)


def ffn_block(nc, sem, sbuf, psum, w_ff, ffn_p, mod, gain, ones, eps, x1, outT):
    with ExitStack() as st:
        xh = sbuf(st, "xh_d", [P, KC, T], F32R)
        xl = sbuf(st, "xl_d", [P, KC, T], F32R)
        hh = sbuf(st, "hh_d", [P, max(GROUPS), T], F32R)
        hl = sbuf(st, "hl_d", [P, max(GROUPS), T], F32R)
        raw = sbuf(st, "raw_d", [P, 2, 1024])
        wh = sbuf(st, "wh_d", [P, 2, KC, P], F32R)
        wl = sbuf(st, "wl_d", [P, 2, KC, P], F32R)
        ca = sbuf(st, "ca", [P, T])
        cg = sbuf(st, "cg", [P, T])
        fp = sbuf(st, "fp", [P, FC, 8])
        gm = sbuf(st, "gm_d", [P, KC])
        fps = sbuf(st, "fps", [P, 8])
        pa = psum(st, "pa", [P, T])
        pg = psum(st, "pg", [P, T])
        pd = psum(st, "pd", [P, 4, HALF])
        fp_in = sem("d_fp_in")
        raw_in = [sem(f"d_raw_in{s}") for s in range(2)]
        squared, sq_used, root, rstd_done = sem("d_squared"), sem("d_sq_used"), sem("d_root"), sem("d_rstd")
        gm_done, scaled, hi_done, lo_done = sem("d_gm"), sem("d_scaled"), sem("d_hi"), sem("d_lo")
        w_hi, w_lo, used = sem("d_w_hi"), sem("d_w_lo"), sem("d_used")
        centre = sem("d_centre")
        conv_step, conved = sem("d_conv_step"), sem("d_conved")
        silu_done, gated, h_hi, h_lo = sem("d_silu"), sem("d_gated"), sem("d_h_hi"), sem("d_h_lo")
        taps_in = sem("d_taps_in")
        full, free = sem("d_full"), sem("d_free")
        stored = sem("d_stored")
        flat = lambda a, s: a[:, s, :, :].rearrange("p k c -> p (k c)")
        starts = []
        n = 0
        for g, pairs in enumerate(GROUPS):
            starts.append((n, sum(GROUPS[:g]), n + 2 * pairs))
            n += 2 * pairs + KC

        with nc.Block() as block:
            @block.sync
            def _(sp):
                sp.dma_start(fp[:, :, :], ffn_p).then_inc(fp_in, 16)
                for n in range(2):
                    sp.dma_start(raw[:, n, :], w_ff[n]).then_inc(raw_in[n], 16)
                with sp.Fori(0, FF_UNITS // 2 - 1) as r:
                    for b in range(2):
                        sp.wait_ge(w_lo, r * 2 + b + 1)
                        sp.dma_start(raw[:, b, :], w_ff[bass.ds(r * 2 + b + 2, 1)].rearrange("a p c -> (a p) c"))\
                          .then_inc(raw_in[b], 16)
                with sp.Fori(0, KC) as m:
                    sp.wait_ge(free, m * 2 + (2 * KC * (len(GROUPS) - 1) + 2))
                    sp.dma_start(outT[bass.ds(m, 1)].rearrange("a p t -> (a p) t"),
                                 x1[:, bass.ds(m, 1), :].rearrange("p a t -> p (a t)")).then_inc(stored, 16)
                sp.wait_ge(stored, 16 * KC)

            @block.tensor
            def _(pe):
                for k in range(KC):
                    pe.wait_ge(squared, k + 1)
                    for half in range(2):
                        last = pe.matmul(pd[:, half, :], ones[:, :], (ca if k % 2 == 0 else cg)[:, HALF * half:HALF * half + HALF],
                                         start=(k == 0), stop=(k == KC - 1))
                    last.then_inc(sq_used, 1)
                pe.wait_ge(lo_done, KC)
                for g, pairs in enumerate(GROUPS):
                    u0, j0, d0 = starts[g]
                    with pe.Fori(0, pairs) as j:
                        for b, bank in enumerate((pa, pg)):
                            pe.wait_ge(w_lo, j * 2 + (u0 + b + 1))
                            pe.wait_ge(conved, j * 2 + (2 * j0 + b) if j0 else j * 2 + b * 0)
                            for half in range(2):
                                cols = slice(HALF * half, HALF * half + HALF)
                                last = three_passes(pe, bank[:, cols], lambda k: wh[:, b, k, :],
                                                    lambda k: wl[:, b, k, :], lambda k: xh[:, k, cols],
                                                    lambda k: xl[:, k, cols], KC)
                            last.then_inc(used, 1)
                    pe.wait_ge(h_lo, j0 + pairs)
                    with pe.Fori(0, KC // 2) as r:
                        for b in range(2):
                            pe.wait_ge(w_lo, r * 2 + (d0 + b + 1))
                            for half in range(2):
                                cols = slice(HALF * half, HALF * half + HALF)
                                back = 2 * KC * g + 2 * b + half - 3
                                pe.wait_ge(free, r * 4 + max(back, 0) if back >= 0 or b == 0 else r * 4)
                                three_passes(pe, pd[:, 2 * b + half, :], lambda k: wh[:, b, k, :],
                                                    lambda k: wl[:, b, k, :], lambda k: hh[:, k, cols],
                                                    lambda k: hl[:, k, cols], pairs).then_inc(full, 1)

            @block.scalar
            def _(act):
                def w_split(n, b):
                    act.wait_ge(raw_in[b], (n // 2) * 16 + 16 if isinstance(n, int) else (n - b) * 8 + 16)
                    act.copy(flat(wh, b), raw[:, b, :]).then_inc(w_hi, 1)

                w_split(0, 0)
                w_split(1, 1)
                for k in range(KC):
                    if k >= 2:
                        act.wait_ge(sq_used, k - 1)
                    act.activation((ca if k % 2 == 0 else cg)[:, :], x1[:, k, :], ACT.Square).then_inc(squared, 1)
                act.wait_ge(sq_used, KC)
                act.activation(ca[:, :], pd[:, 0:2, :].rearrange("p a b -> p (a b)"), ACT.Sqrt,
                               bias=eps[:, :], scale=1.0 / D).then_inc(root, 1)
                for k in range(KC):
                    act.wait_ge(scaled, k + 1)
                    act.activation(xh[:, k, :], (pa if k % 2 == 0 else pg)[:, :], ACT.Identity,
                                   bias=mod[:, 3 * KC + k, 0:1]).then_inc(hi_done, 1)
                act.wait_ge(fp_in, 16)
                for g, pairs in enumerate(GROUPS):
                    u0, j0, d0 = starts[g]
                    with act.Fori(0, pairs) as j:
                        for b, (bank, out) in enumerate(((pa, ca), (pg, cg))):
                            act.wait_ge(used, j * 2 + (2 * j0 + b + 1))
                            if b == 0:
                                act.wait_ge(h_lo, j + j0)
                            if b == 0:
                                act.wait_ge(taps_in, j + (j0 + 1))
                            act.activation(out[:, :], bank[:, :], ACT.Identity, bias=fps[:, 4 * b + 3:4 * b + 4],
                                           scale=fps[:, 4 * b + 1:4 * b + 2]).then_inc(centre, 1)
                            w_split(j * 2 + (u0 + b + 2), b)
                        act.wait_ge(conved, j * 2 + (2 * j0 + 1))
                        act.activation(ca[:, :], ca[:, :], ACT.Silu).then_inc(silu_done, 1)
                    turns = KC // 2 - (g == len(GROUPS) - 1)
                    with act.Fori(0, turns) as r:
                        for b in range(2):
                            act.wait_ge(full, r * 4 + (2 * KC * g + 2 * b + 2))
                            w_split(r * 2 + (d0 + b + 2), b)

            @block.vector
            def _(dve):
                def w_split(n, b):
                    dve.wait_ge(w_hi, n + 1)
                    dve.wait_ge(raw_in[b], (n // 2) * 16 + 16 if isinstance(n, int) else (n - b) * 8 + 16)
                    dve.tensor_tensor(flat(wl, b), raw[:, b, :], flat(wh, b).bitcast(F32), ALU.subtract)\
                       .then_inc(w_lo, 1)

                w_split(0, 0)
                w_split(1, 1)
                dve.scalar_tensor_tensor(gm[:, :], mod[:, 4 * KC:5 * KC, 0], 1.0, gain[:, 1, :], ALU.add, ALU.mult)\
                   .then_inc(gm_done, 1)
                dve.wait_ge(gm_done, 1)
                dve.wait_ge(root, 1)
                dve.reciprocal(cg[:, :], ca[:, :]).then_inc(rstd_done, 1)
                dve.wait_ge(rstd_done, 1)
                dve.tensor_scalar(ca[:, :], pd[:, 0:2, :].rearrange("p a b -> p (a b)"), -0.5 / D, -0.5 * EPS,
                                  ALU.mult, ALU.add).then_inc(rstd_done, 1)
                dve.wait_ge(rstd_done, 2)
                for n in range(2):
                    dve.tensor_tensor(ca[:, :], ca[:, :], cg[:, :], ALU.mult).then_inc(rstd_done, 1)
                    dve.wait_ge(rstd_done, 3 + n)
                dve.scalar_tensor_tensor(cg[:, :], ca[:, :], 1.5, cg[:, :], ALU.add, ALU.mult).then_inc(rstd_done, 1)
                dve.wait_ge(rstd_done, 5)
                for k in range(KC + 1):
                    if k < KC:
                        if k >= 2:
                            dve.wait_ge(lo_done, k - 1)
                        dve.scalar_tensor_tensor((pa if k % 2 == 0 else pg)[:, :], x1[:, k, :], gm[:, k:k + 1],
                                                 cg[:, :], ALU.mult, ALU.mult).then_inc(scaled, 1)
                    if k >= 1:
                        j = k - 1
                        dve.wait_ge(hi_done, k)
                        dve.scalar_tensor_tensor(xl[:, j, :], (pa if j % 2 == 0 else pg)[:, :],
                                                 mod[:, 3 * KC + j, 0:1], xh[:, j, :].bitcast(F32),
                                                 ALU.add, ALU.subtract).then_inc(lo_done, 1)
                dve.wait_ge(fp_in, 16)
                for g, pairs in enumerate(GROUPS):
                    u0, j0, d0 = starts[g]
                    with dve.Fori(0, pairs) as j:
                        dve.wait_ge(centre, j * 2 + 2 * j0)
                        dve.tensor_scalar(fps[:, :], fp[:, bass.ds(j + j0, 1), :].rearrange("p a b -> p (a b)"),
                                          1.0, None, ALU.mult).then_inc(taps_in, 1)
                        dve.wait_ge(taps_in, j + (j0 + 1))
                        for b, (bank, out) in enumerate(((pa, ca), (pg, cg))):
                            tap = lambda k: fps[:, 4 * b + k:4 * b + k + 1]
                            dve.wait_ge(centre, j * 2 + (2 * j0 + b + 1))
                            dve.scalar_tensor_tensor(out[:, 1:T], bank[:, 0:T - 1], tap(0), out[:, 1:T],
                                                     ALU.mult, ALU.add).then_inc(conv_step, 1)
                            dve.wait_ge(conv_step, j * 2 + (2 * j0 + b + 1))
                            dve.scalar_tensor_tensor(out[:, 0:T - 1], bank[:, 1:T], tap(2), out[:, 0:T - 1],
                                                     ALU.mult, ALU.add).then_inc(conved, 1)
                            w_split(j * 2 + (u0 + b + 2), b)
                        dve.wait_ge(conved, j * 2 + (2 * j0 + 2))
                        dve.wait_ge(silu_done, j + (j0 + 1))
                        dve.tensor_tensor(ca[:, :], ca[:, :], cg[:, :], ALU.mult).then_inc(gated, 1)
                        dve.wait_ge(gated, j + (j0 + 1))
                        dve.tensor_scalar(hh[:, bass.ds(j, 1), :].rearrange("p a t -> p (a t)"), ca[:, :],
                                          1.0, None, ALU.mult).then_inc(h_hi, 1)
                        dve.wait_ge(h_hi, j + (j0 + 1))
                        dve.tensor_tensor(hl[:, bass.ds(j, 1), :].rearrange("p a t -> p (a t)"), ca[:, :],
                                          hh[:, bass.ds(j, 1), :].rearrange("p a t -> p (a t)").bitcast(F32),
                                          ALU.subtract).then_inc(h_lo, 1)

                    def down(n, m, b, more):
                        for half in range(2):
                            cols = slice(HALF * half, HALF * half + HALF)
                            out = x1[:, bass.ds(m, 1), cols].rearrange("p a c -> p (a c)")
                            dve.wait_ge(full, m * 2 + (2 * KC * g + half + 1))
                            dve.scalar_tensor_tensor(out, pd[:, 2 * b + half, :],
                                                     mod[:, bass.ds(m + 5 * KC, 1), 0:1].rearrange("p a b -> p (a b)"),
                                                     out, ALU.mult, ALU.add).then_inc(free, 1)
                        if more:
                            w_split(n + 2, b)

                    last_group = g == len(GROUPS) - 1
                    with dve.Fori(0, KC // 2 - last_group) as r:
                        for b in range(2):
                            down(r * 2 + (d0 + b), r * 2 + b, b, True)
                    if last_group:
                        for b in range(2):
                            down(d0 + KC - 2 + b, KC - 2 + b, b, False)


def constants():
    col = np.arange(GW)
    start = np.clip(col - 8, 0, GW - 16)
    inside = (col[None, :] >= start[:, None]) & (col[None, :] < start[:, None] + 16)
    mask = np.where(inside, 0.0, NEG).astype(np.float32)
    mask = np.concatenate([mask, mask], 0)
    n = HD // 4
    freq = (np.float32(10000.0) ** (-np.arange(n, dtype=np.float32) / np.float32(n))).astype(np.float32)
    tok = np.arange(T)
    cos = np.zeros((T, 2, 2, n), np.float32)
    sin = np.zeros((T, 2, 2, n), np.float32)
    for a, pos in enumerate((tok // GW, tok % GW)):
        ang = (pos.astype(np.float32)[:, None] * freq).astype(np.float32)
        for b in range(2):
            cos[:, a, b] = np.cos(ang)
            sin[:, a, b] = np.sin(ang) * (1 if b else -1)
    tiles = lambda a: a.reshape(NT, P, HD).transpose(1, 0, 2).reshape(P, NT * HD)
    table = np.concatenate([np.eye(P, dtype=np.float32), mask, tiles(cos), tiles(sin)], 1)
    lower = (np.arange(P) >= GW).astype(np.float32)
    rows = np.concatenate([lower, 1 - lower, np.full(GW, NEG, np.float32)])[None, :]
    return np.ascontiguousarray(table, np.float32), np.ascontiguousarray(rows, np.float32)


def kernel(**inputs):
    import concourse.bacc as bacc
    from concourse.bass_utils import run_bass_kernel_spmd

    a = {k: np.asarray(v) for k, v in inputs.items()}
    chunks = lambda m: m.reshape(KC, P, -1)
    cols = lambda v: v.reshape(-1, P).T
    blocks = lambda w: w.reshape(w.shape[0] // P, P, w.shape[1] // P, P).transpose(2, 1, 0, 3)
    w_in = a["w_in"][0].reshape(KC, P, 7, KC, P)
    fm = w_in[:, :, [0, 3, 5, 6]].transpose(3, 2, 1, 0, 4).reshape(4 * KC, P, D)
    qkv = w_in[:, :, [4, 1, 2]].transpose(3, 1, 0, 2, 4).reshape(KC, P, 3 * D)
    lru_w = np.stack([a["lru_wa"][0], a["lru_wx"][0]]).reshape(4, KC, P, P).transpose(1, 2, 0, 3)
    lru_p = np.concatenate([a["lru_conv_w"][0], a["lru_conv_b"], a["lru_ba"][0], a["lru_bx"][0],
                            a["lru_lambda"][0]]).reshape(11, KC, P).transpose(2, 0, 1)
    rpb = np.zeros((16 * 16 + 1, P), np.float32)
    rpb[:-1].reshape(16, 16, P)[:, 1:, 48:79] = a["na_rpb"][0]
    up = blocks(a["w_up"][0]).reshape(2, FC, P, D)
    down = blocks(a["w_down"][0])
    units, j = [], 0
    for n in GROUPS:
        units.append(up[:, j:j + n].transpose(1, 0, 2, 3).reshape(2 * n, P, D))
        d = np.zeros((KC, P, KC, P), np.float32)
        d[:, :, 0:n] = down[:, :, j:j + n]
        units.append(d.reshape(KC, P, D))
        j += n
    conv = np.concatenate([a["ffn_conv_w"][0], a["ffn_conv_b"]]).reshape(4, 2, FC, P).transpose(3, 2, 1, 0)
    table, rows = constants()
    arrays = {
        "xT": chunks(a["x"][0].T), "ctxT": chunks(a["ctx"][0].T),
        "svec": np.stack([cols(a["c"][0]), cols(a["c_ctx"])], 2),
        "w_mod": blocks(a["w_mod"][0]), "b_mod": cols(a["b_mod"][0]),
        "gains": np.stack([cols(a["norm_mix_g"][0]), cols(a["norm_ffn_g"][0])], 1),
        "w_fm": fm, "w_qkv": qkv, "lru_w": lru_w.reshape(KC, P, 4 * P), "lru_p": lru_p,
        "qk_g": np.stack([a["q_norm_g"][0], a["k_norm_g"][0]]), "rpb": rpb,
        "w_mix": np.concatenate([blocks(a[n][0]).reshape(KC, P, D) for n in ("w_rnn_out", "w_na_out", "w_out")]),
        "w_ff": np.concatenate(units), "ffn_p": conv.reshape(P, FC, 8), "consts": table, "neg_row": rows,
    }
    arrays = {k: np.ascontiguousarray(v) for k, v in arrays.items()}
    nc = bacc.Bacc("TRN2", target_bir_lowering=False, num_devices=1, dynamic_dma_scratch_size=4096)
    aps = {k: nc.dram_tensor(k, v.shape, mybir.dt.from_np(v.dtype), kind="ExternalInput").ap()
           for k, v in arrays.items()}
    aps["outT"] = nc.dram_tensor("outT", (KC, P, T), F32, kind="ExternalOutput").ap()
    for k in ("yr_d", "yn_d", "smr_d", "smn_d"):
        aps[k] = nc.dram_tensor(k, (KC, P, T), F32, kind="Internal").ap()
    aps["bias_d"] = nc.dram_tensor("bias_d", (P, 2 * PAIRS, 16, GW), F32, kind="Internal").ap()
    build(nc, **aps)
    r = run_bass_kernel_spmd(nc, [arrays], core_ids=[0])
    out = np.asarray(r.results[0]["outT"])
    return np.ascontiguousarray(out.reshape(D, T).T)[None]
```

```python
from contextlib import ExitStack

import numpy as np

import concourse.bass as bass
from concourse import mybir

F32 = mybir.dt.float32
F32R = mybir.dt.float32r
ALU = mybir.AluOpType
ACT = mybir.ActivationFunctionType
AX_X = mybir.AxisListType.X

P = 128
D = 1024
KC = D // P
T = 1024
C = 256
N = C + T
GW = 64
HD = 64
PAIRS = KC
NT = T // P
NCT = C // P
WIN = 8
FF = 2816
FC = FF // P
GROUPS = (8, 7, 7)
UP_UNITS = 2 * FC
FF_UNITS = UP_UNITS + KC * len(GROUPS)
EPS = 1e-6
NEG = -1e30
HALF = 512
assert sum(GROUPS) == FC and GROUPS[0] == KC

KEY_ROW0 = [min(max(2 * t - WIN // 2, 0), 2 * NT - WIN) for t in range(NT)]
KEY_ROWS = [9 if 2 <= t <= 5 else 8 for t in range(NT)]
BIAS_ROW0 = [KEY_ROW0[t] - 2 * t + WIN - 1 for t in range(NT)]
BIAS_ROWS = 14


def three_passes(pe, out, w_hi, w_lo, x_hi, x_lo, chunks):
    last = None
    for k in range(chunks):
        pe.matmul(out, w_hi(k), x_hi(k), start=(k == 0), stop=False)
        pe.matmul(out, w_hi(k), x_lo(k), start=False, stop=False)
        last = pe.matmul(out, w_lo(k), x_hi(k), start=False, stop=(k == chunks - 1))
    return last


def build(nc, xT, ctxT, svec, c_row, w_mod, w_modT, b_mod, gains, w_fm, w_qkv, lru_w, lru_p, qk_g, rpb,
          w_mix, w_ff, ffn_p, consts, outT, yr_d, yn_d, smr_d, smn_d, bias_d):
    with ExitStack() as top:
        def sem(name):
            return top.enter_context(nc.semaphore(name))

        def sbuf(stack, name, shape, dt=F32):
            return stack.enter_context(nc.sbuf_tensor(name, shape, dt))

        def psum(stack, name, shape):
            return stack.enter_context(nc.psum_tensor(name, shape, F32))

        mod = sbuf(top, "mod", [P, 6 * KC, 2])
        gain = sbuf(top, "gain", [P, 2, KC])
        bm = sbuf(top, "bm", [P, 6 * KC])
        ones = sbuf(top, "ones", [P, P])
        eps = sbuf(top, "eps", [P, 1])
        lrup = sbuf(top, "lrup", [P, 11, KC])
        decay = sbuf(top, "decay", [P, 2, 2, KC])
        ab = ExitStack()
        xnh = sbuf(ab, "xnh", [P, KC, N], F32R)
        xnl = sbuf(ab, "xnl", [P, KC, N], F32R)
        setup_block(nc, sem, sbuf, psum, xT, ctxT, svec, w_mod, b_mod, gains, lru_p,
                    mod, bm, gain, ones, eps, lrup, decay, xnh, xnl)
        mixer_block(nc, sem, sbuf, psum, w_fm, w_qkv, lru_w, qk_g, rpb, bias_d, consts,
                    eps, lrup, decay, xnh, xnl, yr_d, yn_d, smr_d, smn_d)
        ab.close()
        with ExitStack() as cd:
            x1 = sbuf(cd, "x1", [P, KC, T])
            sc = sbuf(cd, "sc", [P, D])
            merge_block(nc, sem, sbuf, psum, xT, w_mix, c_row, w_modT, bm, mod, sc, x1, yr_d, yn_d, smr_d, smn_d)
            ffn_block(nc, sem, sbuf, psum, w_ff, ffn_p, w_modT, bm, mod, sc, gain, ones, eps, x1, outT)


def setup_block(nc, sem, sbuf, psum, xT, ctxT, svec, w_mod, b_mod, gains, lru_p,
                mod, bm, gain, ones, eps, lrup, decay, xnh, xnl):
    SL = 2 * KC
    with ExitStack() as st:
        xs = sbuf(st, "xs", [P, KC, N])
        sq = sbuf(st, "sq", [P, 2, N])
        rs = sbuf(st, "rs", [P, N])
        tmp = sbuf(st, "tmp_norm", [P, N])
        wm = sbuf(st, "wm", [P, SL, KC, P])
        sv = sbuf(st, "sv", [P, KC, 2])
        gm = sbuf(st, "gm", [P, 2, KC])
        la = sbuf(st, "la", [P, 6, 2, KC])
        ss = psum(st, "ss", [P, 3, HALF])
        mp = psum(st, "mp", [P, SL, 2])

        small_in = sem("a_small_in")
        x_in = [sem(f"a_x_in{k}") for k in range(KC)]
        wm_in = [sem(f"a_wm_in{s}") for s in range(SL)]
        memset_done = sem("a_memset")
        silu_done = sem("a_silu")
        squared = sem("a_squared")
        sq_used = sem("a_sq_used")
        mod_ready = sem("a_mod_ready")
        mod_out = sem("a_mod_out")
        root = sem("a_root")
        scaled = sem("a_scaled")
        hi_done = sem("a_hi")
        dve_step = sem("a_dve_step")
        normed = sem("a_normed")
        lam_abs = sem("a_lam_abs")
        lam_exp = sem("a_lam_exp")

        with nc.Block() as block:
            @block.sync
            def _(sp):
                sp.dma_start(sv[:, :, :], svec).then_inc(small_in, 16)
                sp.dma_start(bm[:, :], b_mod).then_inc(small_in, 16)
                sp.dma_start(gain[:, :, :], gains).then_inc(small_in, 16)
                sp.dma_start(lrup[:, :, :], lru_p).then_inc(small_in, 16)
                for k in range(KC):
                    sp.dma_start(xs[:, k, 0:C], ctxT[k]).then_inc(x_in[k], 16)
                    sp.dma_start(xs[:, k, C:N], xT[k]).then_inc(x_in[k], 16)
                for s in range(SL):
                    sp.dma_start(wm[:, s, :, :], w_mod[s]).then_inc(wm_in[s], 16)

            @block.gpsimd
            def _(pool):
                pool.memset(ones[:, :], 1.0).then_inc(memset_done, 1)
                pool.memset(eps[:, :], EPS).then_inc(memset_done, 1)

            @block.tensor
            def _(pe):
                pe.wait_ge(memset_done, 2)
                for k in range(KC):
                    pe.wait_ge(squared, k + 1)
                    for b, (c0, c1) in enumerate(((0, 512), (512, 1024), (1024, N))):
                        last = pe.matmul(ss[:, b, 0:c1 - c0], ones[:, :], sq[:, k % 2, c0:c1],
                                         start=(k == 0), stop=(k == KC - 1))
                    last.then_inc(sq_used, 1)
                pe.wait_ge(silu_done, 1)
                for b in range(SL):
                    pe.wait_ge(wm_in[b], 16)
                    for k in range(KC):
                        last = pe.matmul(mp[:, b, :], wm[:, b, k, :], sv[:, k, :],
                                         start=(k == 0), stop=(k == KC - 1))
                last.then_inc(mod_ready, 1)

            @block.scalar
            def _(act):
                act.wait_ge(small_in, 64)
                act.activation(sv[:, :, :], sv[:, :, :], ACT.Silu).then_inc(silu_done, 1)
                act.wait_ge(lam_abs, 1)
                act.activation(la[:, 1], la[:, 0], ACT.Exp).then_inc(lam_exp, 1)
                for k in range(KC):
                    act.wait_ge(x_in[k], 32)
                    if k >= 2:
                        act.wait_ge(sq_used, k - 1)
                    act.activation(sq[:, k % 2, :], xs[:, k, :], ACT.Square).then_inc(squared, 1)
                act.wait_ge(sq_used, KC)
                act.activation(tmp[:, :], ss[:, :, :].rearrange("p a b -> p (a b)")[:, 0:N], ACT.Sqrt,
                               bias=eps[:, :], scale=1.0 / D).then_inc(root, 1)
                for k in range(KC):
                    act.wait_ge(scaled, k + 1)
                    act.copy(xnh[:, k, :], xs[:, k, :]).then_inc(hi_done, 1)

            @block.vector
            def _(dve):
                steps = [0]

                def then(ins):
                    steps[0] += 1
                    ins.then_inc(dve_step, 1)
                    dve.wait_ge(dve_step, steps[0])

                dve.wait_ge(small_in, 64)
                lam = lrup[:, 9:11, :]
                dve.scalar_tensor_tensor(la[:, 0], lam, -1.0, lam, ALU.mult, ALU.min).then_inc(lam_abs, 1)
                dve.wait_ge(lam_exp, 1)
                then(dve.tensor_scalar(la[:, 2], la[:, 1], 2.0, None, ALU.add))
                then(dve.reciprocal(la[:, 2], la[:, 2]))
                then(dve.tensor_tensor(la[:, 2], la[:, 1], la[:, 2], ALU.mult))
                then(dve.tensor_tensor(la[:, 3], la[:, 2], la[:, 2], ALU.mult))
                then(dve.tensor_scalar(la[:, 4], la[:, 3], 1.0 / 15, None, ALU.mult))
                for odd in (13, 11, 9, 7, 5, 3):
                    then(dve.scalar_tensor_tensor(la[:, 4], la[:, 4], 1.0 / odd, la[:, 3], ALU.add, ALU.mult))
                then(dve.scalar_tensor_tensor(la[:, 4], la[:, 4], 1.0, la[:, 2], ALU.add, ALU.mult))
                then(dve.tensor_scalar(la[:, 5], lam, -1.0, 0.0, ALU.mult, ALU.max))
                then(dve.scalar_tensor_tensor(la[:, 5], la[:, 4], 2.0, la[:, 5], ALU.mult, ALU.add))
                then(dve.tensor_scalar(decay[:, 0], la[:, 5], -8.0, None, ALU.mult))
                then(dve.tensor_scalar(decay[:, 1], la[:, 5], 8.0, None, ALU.mult))

                dve.wait_ge(root, 1)
                then(dve.reciprocal(rs[:, :], tmp[:, :]))
                then(dve.tensor_scalar(tmp[:, :], ss[:, :, :].rearrange("p a b -> p (a b)")[:, 0:N],
                                       -0.5 / D, -0.5 * EPS, ALU.mult, ALU.add))
                then(dve.tensor_tensor(tmp[:, :], tmp[:, :], rs[:, :], ALU.mult))
                then(dve.tensor_tensor(tmp[:, :], tmp[:, :], rs[:, :], ALU.mult))
                then(dve.scalar_tensor_tensor(rs[:, :], tmp[:, :], 1.5, rs[:, :], ALU.add, ALU.mult))
                for k in range(KC):
                    dve.tensor_tensor(xs[:, k, :], xs[:, k, :], rs[:, :], ALU.mult).then_inc(normed, 1)
                dve.wait_ge(mod_ready, 1)
                dve.tensor_tensor(mod[:, 0:SL, :], mp[:, :, :],
                                  bm[:, 0:SL].unsqueeze(2).broadcast_to([P, SL, 2]), ALU.add).then_inc(mod_out, 1)
                dve.wait_ge(mod_out, 1)
                for w in range(2):
                    then(dve.scalar_tensor_tensor(gm[:, w, :], mod[:, KC:2 * KC, w], 1.0, gain[:, 0, :],
                                                  ALU.add, ALU.mult))
                dve.wait_ge(normed, KC)
                for k in range(KC + 1):
                    if k < KC:
                        dve.tensor_scalar(xs[:, k, 0:C], xs[:, k, 0:C], gm[:, 1, k:k + 1], mod[:, k, 1:2],
                                          ALU.mult, ALU.add)
                        dve.tensor_scalar(xs[:, k, C:N], xs[:, k, C:N], gm[:, 0, k:k + 1], mod[:, k, 0:1],
                                          ALU.mult, ALU.add).then_inc(scaled, 1)
                    if k >= 1:
                        dve.wait_ge(hi_done, k)
                        dve.tensor_tensor(xnl[:, k - 1, :], xs[:, k - 1, :], xnh[:, k - 1, :].bitcast(F32),
                                          ALU.subtract)


XR, Q0, Q1, Q2, G, MR, MN = range(7)
RAW_SLOT = [0, 1, 2, 0, 1, 2, 1]
RAW_USE = [(0, 2), (0, 3), (0, 2), (1, 2), (1, 3), (1, 2), (2, 3)]
UNITS = 7
F_USES = 21
Q_TILES = NT + NCT
ATT = 2 * NT


def mixer_block(nc, sem, sbuf, psum, w_fm, w_qkv, lru_w, qk_g, rpb, bias_d, consts,
                eps, lrup, decay, xnh, xnl, yr_d, yn_d, smr_d, smn_d):
    with ExitStack() as st:
        raw = sbuf(st, "raw", [P, 3, 1024])
        fh = sbuf(st, "fh", [P, 2, KC, P], F32R)
        fl = sbuf(st, "fl", [P, 2, KC, P], F32R)
        qkv = sbuf(st, "qkv", [P, Q_TILES, 384])
        stage = sbuf(st, "stage", [P, HALF])
        bias = sbuf(st, "bias", [P, 2, BIAS_ROWS + 2, GW])
        cst = sbuf(st, "cst", [P, P + 3 * GW + 2 * NT * HD])
        gqk = sbuf(st, "gqk", [P, 2, HD])
        sqs = sbuf(st, "sqs", [P, 2, 256])
        ssq = sbuf(st, "ssq", [P, Q_TILES, 4])
        rstd = sbuf(st, "rstd", [P, 2, Q_TILES, 4])
        lw = sbuf(st, "lw", [P, 4, P])
        lp = sbuf(st, "lp", [P, 15])
        stat = sbuf(st, "stat", [P, ATT, 7])
        ysc = sbuf(st, "ysc", [P, ATT, 2])
        ytmp = sbuf(st, "ytmp", [P, 2, HD])
        zero = sbuf(st, "zero", [P, 3])
        one = sbuf(st, "one", [P, 1])
        ytok = sbuf(st, "ytok", [P, 4, P])
        yT = sbuf(st, "yT", [P, HALF])
        ident = cst[:, 0:P]
        colmask = cst[:, P:P + GW]
        edgemask = cst[:, P + GW:P + 3 * GW].rearrange("p (a c) -> p a c", c=GW)
        cosT = cst[:, P + 3 * GW:P + 3 * GW + NT * HD].rearrange("p (t f) -> p t f", f=HD)
        sinT = cst[:, P + 3 * GW + NT * HD:].rearrange("p (t f) -> p t f", f=HD)
        with ExitStack() as rnn:
            qh = sbuf(rnn, "qh", [P, KC, 384], F32R)
            ql = sbuf(rnn, "ql", [P, KC, 384], F32R)
            pad = sbuf(rnn, "pad", [P, 1288])
            xc = sbuf(rnn, "xc", [P, N])
            h0 = sbuf(rnn, "h0", [P, N])
            gD = sbuf(rnn, "gD", [P, N])
            gR = sbuf(rnn, "gR", [P, N])
            gI = sbuf(rnn, "gI", [P, N])
            gA = sbuf(rnn, "gA", [P, N])
            gel = sbuf(rnn, "gel", [P, T])
        att = st.enter_context(ExitStack())
        qpS = sbuf(att, "qpS", [P, 2, T], F32R)
        qrS = sbuf(att, "qrS", [P, 2, T], F32R)
        kS = sbuf(att, "kS", [P, 2, T], F32R)
        kX = sbuf(att, "kX", [P, 2, T], F32R)
        kcS = sbuf(att, "kcS", [P, 2, C], F32R)
        kcX = sbuf(att, "kcX", [P, 2, C], F32R)
        vS = sbuf(att, "vS", [P, Q_TILES, 2, P], F32R)
        with ExitStack() as rot:
            qrot = sbuf(rot, "qrot", [P, T])
            krot = sbuf(rot, "krot", [P, T])
            swp = sbuf(rot, "swp", [P, T])
        probT = [[sbuf(att, f"probT{part}{n}", [P, 7, P], F32R) for n in range(2)] for part in "HL"]
        prob = [sbuf(att, f"prob{n}", [P, 13, GW]) for n in range(3)]

        f_ps = [psum(st, f"f_ps{b}", [P, HALF]) for b in range(2)]
        q_ps = [psum(st, f"q_ps{b}", [P, HALF]) for b in range(2)]
        t_ps = [psum(st, f"t_ps{b}", [P, HALF]) for b in range(2)]
        o_ps = [psum(st, f"o_ps{b}", [P, HALF]) for b in range(2)]
        tr_banks = t_ps + o_ps

        raw_in = [sem(f"b_raw_in{s}") for s in range(3)]
        w_hi = sem("b_w_hi")
        w_lo = sem("b_w_lo")
        f_full = sem("b_f_full")
        f_free = sem("b_f_free")
        q_full = sem("b_q_full")
        q_free = sem("b_q_free")
        sq_used = sem("b_sq_used")
        conv_done = sem("b_conv_done")
        lw_in = sem("b_lw_in")
        decayed = sem("b_decayed")
        one_minus = sem("b_one_minus")
        rooted = sem("b_rooted")
        gates_free = sem("b_gates_free")
        dve_step = sem("b_dve_step")
        rms_root = sem("b_rms_root")
        yr_ready = sem("b_yr_ready")
        yr_out = sem("b_yr_out")
        stage_out = sem("b_stage_out")
        rope_q = sem("b_rope_q")
        rope_k = sem("b_rope_k")
        normed = sem("b_normed")
        tr_full = sem("b_tr_full")
        tr_hi = sem("b_tr_hi")
        tr_lo = sem("b_tr_lo")
        v_hi = sem("b_v_hi")
        v_lo = sem("b_v_lo")
        zeroed = sem("b_zeroed")
        high_exchanged = sem("b_high_exchanged")
        low_exchanged = sem("b_low_exchanged")
        bias_set = sem("b_bias_set")
        bias_in = sem("b_bias_in")
        bias_done = sem("b_bias_done")
        const_in = sem("b_const_in")
        set_done = sem("b_set_done")
        qk_done = sem("b_qk_done")
        bound_done = sem("b_bound_done")
        exp_done = sem("b_exp_done")
        pt_full = sem("b_pt_full")
        pt_hi = sem("b_pt_hi")
        pt_lo = sem("b_pt_lo")
        pv_done = sem("b_pv_done")
        y_step = sem("b_y_step")
        y_done = sem("b_y_done")
        yt_full = sem("b_yt_full")
        yt_ready = sem("b_yt_ready")
        yt_out = sem("b_yt_out")

        def hi_parts(u):
            if u in (Q0, Q1, Q2):
                j = u - Q0
                return (qh[:, :, :].rearrange("p k c -> p (k c)")[:, 1024 * j:1024 * j + 1024],
                        ql[:, :, :].rearrange("p k c -> p (k c)")[:, 1024 * j:1024 * j + 1024])
            s = 0 if u in (XR, MR) else 1
            return (fh[:, s, :, :].rearrange("p k c -> p (k c)"), fl[:, s, :, :].rearrange("p k c -> p (k c)"))

        values = qkv[:, :, 2 * P:3 * P].rearrange("p t (h f) -> p t h f", f=HD)

        def raw_wait(eng, u, i):
            use, uses = RAW_USE[u]
            eng.wait_ge(raw_in[RAW_SLOT[u]], (i * uses + use + 1) * 16)

        SEGS = ((0, C), (C, C + HALF), (C + HALF, N))
        TR_JOBS = ((kcS, 0, 2), (kS, 0, 4), (kS, 4, 4), (qpS, 0, 4), (qpS, 4, 4), (qrS, 0, 4), (qrS, 4, 4))
        GATES_AFTER = {1: (0, (0, 1)), 2: (0, (2, 3)), 3: (0, (4, 5)),
                       7: (1, (0, 1)), 8: (1, (2, 3)), 9: (1, (4, 5))}
        HEAD_ROWS = (slice(0, HD), slice(HD, P))

        with nc.Block() as block:
            @block.sync
            def _(sp):
                sp.dma_start(cst[:, :], consts).then_inc(const_in, 16)
                sp.dma_start(gqk[:, :, :], bass.AP(tensor=qk_g.tensor, offset=0, ap=[[0, P], [HD, 2], [1, HD]]))\
                  .then_inc(const_in, 16)

                def load(u, i):
                    if u in (Q0, Q1, Q2):
                        src = w_qkv[bass.ds(i, 1), :, 1024 * (u - Q0):1024 * (u - Q0) + 1024]
                    else:
                        src = w_fm[bass.ds(i * 4 + (u - 3 if u else 0), 1), :, :]
                    sp.dma_start(raw[:, RAW_SLOT[u], :], src.rearrange("a p c -> (a p) c"))\
                      .then_inc(raw_in[RAW_SLOT[u]], 16)

                for u in (XR, Q0, Q1):
                    load(u, 0)
                sp.wait_ge(w_lo, XR + 1)
                load(Q2, 0)

                def store(dst, i, half, src, done):
                    rows = dst[bass.ds(i, 1), :, :] if half is None else \
                        dst[bass.ds(i, 1), :, HALF * half:HALF * half + HALF]
                    sp.dma_start(rows.rearrange("a p t -> (a p) t"), src).then_inc(done, 16)

                def turn(i, first, last):
                    def load_bias():
                        for r in range(2):
                            sp.dma_start(bias[GW * r:GW * r + GW, :, 0:BIAS_ROWS, :].rearrange("p h e c -> p h (e c)"),
                                         bias_d[:, bass.ds(i * 2, 2), 2 - r:2 - r + BIAS_ROWS, :]
                                         .rearrange("p h e c -> p h (e c)")).then_inc(bias_in, 16)

                    if not first:
                        sp.wait_ge(bound_done, i * ATT)
                        load_bias()
                    if not first:
                        sp.wait_ge(f_full, i * F_USES)
                    sp.dma_start(lw[:, :, :].rearrange("p a b -> p (a b)"),
                                 lru_w[bass.ds(i, 1)].rearrange("a p c -> (a p) c")).then_inc(lw_in, 16)
                    def next_block(u, before, n):
                        sp.wait_ge(w_lo, i * UNITS + before + 1)
                        load(u, n)

                    if not first:
                        sp.wait_ge(yt_ready, i * 2)
                        store(yn_d, i - 1, 1, yT[:, :], yt_out)
                    next_block(G, Q0, i)
                    next_block(MR, Q1, i)
                    next_block(MN, G, i)
                    if not last:
                        next_block(XR, Q2, i + 1)
                    if first:
                        sp.wait_ge(bias_set, 16)
                        load_bias()
                    sp.wait_ge(yr_ready, i + 1)
                    store(yr_d, i, None, gel[:, :], yr_out)
                    for j, dst in enumerate((smr_d, smr_d, smn_d, smn_d)):
                        sp.wait_ge(f_free, i * F_USES + (17 + j + 1))
                        store(dst, i, j % 2, stage[:, :], stage_out)
                        if not last and j in (1, 3):
                            next_block(*((Q0, MN), (Q1, MR))[j // 2], i + 1)
                    if not last:
                        sp.wait_ge(w_lo, i * UNITS + (UNITS + XR + 1))
                        load(Q2, i + 1)
                    sp.wait_ge(yt_ready, i * 2 + 1)
                    store(yn_d, i, 0, yT[:, :], yt_out)

                turn(0, True, False)
                with sp.Fori(1, PAIRS - 1) as i:
                    turn(i, False, False)
                turn(PAIRS - 1, False, True)
                sp.wait_ge(yt_ready, PAIRS * 2)
                store(yn_d, PAIRS - 1, 1, yT[:, :], yt_out)
                sp.wait_ge(yr_out, PAIRS * 16)
                sp.wait_ge(stage_out, PAIRS * 64)
                sp.wait_ge(yt_out, PAIRS * 32)

            @block.gpsimd
            def _(pool):
                pool.memset(ssq[:, :, :], 1.0).then_inc(set_done, 1)
                pool.memset(zero[:, :], 0.0).then_inc(set_done, 1)
                pool.memset(one[:, :], 1.0).then_inc(set_done, 1)
                pool.wait_ge(set_done, 3)
                pool.wait_ge(const_in, 32)

                def turn(i, first):
                    if not first:
                        pool.wait_ge(qk_done, i * ATT)
                    for c0, n in ((0, 2), (2 + C, 3), (261 + T, 3)):
                        pool.tensor_tensor(pad[:, c0:c0 + n], zero[:, 0:n], zero[:, 0:n], ALU.add)\
                            .then_inc(zeroed, 1)
                    pool.wait_ge(bias_in, i * 32 + 32)
                    pool.tensor_tensor(bias[:, :, BIAS_ROWS:, :], bias[:, :, 2:11:8, :],
                                       edgemask.unsqueeze(1).broadcast_to([P, 2, 2, GW]), ALU.add)\
                        .then_inc(bias_done, 1)
                    pool.wait_ge(bias_done, i * 3 + 1)
                    for h in range(2):
                        pool.tensor_tensor(bias[:, h, 0:BIAS_ROWS, :], bias[:, h, 0:BIAS_ROWS, :],
                                           colmask.unsqueeze(1).broadcast_to([P, BIAS_ROWS, GW]), ALU.add)\
                            .then_inc(bias_done, 1)
                    pool.wait_ge(bias_done, i * 3 + 3)
                    copies = 0
                    for n, (src, t0, tiles) in enumerate(TR_JOBS):
                        if src is kS or src is kcS:
                            pool.wait_ge(tr_lo, i * len(TR_JOBS) + n + 1)
                            cols = slice(P * t0, P * (t0 + tiles))
                            for h, rows in enumerate(HEAD_ROWS):
                                if copies:
                                    pool.wait_ge(low_exchanged, i * 6 + copies)
                                copies += 1
                                part = src[HEAD_ROWS[1 - h], h, cols].bitcast(F32)
                                pool.tensor_tensor((kX if src is kS else kcX)[rows, h, cols], part,
                                                   one[HEAD_ROWS[1 - h], :].broadcast_to(part.shape),
                                                   ALU.mult).then_inc(low_exchanged, 1)

                turn(0, True)
                with pool.Fori(1, PAIRS) as i:
                    pool.wait_ge(low_exchanged, i * 6)
                    turn(i, False)

            @block.tensor
            def _(pe):
                def f_bank(i, j):
                    if j >= 2:
                        pe.wait_ge(f_free, i * F_USES + j - 1)
                    return f_ps[j % 2]

                def fm(i, j, u, slot, c0, c1):
                    bank = f_bank(i, j)
                    return three_passes(pe, bank[:, 0:c1 - c0], lambda k: fh[:, slot, k, :],
                                        lambda k: fl[:, slot, k, :], lambda k: xnh[:, k, c0:c1],
                                        lambda k: xnl[:, k, c0:c1], KC).then_inc(f_full, 1)

                def fm_block(i, j, u, segs):
                    pe.wait_ge(w_lo, i * UNITS + u + 1)
                    for n, (c0, c1) in enumerate(segs):
                        fm(i, j + n, u, 0 if u in (XR, MR) else 1, c0, c1)

                def q_tile(i, t):
                    c0 = C + P * t if t < NT else P * (t - NT)
                    w0 = 0 if t < NT else P
                    if t >= 2:
                        pe.wait_ge(q_free, i * Q_TILES + t - 1)
                    last = three_passes(pe, q_ps[t % 2][:, w0:384], lambda k: xnh[:, k, c0:c0 + P],
                                        lambda k: xnl[:, k, c0:c0 + P], lambda k: qh[:, k, w0:384],
                                        lambda k: ql[:, k, w0:384], KC)
                    last.then_inc(q_full, 1)

                def gate_pieces(i, d, pieces):
                    if d == 0 and pieces[0] == 0:
                        pe.wait_ge(lw_in, i * 16 + 16)
                        pe.wait_ge(conv_done, i + 1)
                    for n in pieces:
                        c0, c1 = SEGS[n % 3]
                        bank = f_bank(i, 3 + 6 * d + n)
                        pe.matmul(bank[:, 0:c1 - c0], lw[:, 2 * (n // 3) + d, :], xc[:, c0:c1],
                                  start=True, stop=True).then_inc(f_full, 1)

                def transposes(i, jobs):
                    for n in jobs:
                        dst, t0, tiles = TR_JOBS[n]
                        if n == 0:
                            pe.wait_ge(normed, i * 2 + 2)
                            pe.wait_ge(rope_k, i + 1)
                        if n == 5:
                            pe.wait_ge(rope_q, i + 1)
                        if n >= 4:
                            pe.wait_ge(tr_lo, i * len(TR_JOBS) + n - 3)
                        for t in range(t0, t0 + tiles):
                            src = (qkv[:, t, 0:P] if dst is qpS else qkv[:, NT + t, P:2 * P] if dst is kcS
                                   else (qrot if dst is qrS else krot)[:, P * t:P * t + P])
                            last = pe.transpose(tr_banks[n % 4][:, P * (t - t0):P * (t - t0) + P], src, ident)
                        last.then_inc(tr_full, 1)

                def scores(i, u):
                    t, h = u // 2, u % 2
                    a, b = (f_ps if u % 2 == 0 else q_ps)
                    if u >= 2:
                        pe.wait_ge(exp_done, i * ATT + u - 1)
                    r0 = KEY_ROW0[t]
                    inner = KEY_ROWS[t] == 9
                    k0, n = (r0 + inner) * GW, HALF - GW * inner
                    q = qrS[:, h, P * t:P * t + P]
                    for part, k in enumerate((kS, kX)):
                        pe.matmul(a[:, 0:n], q, k[:, h, k0:k0 + n], start=(part == 0), stop=(part == 1))
                    if inner:
                        for part, k in enumerate((kS, kX)):
                            rows = k[:, h, :].rearrange("p (r c) -> p r c", c=GW)[:, r0:r0 + 9:8, :]
                            pe.matmul(b[:, 0:P], q, rows, start=(part == 0), stop=(part == 1))
                    for part, k in enumerate((kcS, kcX)):
                        last = pe.matmul(b[:, P:P + C], qpS[:, h, P * t:P * t + P], k[:, h, :],
                                         start=(part == 0), stop=(part == 1))
                    last.then_inc(qk_done, 1)

                def prob_transposes(i, u):
                    p = prob[u % 3][:, :, :].rearrange("p r c -> p (r c)")
                    pe.wait_ge(exp_done, i * ATT + u + 1)
                    if u >= 1:
                        pe.wait_ge(pt_lo, i * (2 * ATT) + 2 * u - 1)
                    for b in range(4):
                        last = pe.transpose(t_ps[0][:, P * b:P * b + P], p[:, P * b:P * b + P], ident)
                    last.then_inc(pt_full, 1)
                    if u >= 1:
                        pe.wait_ge(pt_lo, i * (2 * ATT) + 2 * u)
                    for b in range(2):
                        last = pe.transpose(t_ps[1][:, P + P * b:2 * P + P * b],
                                            p[:, 576 + P * b:576 + P * b + P], ident)
                    if KEY_ROWS[u // 2] == 9:
                        last = pe.transpose(t_ps[1][0:GW, 0:P], p[:, HALF:HALF + GW], ident)
                    last.then_inc(pt_full, 1)

                def weighted_values(i, u):
                    t, h = u // 2, u % 2
                    out = o_ps[u % 2][:, 0:P]
                    pe.wait_ge(pt_lo, i * (2 * ATT) + 2 * u + 2)
                    if u == 0:
                        pe.wait_ge(v_lo, i + 1)
                    if u >= 2:
                        pe.wait_ge(y_done, i * ATT + u - 1)
                    if u == 9:
                        pe.wait_ge(yt_ready, i * 2 + 1)
                    blocks = [(b, P, KEY_ROW0[t] // 2 + b) for b in range(4)]
                    if KEY_ROWS[t] == 9:
                        blocks.append((4, GW, KEY_ROW0[t] // 2 + 4))
                    blocks += [(5 + b, P, NT + b) for b in range(2)]
                    for b, keys, tile in blocks:
                        for part in range(2):
                            last = pe.matmul(out, probT[part][u % 2][0:keys, b, :], vS[0:keys, tile, h, :],
                                             start=(b == 0 and part == 0), stop=(b == 6 and part == 1))
                    last.then_inc(pv_done, 1)

                def y_transposes(i, j):
                    pe.wait_ge(y_done, i * ATT + (8 * j + 8))
                    for b in range(4):
                        last = pe.transpose(o_ps[1][:, P * b:P * b + P], ytok[:, b, :], ident)
                    last.then_inc(yt_full, 1)

                def turn(i, first):
                    pe.wait_ge(w_lo, i * UNITS + XR + 1)
                    fm(i, 0, XR, 0, *SEGS[0])
                    if not first:
                        y_transposes(i - 1, 1)
                    fm(i, 1, XR, 0, *SEGS[1])
                    fm(i, 2, XR, 0, *SEGS[2])
                    pe.wait_ge(w_lo, i * UNITS + Q2 + 1)
                    for t in range(Q_TILES):
                        q_tile(i, t)
                        if t in GATES_AFTER:
                            gate_pieces(i, *GATES_AFTER[t])
                    fm_block(i, 15, G, SEGS[1:])
                    pe.wait_ge(w_lo, i * UNITS + MR + 1)
                    fm(i, 17, MR, 0, *SEGS[1])
                    fm(i, 18, MR, 0, *SEGS[2])
                    transposes(i, range(0, 3))
                    pe.wait_ge(w_lo, i * UNITS + MN + 1)
                    fm(i, 19, MN, 1, *SEGS[1])
                    transposes(i, range(3, 7))
                    fm(i, 20, MN, 1, *SEGS[2])
                    pe.wait_ge(f_free, i * F_USES + F_USES)
                    pe.wait_ge(q_free, i * Q_TILES + Q_TILES)
                    pe.wait_ge(tr_lo, i * len(TR_JOBS) + len(TR_JOBS))
                    pe.wait_ge(high_exchanged, i * 6 + 6)
                    pe.wait_ge(low_exchanged, i * 6 + 6)
                    scores(i, 0)
                    scores(i, 1)
                    for u in range(ATT):
                        if u + 2 < ATT:
                            scores(i, u + 2)
                        prob_transposes(i, u)
                        if u == 9:
                            y_transposes(i, 0)
                        if u >= 1:
                            weighted_values(i, u - 1)
                    weighted_values(i, ATT - 1)
                    pe.wait_ge(exp_done, i * ATT + ATT)

                pe.wait_ge(const_in, 32)
                turn(0, True)
                with pe.Fori(1, PAIRS) as i:
                    turn(i, False)
                y_transposes(PAIRS - 1, 1)

            @block.scalar
            def _(act):
                def split_hi(u, i):
                    raw_wait(act, u, i)
                    act.copy(hi_parts(u)[0], raw[:, RAW_SLOT[u], :]).then_inc(w_hi, 1)

                def f_evac(i, j, out, func, **kw):
                    act.wait_ge(f_full, i * F_USES + j + 1)
                    return act.activation(out, f_ps[j % 2][:, 0:out.shape[1]], func, **kw).then_inc(f_free, 1)

                def q_evac(i, t):
                    w0 = 0 if t < NT else P
                    act.wait_ge(q_full, i * Q_TILES + t + 1)
                    act.copy(qkv[:, t, w0:384], q_ps[t % 2][:, w0:384])
                    if t >= 2:
                        act.wait_ge(sq_used, i * Q_TILES + t - 1)
                    act.activation(sqs[:, t % 2, w0:256], q_ps[t % 2][:, w0:256], ACT.Square).then_inc(q_free, 1)

                def gate_pieces(i, d, pieces):
                    if d == 1 and pieces[0] == 0:
                        act.wait_ge(gates_free, i + 1)
                    for n in pieces:
                        c0, c1 = SEGS[n % 3]
                        f_evac(i, 3 + 6 * d + n, (gR, gI)[n // 3][:, c0:c1], ACT.Sigmoid,
                               bias=lp[:, 5 + 2 * (n // 3) + d:6 + 2 * (n // 3) + d])

                def decays(i, d):
                    act.wait_ge(f_free, i * F_USES + 9 + 6 * d)
                    act.activation(gA[:, :], gR[:, :], ACT.Exp, scale=lp[:, 11 + d:12 + d])\
                       .then_inc(decayed, 1)
                    act.activation(gR[:, :], gR[:, :], ACT.Tanh, scale=lp[:, 13 + d:14 + d])
                    act.wait_ge(decayed, 4 * i + 2 * d + 1)
                    act.activation(gD[:, :], gA[:, :], ACT.Square).then_inc(decayed, 1)

                def root(i, d):
                    act.wait_ge(one_minus, 2 * i + d + 1)
                    act.activation(gD[:, :], gD[:, :], ACT.Sqrt).then_inc(rooted, 1)

                def tr_high(i, jobs):
                    for n in jobs:
                        dst, t0, tiles = TR_JOBS[n]
                        if dst is kcS:
                            act.wait_ge(yr_ready, i + 1)
                        act.wait_ge(tr_full, i * len(TR_JOBS) + n + 1)
                        for h, rows in enumerate(HEAD_ROWS):
                            last = act.copy(dst[rows, h, P * t0:P * (t0 + tiles)],
                                            tr_banks[n % 4][rows, 0:P * tiles])
                        last.then_inc(tr_hi, 1)
                        if dst is kS or dst is kcS:
                            act.wait_ge(tr_hi, i * len(TR_JOBS) + n + 1)
                            for h, rows in enumerate(HEAD_ROWS):
                                act.copy((kX if dst is kS else kcX)[HEAD_ROWS[1 - h], h, P * t0:P * (t0 + tiles)],
                                         dst[rows, h, P * t0:P * (t0 + tiles)].bitcast(F32))\
                                    .then_inc(high_exchanged, 1)

                def v_high(i):
                    act.wait_ge(yr_ready, i + 1)
                    act.copy(vS[:, :, :, 0:HD], values).then_inc(v_hi, 1)

                def soft(i, u):
                    b = (f_ps if u % 2 == 0 else q_ps)[1]
                    act.wait_ge(bound_done, i * ATT + u + 1)
                    rows = KEY_ROWS[u // 2]
                    act.activation(prob[u % 3][:, 0:rows, :], prob[u % 3][:, 0:rows, :], ACT.Exp,
                                   bias=stat[:, u, 4:5], accum_out=stat[:, u, 5:6])
                    act.activation(prob[u % 3][:, 9:13, :], b[:, P:P + C].rearrange("p (r c) -> p r c", c=GW),
                                   ACT.Exp, bias=stat[:, u, 4:5], accum_out=stat[:, u, 6:7])\
                       .then_inc(exp_done, 1)

                def probT_high(i, u):
                    act.wait_ge(pt_full, i * (2 * ATT) + 2 * u + 1)
                    if u >= 2:
                        act.wait_ge(pv_done, i * ATT + u - 1)
                    act.copy(probT[0][u % 2][:, 0:4, :], t_ps[0][:, :].rearrange("p (a b) -> p a b", b=P))\
                       .then_inc(pt_hi, 1)
                    act.wait_ge(pt_full, i * (2 * ATT) + 2 * u + 2)
                    if KEY_ROWS[u // 2] == 9:
                        act.copy(probT[0][u % 2][0:GW, 4, :], t_ps[1][0:GW, 0:P])
                    act.copy(probT[0][u % 2][:, 5:7, :], t_ps[1][:, P:3 * P].rearrange("p (a b) -> p a b", b=P))\
                       .then_inc(pt_hi, 1)

                def y_evac(i, j):
                    act.wait_ge(yt_full, i * 2 + (j + 1))
                    if not (isinstance(i, int) and i == 0 and j == 0):
                        act.wait_ge(yt_out, i * 32 + j * 16)
                    act.copy(yT[:, :], o_ps[1][:, :]).then_inc(yt_ready, 1)

                def branch_gate(i, first, j):
                    if j or not first:
                        act.wait_ge(stage_out, i * 64 + j * 16)
                    f_evac(i, 17 + j, stage[:, :], ACT.Sigmoid)

                act.dma_start(bias_d.rearrange("p h e c -> (h e) p c"),
                              bass.AP(tensor=rpb.tensor, offset=GW - 1,
                                      ap=[[P, 2 * PAIRS * 16], [-1, GW], [1, GW]])).then_inc(bias_set, 16)
                act.wait_ge(set_done, 3)
                split_hi(XR, 0)

                def turn(i, first, last):
                    if not first:
                        act.wait_ge(qk_done, i * ATT)
                    for u in (Q0, Q1, Q2):
                        split_hi(u, i)
                    f_evac(i, 0, pad[:, 2:2 + C], ACT.Copy)
                    if not first:
                        y_evac(i - 1, 1)
                    f_evac(i, 1, pad[:, 261:261 + HALF], ACT.Copy)
                    f_evac(i, 2, pad[:, 261 + HALF:261 + T], ACT.Copy)
                    for t in range(Q_TILES):
                        q_evac(i, t)
                        if t in GATES_AFTER:
                            gate_pieces(i, *GATES_AFTER[t])
                        if t == 3:
                            decays(i, 0)
                        if t == 4:
                            root(i, 0)
                        if t == 5:
                            split_hi(G, i)
                        if t == 6:
                            split_hi(MR, i)
                    act.wait_ge(sq_used, i * Q_TILES + Q_TILES)
                    act.activation(rstd[:, 0, :, :], ssq[:, :, :], ACT.Sqrt, bias=eps[:, :], scale=1.0 / HD)\
                       .then_inc(rms_root, 1)
                    decays(i, 1)
                    root(i, 1)
                    f_evac(i, 15, gel[:, 0:HALF], ACT.Gelu_apprx_tanh)
                    f_evac(i, 16, gel[:, HALF:T], ACT.Gelu_apprx_tanh)
                    split_hi(MN, i)
                    branch_gate(i, first, 0)
                    branch_gate(i, first, 1)
                    tr_high(i, range(0, 3))
                    v_high(i)
                    if not last:
                        split_hi(XR, i + 1)
                    branch_gate(i, first, 2)
                    tr_high(i, range(3, 7))
                    branch_gate(i, first, 3)
                    soft(i, 0)
                    soft(i, 1)
                    for u in range(ATT):
                        probT_high(i, u)
                        if u + 2 < ATT:
                            soft(i, u + 2)
                        if u == 9:
                            y_evac(i, 0)

                turn(0, True, False)
                with act.Fori(1, PAIRS - 1) as i:
                    turn(i, False, False)
                turn(PAIRS - 1, False, True)
                y_evac(PAIRS - 1, 1)

            @block.vector
            def _(dve):
                def split_lo(u, i):
                    raw_wait(dve, u, i)
                    dve.wait_ge(w_hi, i * UNITS + u + 1)
                    hi, lo = hi_parts(u)
                    dve.tensor_tensor(lo, raw[:, RAW_SLOT[u], :], hi.bitcast(F32), ALU.subtract).then_inc(w_lo, 1)

                steps = [0]

                def then(ins):
                    steps[0] += 1
                    ins.then_inc(dve_step, 1)
                    dve.wait_ge(dve_step, base[0] + steps[0])

                base = [0]

                def conv(i, first):
                    if not first:
                        dve.wait_ge(decayed, i * 4)
                    dve.tensor_scalar(lp[:, 0:11], lrup[:, :, bass.ds(i, 1)].rearrange("p a b -> p (a b)"),
                                      1.0, None, ALU.mult)
                    then(dve.tensor_scalar(lp[:, 11:15], decay[:, :, :, bass.ds(i, 1)].rearrange("p a b c -> p (a b c)"),
                                           1.0, None, ALU.mult))
                    dve.wait_ge(f_free, i * F_USES + 3)
                    dve.wait_ge(zeroed, i * 3 + 3)
                    for o, p0, n in ((0, 0, C), (C, 259, T)):
                        then(dve.tensor_scalar(xc[:, o:o + n], pad[:, p0:p0 + n], lp[:, 0:1],
                                               lp[:, 4:5], ALU.mult, ALU.add))
                        for k in range(1, 4):
                            last = dve.scalar_tensor_tensor(xc[:, o:o + n], pad[:, p0 + k:p0 + k + n],
                                                            lp[:, k:k + 1], xc[:, o:o + n],
                                                            ALU.mult, ALU.add)
                            if k < 3:
                                then(last)
                    last.then_inc(conv_done, 1)

                def head_squares(i, t):
                    g0 = 0 if t < NT else 2
                    dve.wait_ge(q_free, i * Q_TILES + t + 1)
                    dve.tensor_reduce(ssq[:, t, g0:4], sqs[:, t % 2, HD * g0:256].rearrange("p (g f) -> p g f", f=HD),
                                      AX_X, ALU.add).then_inc(sq_used, 1)

                def gated_input(i, d):
                    dve.wait_ge(f_free, i * F_USES + 9 + 6 * d)
                    then(dve.tensor_tensor(gI[:, :], gI[:, :], xc[:, :], ALU.mult))

                def complement(i, d):
                    dve.wait_ge(decayed, 4 * i + 2 * d + 2)
                    dve.scalar_tensor_tensor(gD[:, :], gD[:, :], 1.0, gR[:, :], ALU.add, ALU.mult)\
                       .then_inc(one_minus, 1)

                def scan(i, d):
                    dve.wait_ge(rooted, 2 * i + d + 1)
                    then(dve.tensor_tensor(gI[:, :], gI[:, :], gD[:, :], ALU.mult))
                    if d == 0:
                        dve.tensor_tensor_scan(h0[:, :], gA[:, :], gI[:, :], 0.0, ALU.mult, ALU.add)\
                           .then_inc(gates_free, 1)
                    else:
                        then(dve.tensor_tensor_scan(gI[:, C - 1::-1], gA[:, C - 1::-1], gI[:, C - 1::-1], 0.0,
                                                    ALU.mult, ALU.add))
                        then(dve.tensor_tensor_scan(gI[:, N - 1:C - 1:-1], gA[:, N - 1:C - 1:-1],
                                                    gI[:, N - 1:C - 1:-1], gI[:, 0:1], ALU.mult, ALU.add))
                        last = dve.tensor_tensor(h0[:, C:N], h0[:, C:N], gI[:, C:N], ALU.add)
                        then(last)

                def rnn_out(i):
                    dve.wait_ge(f_free, i * F_USES + 17)
                    dve.tensor_tensor(gel[:, :], gel[:, :], h0[:, C:N], ALU.mult).then_inc(yr_ready, 1)

                def head_norm(i, col, tiles, g):
                    x = qkv[:, 0:tiles, P * col:P * col + P].rearrange("p t (h f) -> p t h f", f=HD)
                    then(dve.tensor_tensor(x, x, ssq[:, 0:tiles, 2 * col:2 * col + 2].unsqueeze(3)
                                           .broadcast_to([P, tiles, 2, HD]), ALU.mult))
                    gb = g.unsqueeze(1).unsqueeze(1).broadcast_to([P, tiles, 2, HD])
                    dve.tensor_tensor(x, x, gb, ALU.mult).then_inc(normed, 1)

                def rotate(i, col, out, done):
                    o4 = out.rearrange("p (t h f) -> p t h f", h=2, f=HD)
                    s4 = swp[:, :].rearrange("p (t h f) -> p t h f", h=2, f=HD)
                    x = qkv[:, 0:NT, P * col:P * col + P].rearrange("p t (h f) -> p t h f", f=HD)
                    dve.tensor_tensor(o4, x, cosT.unsqueeze(2).broadcast_to([P, NT, 2, HD]), ALU.mult)
                    for h in range(2):
                        for b in range(2):
                            xs = x[:, :, h, :].rearrange("p t (a b f) -> p t a b f", a=2, b=2)[:, :, :, 1 - b, :]
                            sn = sinT.rearrange("p t (a b f) -> p t a b f", a=2, b=2)[:, :, :, b, :]
                            so = s4[:, :, h, :].rearrange("p t (a b f) -> p t a b f", a=2, b=2)[:, :, :, b, :]
                            last = dve.tensor_tensor(so, xs, sn, ALU.mult)
                    then(last)
                    dve.tensor_tensor(out, out, swp[:, :], ALU.add).then_inc(done, 1)

                def tr_low(i, jobs):
                    for n in jobs:
                        dst, t0, tiles = TR_JOBS[n]
                        cols = slice(P * t0, P * (t0 + tiles))
                        dve.wait_ge(tr_hi, i * len(TR_JOBS) + n + 1)
                        for h, rows in enumerate(HEAD_ROWS):
                            last = dve.tensor_tensor(dst[HEAD_ROWS[1 - h], h, cols],
                                                     tr_banks[n % 4][rows, 0:P * tiles],
                                                     dst[rows, h, cols].bitcast(F32), ALU.subtract)
                        last.then_inc(tr_lo, 1)

                def v_low(i):
                    dve.wait_ge(v_hi, i + 1)
                    dve.tensor_tensor(vS[:, :, :, HD:P], values, vS[:, :, :, 0:HD].bitcast(F32), ALU.subtract)\
                       .then_inc(v_lo, 1)

                def mark(ins):
                    steps[0] += 1
                    ins.then_inc(dve_step, 1)
                    return steps[0]

                def needs(step):
                    dve.wait_ge(dve_step, base[0] + step)

                def raw_maxima(i, u):
                    t, h = u // 2, u % 2
                    a, b = (f_ps if u % 2 == 0 else q_ps)
                    inner = KEY_ROWS[t] == 9
                    e = BIAS_ROW0[t] - 1 + inner
                    p = prob[u % 3]
                    dve.wait_ge(qk_done, i * ATT + u + 1)
                    dve.tensor_reduce(stat[:, u, 0:1], b[:, P:P + C], AX_X, ALU.max)
                    last = dve.tensor_tensor_reduce(
                        out=p[:, inner:8, :], in0=a[:, 0:HALF - GW * inner].rearrange("p (r c) -> p r c", c=GW),
                        in1=bias[:, h, e:e + 8 - inner, :], scale=1.0, scalar=-3.0e38, op0=ALU.add, op1=ALU.max,
                        accum_out=stat[:, u, 1:2])
                    if inner:
                        last = dve.tensor_tensor_reduce(
                            out=p[:, 0:9:8, :], in0=b[:, 0:P].rearrange("p (r c) -> p r c", c=GW),
                            in1=bias[:, h, BIAS_ROWS:, :], scale=1.0, scalar=-3.0e38, op0=ALU.add, op1=ALU.max,
                            accum_out=stat[:, u, 2:3])
                    return mark(last)

                def probT_low(i, u, bank):
                    inner = KEY_ROWS[u // 2] == 9
                    hi, lo = probT[0][u % 2], probT[1][u % 2]
                    dve.wait_ge(pt_hi, i * (2 * ATT) + (2 * u + bank + 1))
                    if bank == 0:
                        dve.tensor_tensor(lo[:, 0:4, :], t_ps[0][:, :].rearrange("p (a b) -> p a b", b=P),
                                          hi[:, 0:4, :].bitcast(F32), ALU.subtract).then_inc(pt_lo, 1)
                    else:
                        if inner:
                            dve.tensor_tensor(lo[0:GW, 4, :], t_ps[1][0:GW, 0:P], hi[0:GW, 4, :].bitcast(F32),
                                              ALU.subtract)
                        dve.tensor_tensor(lo[:, 5:7, :], t_ps[1][:, P:3 * P].rearrange("p (a b) -> p a b", b=P),
                                          hi[:, 5:7, :].bitcast(F32), ALU.subtract).then_inc(pt_lo, 1)

                def attention_step(i, low, bound, out):
                    if bound is not None:
                        maxima = raw_maxima(i, bound)
                    if out is not None:
                        dve.wait_ge(exp_done, i * ATT + out + 1)
                        total = mark(dve.tensor_tensor(ysc[:, out, 0:1], stat[:, out, 5:6], stat[:, out, 6:7], ALU.add))
                    if bound is not None:
                        needs(maxima)
                        inner = KEY_ROWS[bound // 2] == 9
                        top = mark(dve.tensor_reduce(stat[:, bound, 3:4], stat[:, bound, 0:2 + inner], AX_X, ALU.max))
                    if out is not None:
                        needs(total)
                        inverse = mark(dve.reciprocal(ysc[:, out, 1:2], ysc[:, out, 0:1]))
                    if bound is not None:
                        needs(top)
                        dve.tensor_scalar(stat[:, bound, 4:5], stat[:, bound, 3:4], -1.0, None, ALU.mult)\
                           .then_inc(bound_done, 1)
                    if low is not None:
                        probT_low(i, low, 0)
                        probT_low(i, low, 1)
                    if out is not None:
                        t, h = out // 2, out % 2
                        needs(inverse)
                        dve.wait_ge(pv_done, i * ATT + out + 1)
                        half = mark(dve.tensor_scalar(ytmp[:, out % 2, :], o_ps[out % 2][:, 0:HD], ysc[:, out, 1:2],
                                                      None, ALU.mult))
                        if out == 8:
                            dve.wait_ge(yt_full, i * 2 + 1)
                        if out == 0 and not (isinstance(i, int) and i == 0):
                            dve.wait_ge(yt_full, i * 2)
                        needs(half)
                        dve.scalar_tensor_tensor(ytok[:, t % 4, HD * h:HD * h + HD], o_ps[out % 2][:, HD:P],
                                                 ysc[:, out, 1:2], ytmp[:, out % 2, :], ALU.mult, ALU.add)\
                           .then_inc(y_done, 1)

                dve.wait_ge(const_in, 32)
                then(dve.tensor_scalar(gqk[:, 0, :], gqk[:, 0, :], HD ** -0.5, None, ALU.mult))
                split_lo(XR, 0)

                def turn(i, first, last):
                    base[0] = 1 + i * STEPS
                    steps[0] = 0
                    for u in (Q0, Q1, Q2):
                        split_lo(u, i)
                    conv(i, first)
                    for t in range(Q_TILES):
                        head_squares(i, t)
                        if t == 3:
                            gated_input(i, 0)
                            complement(i, 0)
                        if t == 4:
                            scan(i, 0)
                        if t == 5:
                            split_lo(G, i)
                        if t == 6:
                            split_lo(MR, i)
                    gated_input(i, 1)
                    dve.wait_ge(rms_root, i + 1)
                    rt, v = rstd[:, 0, :, :], ssq[:, :, :]
                    then(dve.reciprocal(rt, rt))
                    dve.tensor_scalar(v, v, -0.5 / HD, -0.5 * EPS, ALU.mult, ALU.add)
                    then(dve.tensor_tensor(rstd[:, 1, :, :], rt, rt, ALU.mult))
                    then(dve.tensor_tensor(v, v, rstd[:, 1, :, :], ALU.mult))
                    then(dve.scalar_tensor_tensor(v, v, 1.5, rt, ALU.add, ALU.mult))
                    head_norm(i, 1, Q_TILES, gqk[:, 1, :])
                    head_norm(i, 0, NT, gqk[:, 0, :])
                    complement(i, 1)
                    scan(i, 1)
                    dve.wait_ge(normed, i * 2 + 1)
                    rotate(i, 1, krot[:, :], rope_k)
                    rnn_out(i)
                    split_lo(MN, i)
                    tr_low(i, range(0, 3))
                    dve.wait_ge(normed, i * 2 + 2)
                    rotate(i, 0, qrot[:, :], rope_q)
                    if not last:
                        split_lo(XR, i + 1)
                    tr_low(i, range(3, 7))
                    v_low(i)
                    dve.wait_ge(bias_done, 3 * i + 3)
                    dve.wait_ge(yr_out, i * 16 + 16)
                    attention_step(i, None, 0, None)
                    attention_step(i, None, 1, None)
                    for u in range(ATT):
                        attention_step(i, u, u + 2 if u + 2 < ATT else None, u - 1 if u >= 1 else None)
                    attention_step(i, None, None, ATT - 1)
                    assert steps[0] == STEPS, steps[0]

                turn(0, True, False)
                with dve.Fori(1, PAIRS - 1) as i:
                    turn(i, False, False)
                turn(PAIRS - 1, False, True)


STEPS = 3 + 1 + 6 + 1 + 1 + 1 + 4 + 1 + 3 + 3 + ATT * 5 - 2


def mod_column(dve, n, b, row, sc, dots, bm, mod, dotted, mod_done, count):
    dve.tensor_tensor_reduce(out=row, in0=row, in1=sc[:, :], scale=1.0, scalar=0.0, op0=ALU.mult, op1=ALU.add,
                             accum_out=dots[:, b:b + 1]).then_inc(dotted, 1)
    dve.wait_ge(dotted, count)
    dve.tensor_tensor(mod[:, bass.ds(n, 1), 0:1].rearrange("p a b -> p (a b)"), dots[:, b:b + 1],
                      bm[:, bass.ds(n, 1)], ALU.add).then_inc(mod_done, 1)


def merge_block(nc, sem, sbuf, psum, xT, w_mix, c_row, w_modT, bm, mod, sc, x1, yr_d, yn_d, smr_d, smn_d):
    with ExitStack() as st:
        raw = sbuf(st, "raw_c", [P, 2, 1024])
        wh = sbuf(st, "wh_c", [P, 2, KC, P], F32R)
        wl = sbuf(st, "wl_c", [P, 2, KC, P], F32R)
        ah = [sbuf(st, f"ah{n}", [P, KC, T], F32R) for n in range(2)]
        al = [sbuf(st, f"al{n}", [P, KC, T], F32R) for n in range(2)]
        aux = sbuf(st, "aux", [P, 2, T])
        ys = sbuf(st, "ys", [P, 2, T])
        rows = sbuf(st, "rows_c", [P, 2, D])
        dots = sbuf(st, "dots_c", [P, 2])
        ps = psum(st, "ps_c", [P, 4, HALF])
        c_in, c_silu = sem("c_c_in"), sem("c_c_silu")
        rows_in = [sem(f"c_rows_in{s}") for s in range(2)]
        dotted, mod_done = sem("c_dotted"), sem("c_mod_done")
        raw_in = [sem(f"c_raw_in{s}") for s in range(2)]
        aux_in = [sem(f"c_aux_in{s}") for s in range(2)]
        ys_in = [sem(f"c_ys_in{s}") for s in range(2)]
        w_hi, w_lo = sem("c_w_hi"), sem("c_w_lo")
        y_hi, y_lo = sem("c_y_hi"), sem("c_y_lo")
        full, free = sem("c_full"), sem("c_free")
        part = sem("c_part")
        merged_hi, merged_lo = sem("c_merged_hi"), sem("c_merged_lo")
        units = 3 * KC
        flat = lambda a, s: a[:, s, :, :].rearrange("p k c -> p (k c)")

        with nc.Block() as block:
            @block.sync
            def _(sp):
                for n in range(2):
                    sp.dma_start(raw[:, n, :], w_mix[n]).then_inc(raw_in[n], 16)
                sp.dma_start(sc[:, :], bass.AP(tensor=c_row.tensor, offset=0, ap=[[0, P], [1, D]])).then_inc(c_in, 16)
                for n in range(2):
                    sp.dma_start(rows[:, n, :], w_modT[n]).then_inc(rows_in[n], 16)
                with sp.Fori(0, units // 2 - 1) as r:
                    for b in range(2):
                        sp.wait_ge(w_lo, r * 2 + b + 1)
                        sp.dma_start(raw[:, b, :], w_mix[bass.ds(r * 2 + b + 2, 1)].rearrange("a p c -> (a p) c"))\
                          .then_inc(raw_in[b], 16)
                        sp.wait_ge(mod_done, r * 2 + b + 1)
                        sp.dma_start(rows[:, b, :], w_modT[bass.ds(r * 2 + b + 2, 1)].rearrange("a p c -> (a p) c"))\
                          .then_inc(rows_in[b], 16)

            @block.gpsimd
            def _(pool):
                for n in range(2 * KC):
                    if n >= 2:
                        pool.wait_ge(y_lo, n - 1)
                    pool.dma_start(ys[:, n % 2, :], (yr_d if n < KC else yn_d)[n % KC]).then_inc(ys_in[n % 2], 16)
                    if n in (8, 9):
                        pool.dma_start(aux[:, n % 2, :], smr_d[n % 2]).then_inc(aux_in[n % 2], 16)
                for n in range(2, units):
                    src = (smr_d, smn_d, xT)[n // KC]
                    pool.wait_ge(free, 2 * n - 2)
                    pool.dma_start(aux[:, n % 2, :], src[n % KC]).then_inc(aux_in[n % 2], 16)

            @block.tensor
            def _(pe):
                for ph in range(3):
                    if ph < 2:
                        pe.wait_ge(y_lo, KC * (ph + 1))
                    else:
                        pe.wait_ge(merged_lo, 2 * KC)
                    s = ph % 2

                    def block_pair(r):
                        for b in range(2):
                            n = r * 2 + (KC * ph + b)
                            pe.wait_ge(w_lo, n + 1)
                            for half in range(2):
                                if not (isinstance(n, int) and n < 2):
                                    pe.wait_ge(free, n * 2 + half - 3)
                                cols = slice(HALF * half, HALF * half + HALF)
                                three_passes(pe, ps[:, 2 * b + half, :], lambda k: wh[:, b, k, :],
                                             lambda k: wl[:, b, k, :], lambda k: ah[s][:, k, cols],
                                             lambda k: al[s][:, k, cols], KC).then_inc(full, 1)

                    block_pair(0)
                    with pe.Fori(1, KC // 2) as r:
                        block_pair(r)

            @block.scalar
            def _(act):
                def w_split(n, b):
                    act.wait_ge(raw_in[b], (n // 2) * 16 + 16 if isinstance(n, int) else (n - b) * 8 + 16)
                    act.copy(flat(wh, b), raw[:, b, :]).then_inc(w_hi, 1)

                def y_split(n):
                    act.wait_ge(ys_in[n % 2], (n // 2) * 16 + 16)
                    act.copy(ah[n // KC][:, n % KC, :], ys[:, n % 2, :]).then_inc(y_hi, 1)

                w_split(0, 0)
                for n in range(KC):
                    y_split(n)
                w_split(1, 1)
                act.wait_ge(c_in, 16)
                act.activation(sc[:, :], sc[:, :], ACT.Silu).then_inc(c_silu, 1)
                for n in range(KC, 2 * KC):
                    y_split(n)
                with act.Fori(0, units // 2 - 1) as r:
                    for b in range(2):
                        act.wait_ge(full, r * 4 + (2 * b + 2))
                        w_split(r * 2 + (b + 2), b)

            @block.vector
            def _(dve):
                def w_split(n, b):
                    dve.wait_ge(w_hi, n + 1)
                    dve.wait_ge(raw_in[b], (n // 2) * 16 + 16 if isinstance(n, int) else (n - b) * 8 + 16)
                    dve.tensor_tensor(flat(wl, b), raw[:, b, :], flat(wh, b).bitcast(F32), ALU.subtract)\
                       .then_inc(w_lo, 1)

                def y_split(n):
                    dve.wait_ge(y_hi, n + 1)
                    dve.wait_ge(ys_in[n % 2], (n // 2) * 16 + 16)
                    dve.tensor_tensor(al[n // KC][:, n % KC, :], ys[:, n % 2, :],
                                      ah[n // KC][:, n % KC, :].bitcast(F32), ALU.subtract).then_inc(y_lo, 1)

                w_split(0, 0)
                for n in range(KC):
                    y_split(n)
                w_split(1, 1)
                for n in range(KC, 2 * KC):
                    y_split(n)
                dve.wait_ge(c_silu, 1)
                for ph in range(3):
                    if ph == 2:
                        dve.wait_ge(mod_done, KC)

                    def step(n, m, b, more):
                        dve.wait_ge(rows_in[b], (n - b) * 8 + 16)
                        dve.wait_ge(aux_in[b], (n - b) * 8 + 16)
                        for half in range(2):
                            cols = slice(HALF * half, HALF * half + HALF)
                            out = x1[:, bass.ds(m, 1), cols].rearrange("p a c -> p (a c)")
                            dve.wait_ge(full, n * 2 + half + 1)
                            if ph == 0:
                                dve.tensor_tensor(out, ps[:, 2 * b + half, :], aux[:, b, cols], ALU.mult)\
                                   .then_inc(free, 1)
                            elif ph == 1:
                                dve.tensor_tensor(aux[:, b, cols], ps[:, 2 * b + half, :], aux[:, b, cols],
                                                  ALU.mult).then_inc(part, 1)
                                dve.wait_ge(part, m * 2 + half + 1)
                                dve.tensor_tensor(out, out, aux[:, b, cols], ALU.add)\
                                   .then_inc(free, 1)
                                dve.wait_ge(free, n * 2 + half + 1)
                            else:
                                dve.scalar_tensor_tensor(out, ps[:, 2 * b + half, :],
                                                         mod[:, bass.ds(m + 2 * KC, 1), 0:1].rearrange("p a b -> p (a b)"),
                                                         aux[:, b, cols], ALU.mult, ALU.add).then_inc(free, 1)
                            if half == 0:
                                mod_column(dve, n + 2 * KC, b, rows[:, b, :], sc, dots, bm, mod,
                                           dotted, mod_done, n + 1)
                        if more:
                            w_split(n + 2, b)
                        if ph == 1:
                            for half in range(2):
                                cols = slice(HALF * half, HALF * half + HALF)
                                out = x1[:, bass.ds(m, 1), cols]
                                dve.tensor_scalar(ah[0][:, bass.ds(m, 1), cols], out, 1.0, None, ALU.mult)\
                                   .then_inc(merged_hi, 1)
                                dve.wait_ge(merged_hi, m * 2 + half + 1)
                                dve.tensor_tensor(al[0][:, bass.ds(m, 1), cols], out,
                                                  ah[0][:, bass.ds(m, 1), cols].bitcast(F32), ALU.subtract)\
                                   .then_inc(merged_lo, 1)

                    turns = KC // 2 - (ph == 2)
                    with dve.Fori(0, turns) as r:
                        for b in range(2):
                            step(r * 2 + (KC * ph + b), r * 2 + b, b, True)
                    if ph == 2:
                        for b in range(2):
                            step(units - 2 + b, KC - 2 + b, b, False)


def ffn_block(nc, sem, sbuf, psum, w_ff, ffn_p, w_modT, bm, mod, sc, gain, ones, eps, x1, outT):
    with ExitStack() as st:
        xh = sbuf(st, "xh_d", [P, KC, T], F32R)
        xl = sbuf(st, "xl_d", [P, KC, T], F32R)
        hh = sbuf(st, "hh_d", [P, max(GROUPS), T], F32R)
        hl = sbuf(st, "hl_d", [P, max(GROUPS), T], F32R)
        raw = sbuf(st, "raw_d", [P, 2, 1024])
        wh = sbuf(st, "wh_d", [P, 2, KC, P], F32R)
        wl = sbuf(st, "wl_d", [P, 2, KC, P], F32R)
        ca = sbuf(st, "ca", [P, T])
        cg = sbuf(st, "cg", [P, T])
        fp = sbuf(st, "fp", [P, FC, 8])
        gm = sbuf(st, "gm_d", [P, KC])
        fps = sbuf(st, "fps", [P, 8])
        rows = sbuf(st, "rows_d", [P, D])
        dots = sbuf(st, "dots_d", [P, 1])
        rows_in, dotted, mod_done = sem("d_rows_in"), sem("d_dotted"), sem("d_mod_done")
        pa = psum(st, "pa", [P, T])
        pg = psum(st, "pg", [P, T])
        pd = psum(st, "pd", [P, 4, HALF])
        fp_in = sem("d_fp_in")
        raw_in = [sem(f"d_raw_in{s}") for s in range(2)]
        squared, sq_used, root, rstd_done = sem("d_squared"), sem("d_sq_used"), sem("d_root"), sem("d_rstd")
        gm_done, scaled, hi_done, lo_done = sem("d_gm"), sem("d_scaled"), sem("d_hi"), sem("d_lo")
        w_hi, w_lo, used = sem("d_w_hi"), sem("d_w_lo"), sem("d_used")
        centre = sem("d_centre")
        conv_step, conved = sem("d_conv_step"), sem("d_conved")
        silu_done, gated, h_hi, h_lo = sem("d_silu"), sem("d_gated"), sem("d_h_hi"), sem("d_h_lo")
        taps_in = sem("d_taps_in")
        full, free = sem("d_full"), sem("d_free")
        stored = sem("d_stored")
        flat = lambda a, s: a[:, s, :, :].rearrange("p k c -> p (k c)")
        starts = []
        n = 0
        for g, pairs in enumerate(GROUPS):
            starts.append((n, sum(GROUPS[:g]), n + 2 * pairs))
            n += 2 * pairs + KC

        with nc.Block() as block:
            @block.sync
            def _(sp):
                sp.dma_start(fp[:, :, :], ffn_p).then_inc(fp_in, 16)
                for n in range(2):
                    sp.dma_start(raw[:, n, :], w_ff[n]).then_inc(raw_in[n], 16)
                sp.dma_start(rows[:, :], w_modT[3 * KC]).then_inc(rows_in, 16)

                def load_pair(r):
                    for b in range(2):
                        sp.wait_ge(w_lo, r * 2 + b + 1)
                        sp.dma_start(raw[:, b, :], w_ff[bass.ds(r * 2 + b + 2, 1)].rearrange("a p c -> (a p) c"))\
                          .then_inc(raw_in[b], 16)

                with sp.Fori(0, GROUPS[0] - 1) as r:
                    load_pair(r)
                    sp.wait_ge(mod_done, r + 1)
                    sp.dma_start(rows[:, :], w_modT[bass.ds(r + (3 * KC + 1), 1)].rearrange("a p c -> (a p) c"))\
                      .then_inc(rows_in, 16)
                with sp.Fori(GROUPS[0] - 1, FF_UNITS // 2 - 1) as r:
                    load_pair(r)
                with sp.Fori(0, KC) as m:
                    sp.wait_ge(free, m * 2 + (2 * KC * (len(GROUPS) - 1) + 2))
                    sp.dma_start(outT[bass.ds(m, 1)].rearrange("a p t -> (a p) t"),
                                 x1[:, bass.ds(m, 1), :].rearrange("p a t -> p (a t)")).then_inc(stored, 16)
                sp.wait_ge(stored, 16 * KC)

            @block.tensor
            def _(pe):
                for k in range(KC):
                    pe.wait_ge(squared, k + 1)
                    for half in range(2):
                        last = pe.matmul(pd[:, half, :], ones[:, :], (ca if k % 2 == 0 else cg)[:, HALF * half:HALF * half + HALF],
                                         start=(k == 0), stop=(k == KC - 1))
                    last.then_inc(sq_used, 1)
                pe.wait_ge(lo_done, KC)
                for g, pairs in enumerate(GROUPS):
                    u0, j0, d0 = starts[g]
                    def up_pair(j):
                        for b, bank in enumerate((pa, pg)):
                            pe.wait_ge(w_lo, j * 2 + (u0 + b + 1))
                            if not (isinstance(j, int) and j0 == 0):
                                pe.wait_ge(conved, j * 2 + (2 * j0 + b - 1))
                            for half in range(2):
                                cols = slice(HALF * half, HALF * half + HALF)
                                last = three_passes(pe, bank[:, cols], lambda k: wh[:, b, k, :],
                                                    lambda k: wl[:, b, k, :], lambda k: xh[:, k, cols],
                                                    lambda k: xl[:, k, cols], KC)
                            last.then_inc(used, 1)

                    up_pair(0)
                    with pe.Fori(1, pairs) as j:
                        up_pair(j)
                    pe.wait_ge(h_lo, j0 + pairs)

                    def down_pair(r):
                        for b in range(2):
                            pe.wait_ge(w_lo, r * 2 + (d0 + b + 1))
                            for half in range(2):
                                cols = slice(HALF * half, HALF * half + HALF)
                                if not (isinstance(r, int) and g == 0):
                                    pe.wait_ge(free, r * 4 + (2 * KC * g + 2 * b + half - 3))
                                three_passes(pe, pd[:, 2 * b + half, :], lambda k: wh[:, b, k, :],
                                                    lambda k: wl[:, b, k, :], lambda k: hh[:, k, cols],
                                                    lambda k: hl[:, k, cols], pairs).then_inc(full, 1)

                    down_pair(0)
                    with pe.Fori(1, KC // 2) as r:
                        down_pair(r)

            @block.scalar
            def _(act):
                def w_split(n, b):
                    act.wait_ge(raw_in[b], (n // 2) * 16 + 16 if isinstance(n, int) else (n - b) * 8 + 16)
                    act.copy(flat(wh, b), raw[:, b, :]).then_inc(w_hi, 1)

                w_split(0, 0)
                w_split(1, 1)
                for k in range(KC):
                    if k >= 2:
                        act.wait_ge(sq_used, k - 1)
                    act.activation((ca if k % 2 == 0 else cg)[:, :], x1[:, k, :], ACT.Square).then_inc(squared, 1)
                act.wait_ge(sq_used, KC)
                act.activation(ca[:, :], pd[:, 0:2, :].rearrange("p a b -> p (a b)"), ACT.Sqrt,
                               bias=eps[:, :], scale=1.0 / D).then_inc(root, 1)
                for k in range(KC):
                    act.wait_ge(scaled, k + 1)
                    act.activation(xh[:, k, :], (pa if k % 2 == 0 else pg)[:, :], ACT.Identity,
                                   bias=mod[:, 3 * KC + k, 0:1]).then_inc(hi_done, 1)
                act.wait_ge(fp_in, 16)
                for g, pairs in enumerate(GROUPS):
                    u0, j0, d0 = starts[g]
                    def up_pair(j):
                        for b, (bank, out) in enumerate(((pa, ca), (pg, cg))):
                            act.wait_ge(used, j * 2 + (2 * j0 + b + 1))
                            if b == 0 and not (isinstance(j, int) and j0 == 0):
                                act.wait_ge(h_lo, j + j0)
                            if b == 0:
                                act.wait_ge(taps_in, j + (j0 + 1))
                            act.activation(out[:, :], bank[:, :], ACT.Identity, bias=fps[:, 4 * b + 3:4 * b + 4],
                                           scale=fps[:, 4 * b + 1:4 * b + 2]).then_inc(centre, 1)
                            w_split(j * 2 + (u0 + b + 2), b)
                        act.wait_ge(conved, j * 2 + (2 * j0 + 1))
                        act.activation(ca[:, :], ca[:, :], ACT.Silu).then_inc(silu_done, 1)

                    up_pair(0)
                    with act.Fori(1, pairs) as j:
                        up_pair(j)
                    turns = KC // 2 - (g == len(GROUPS) - 1)
                    with act.Fori(0, turns) as r:
                        for b in range(2):
                            act.wait_ge(full, r * 4 + (2 * KC * g + 2 * b + 2))
                            w_split(r * 2 + (d0 + b + 2), b)

            @block.vector
            def _(dve):
                def w_split(n, b):
                    dve.wait_ge(w_hi, n + 1)
                    dve.wait_ge(raw_in[b], (n // 2) * 16 + 16 if isinstance(n, int) else (n - b) * 8 + 16)
                    dve.tensor_tensor(flat(wl, b), raw[:, b, :], flat(wh, b).bitcast(F32), ALU.subtract)\
                       .then_inc(w_lo, 1)

                w_split(0, 0)
                w_split(1, 1)
                dve.scalar_tensor_tensor(gm[:, :], mod[:, 4 * KC:5 * KC, 0], 1.0, gain[:, 1, :], ALU.add, ALU.mult)\
                   .then_inc(gm_done, 1)
                dve.wait_ge(gm_done, 1)
                dve.wait_ge(root, 1)
                dve.reciprocal(cg[:, :], ca[:, :]).then_inc(rstd_done, 1)
                dve.wait_ge(rstd_done, 1)
                dve.tensor_scalar(ca[:, :], pd[:, 0:2, :].rearrange("p a b -> p (a b)"), -0.5 / D, -0.5 * EPS,
                                  ALU.mult, ALU.add).then_inc(rstd_done, 1)
                dve.wait_ge(rstd_done, 2)
                for n in range(2):
                    dve.tensor_tensor(ca[:, :], ca[:, :], cg[:, :], ALU.mult).then_inc(rstd_done, 1)
                    dve.wait_ge(rstd_done, 3 + n)
                dve.scalar_tensor_tensor(cg[:, :], ca[:, :], 1.5, cg[:, :], ALU.add, ALU.mult).then_inc(rstd_done, 1)
                dve.wait_ge(rstd_done, 5)
                for k in range(KC + 1):
                    if k < KC:
                        if k >= 2:
                            dve.wait_ge(lo_done, k - 1)
                        dve.scalar_tensor_tensor((pa if k % 2 == 0 else pg)[:, :], x1[:, k, :], gm[:, k:k + 1],
                                                 cg[:, :], ALU.mult, ALU.mult).then_inc(scaled, 1)
                    if k >= 1:
                        j = k - 1
                        dve.wait_ge(hi_done, k)
                        dve.scalar_tensor_tensor(xl[:, j, :], (pa if j % 2 == 0 else pg)[:, :],
                                                 mod[:, 3 * KC + j, 0:1], xh[:, j, :].bitcast(F32),
                                                 ALU.add, ALU.subtract).then_inc(lo_done, 1)
                dve.wait_ge(fp_in, 16)
                for g, pairs in enumerate(GROUPS):
                    u0, j0, d0 = starts[g]
                    def up_pair(j):
                        if not (isinstance(j, int) and j0 == 0):
                            dve.wait_ge(centre, j * 2 + 2 * j0)
                        dve.tensor_scalar(fps[:, :], fp[:, bass.ds(j + j0, 1), :].rearrange("p a b -> p (a b)"),
                                          1.0, None, ALU.mult).then_inc(taps_in, 1)
                        dve.wait_ge(taps_in, j + (j0 + 1))
                        for b, (bank, out) in enumerate(((pa, ca), (pg, cg))):
                            tap = lambda k: fps[:, 4 * b + k:4 * b + k + 1]
                            dve.wait_ge(centre, j * 2 + (2 * j0 + b + 1))
                            dve.scalar_tensor_tensor(out[:, 1:T], bank[:, 0:T - 1], tap(0), out[:, 1:T],
                                                     ALU.mult, ALU.add).then_inc(conv_step, 1)
                            dve.wait_ge(conv_step, j * 2 + (2 * j0 + b + 1))
                            dve.scalar_tensor_tensor(out[:, 0:T - 1], bank[:, 1:T], tap(2), out[:, 0:T - 1],
                                                     ALU.mult, ALU.add).then_inc(conved, 1)
                            if g == 0 and b == 0:
                                dve.wait_ge(rows_in, j * 16 + 16)
                            w_split(j * 2 + (u0 + b + 2), b)
                            if g == 0 and b == 0:
                                mod_column(dve, j + 5 * KC, 0, rows[:, :], sc, dots, bm, mod, dotted, mod_done, j + 1)
                        dve.wait_ge(conved, j * 2 + (2 * j0 + 2))
                        dve.wait_ge(silu_done, j + (j0 + 1))
                        dve.tensor_tensor(ca[:, :], ca[:, :], cg[:, :], ALU.mult).then_inc(gated, 1)
                        dve.wait_ge(gated, j + (j0 + 1))
                        dve.tensor_scalar(hh[:, bass.ds(j, 1), :].rearrange("p a t -> p (a t)"), ca[:, :],
                                          1.0, None, ALU.mult).then_inc(h_hi, 1)
                        dve.wait_ge(h_hi, j + (j0 + 1))
                        dve.tensor_tensor(hl[:, bass.ds(j, 1), :].rearrange("p a t -> p (a t)"), ca[:, :],
                                          hh[:, bass.ds(j, 1), :].rearrange("p a t -> p (a t)").bitcast(F32),
                                          ALU.subtract).then_inc(h_lo, 1)

                    up_pair(0)
                    with dve.Fori(1, pairs) as j:
                        up_pair(j)
                    if g == 0:
                        dve.wait_ge(mod_done, KC)

                    def down(n, m, b, more):
                        for half in range(2):
                            cols = slice(HALF * half, HALF * half + HALF)
                            out = x1[:, bass.ds(m, 1), cols].rearrange("p a c -> p (a c)")
                            dve.wait_ge(full, m * 2 + (2 * KC * g + half + 1))
                            dve.scalar_tensor_tensor(out, pd[:, 2 * b + half, :],
                                                     mod[:, bass.ds(m + 5 * KC, 1), 0:1].rearrange("p a b -> p (a b)"),
                                                     out, ALU.mult, ALU.add).then_inc(free, 1)
                        if more:
                            w_split(n + 2, b)

                    last_group = g == len(GROUPS) - 1
                    with dve.Fori(0, KC // 2 - last_group) as r:
                        for b in range(2):
                            down(r * 2 + (d0 + b), r * 2 + b, b, True)
                    if last_group:
                        for b in range(2):
                            down(d0 + KC - 2 + b, KC - 2 + b, b, False)


def constants():
    col = np.arange(GW)
    start = np.clip(col - 8, 0, GW - 16)
    inside = (col[None, :] >= start[:, None]) & (col[None, :] < start[:, None] + 16)
    mask = np.where(inside, 0.0, NEG).astype(np.float32)
    mask = np.concatenate([mask, mask], 0)
    lower = np.where(np.arange(P) >= GW, NEG, 0.0).astype(np.float32)[:, None]
    edges = np.concatenate([mask + lower, mask + (np.float32(NEG) - lower)], 1)
    n = HD // 4
    freq = (np.float32(10000.0) ** (-np.arange(n, dtype=np.float32) / np.float32(n))).astype(np.float32)
    tok = np.arange(T)
    cos = np.zeros((T, 2, 2, n), np.float32)
    sin = np.zeros((T, 2, 2, n), np.float32)
    for a, pos in enumerate((tok // GW, tok % GW)):
        ang = (pos.astype(np.float32)[:, None] * freq).astype(np.float32)
        for b in range(2):
            cos[:, a, b] = np.cos(ang)
            sin[:, a, b] = np.sin(ang) * (1 if b else -1)
    tiles = lambda a: a.reshape(NT, P, HD).transpose(1, 0, 2).reshape(P, NT * HD)
    table = np.concatenate([np.eye(P, dtype=np.float32), mask, edges, tiles(cos), tiles(sin)], 1)
    return np.ascontiguousarray(table, np.float32)


def kernel(**inputs):
    import concourse.bacc as bacc
    from concourse.bass_utils import run_bass_kernel_spmd

    a = {k: np.asarray(v) for k, v in inputs.items()}
    chunks = lambda m: m.reshape(KC, P, -1)
    cols = lambda v: v.reshape(-1, P).T
    blocks = lambda w: w.reshape(w.shape[0] // P, P, w.shape[1] // P, P).transpose(2, 1, 0, 3)
    w_in = a["w_in"][0].reshape(KC, P, 7, KC, P)
    fm = w_in[:, :, [0, 3, 5, 6]].transpose(3, 2, 1, 0, 4).reshape(4 * KC, P, D)
    qkv = w_in[:, :, [4, 1, 2]].transpose(3, 1, 0, 2, 4).reshape(KC, P, 3 * D)
    lru_w = np.stack([a["lru_wa"][0], a["lru_wx"][0]]).reshape(4, KC, P, P).transpose(1, 2, 0, 3)
    lru_p = np.concatenate([a["lru_conv_w"][0], a["lru_conv_b"], a["lru_ba"][0], a["lru_bx"][0],
                            a["lru_lambda"][0]]).reshape(11, KC, P).transpose(2, 0, 1)
    rpb = np.zeros((16 * 16 + 1, P), np.float32)
    rpb[:-1].reshape(16, 16, P)[:, 1:, 48:79] = a["na_rpb"][0]
    up = blocks(a["w_up"][0]).reshape(2, FC, P, D)
    down = blocks(a["w_down"][0])
    units, j = [], 0
    for n in GROUPS:
        units.append(up[:, j:j + n].transpose(1, 0, 2, 3).reshape(2 * n, P, D))
        d = np.zeros((KC, P, KC, P), np.float32)
        d[:, :, 0:n] = down[:, :, j:j + n]
        units.append(d.reshape(KC, P, D))
        j += n
    conv = np.concatenate([a["ffn_conv_w"][0], a["ffn_conv_b"]]).reshape(4, 2, FC, P).transpose(3, 2, 1, 0)
    arrays = {
        "xT": chunks(a["x"][0].T), "ctxT": chunks(a["ctx"][0].T),
        "svec": np.stack([cols(a["c"][0]), cols(a["c_ctx"])], 2),
        "c_row": a["c"], "w_mod": blocks(a["w_mod"][0])[0:2 * KC],
        "w_modT": a["w_mod"][0][:, 2 * D:].T.reshape(4 * KC, P, D), "b_mod": cols(a["b_mod"][0]),
        "gains": np.stack([cols(a["norm_mix_g"][0]), cols(a["norm_ffn_g"][0])], 1),
        "w_fm": fm, "w_qkv": qkv, "lru_w": lru_w.reshape(KC, P, 4 * P), "lru_p": lru_p,
        "qk_g": np.stack([a["q_norm_g"][0], a["k_norm_g"][0]]), "rpb": rpb,
        "w_mix": np.concatenate([blocks(a[n][0]).reshape(KC, P, D) for n in ("w_rnn_out", "w_na_out", "w_out")]),
        "w_ff": np.concatenate(units), "ffn_p": conv.reshape(P, FC, 8), "consts": constants(),
    }
    arrays = {k: np.ascontiguousarray(v) for k, v in arrays.items()}
    nc = bacc.Bacc("TRN2", target_bir_lowering=False, num_devices=1, dynamic_dma_scratch_size=4096)
    aps = {k: nc.dram_tensor(k, v.shape, mybir.dt.from_np(v.dtype), kind="ExternalInput").ap()
           for k, v in arrays.items()}
    aps["outT"] = nc.dram_tensor("outT", (KC, P, T), F32, kind="ExternalOutput").ap()
    for k in ("yr_d", "yn_d", "smr_d", "smn_d"):
        aps[k] = nc.dram_tensor(k, (KC, P, T), F32, kind="Internal").ap()
    aps["bias_d"] = nc.dram_tensor("bias_d", (GW, 2 * PAIRS, 16, GW), F32, kind="Internal").ap()
    build(nc, **aps)
    r = run_bass_kernel_spmd(nc, [arrays], core_ids=[0])
    out = np.asarray(r.results[0]["outT"])
    return np.ascontiguousarray(out.reshape(D, T).T)[None]
```

```python
from contextlib import ExitStack

import numpy as np

import concourse.bass as bass
from concourse import mybir

F32 = mybir.dt.float32
F32R = mybir.dt.float32r
ALU = mybir.AluOpType
ACT = mybir.ActivationFunctionType
AX_X = mybir.AxisListType.X

P = 128
D = 1024
KC = D // P
T = 1024
C = 256
N = C + T
GW = 64
HD = 64
PAIRS = KC
NT = T // P
NCT = C // P
WIN = 8
FF = 2816
FC = FF // P
GROUPS = (8, 7, 7)
UP_UNITS = 2 * FC
FF_UNITS = UP_UNITS + KC * len(GROUPS)
EPS = 1e-6
NEG = -1e30
HALF = 512
assert sum(GROUPS) == FC and GROUPS[0] == KC

KEY_ROW0 = [min(max(2 * t - WIN // 2, 0), 2 * NT - WIN) for t in range(NT)]
KEY_ROWS = [9 if 2 <= t <= 5 else 8 for t in range(NT)]
BIAS_ROW0 = [KEY_ROW0[t] - 2 * t + WIN - 1 for t in range(NT)]
BIAS_ROWS = 14


def three_passes(pe, out, w_hi, w_lo, x_hi, x_lo, chunks):
    last = None
    for k in range(chunks):
        pe.matmul(out, w_hi(k), x_hi(k), start=(k == 0), stop=False)
        pe.matmul(out, w_hi(k), x_lo(k), start=False, stop=False)
        last = pe.matmul(out, w_lo(k), x_hi(k), start=False, stop=(k == chunks - 1))
    return last


def build(nc, xT, ctxT, svec, c_rows, w_mod, w_scaleT, w_modT, b_mod, gains, w_fm, w_qkv, lru_w, lru_p, qk_g, rpb,
          w_mix, w_ff, ffn_p, consts, outT, yr_d, yn_d, smr_d, smn_d, bias_d):
    with ExitStack() as top:
        def sem(name):
            return top.enter_context(nc.semaphore(name))

        def sbuf(stack, name, shape, dt=F32):
            return stack.enter_context(nc.sbuf_tensor(name, shape, dt))

        def psum(stack, name, shape):
            return stack.enter_context(nc.psum_tensor(name, shape, F32))

        mod = sbuf(top, "mod", [P, 6 * KC, 2])
        gain = sbuf(top, "gain", [P, 2, KC])
        bm = sbuf(top, "bm", [P, 6 * KC])
        ones = sbuf(top, "ones", [P, P])
        eps = sbuf(top, "eps", [P, 1])
        lrup = sbuf(top, "lrup", [P, 11, KC])
        decay = sbuf(top, "decay", [P, 2, 2, KC])
        ab = ExitStack()
        xnh = sbuf(ab, "xnh", [P, KC, N], F32R)
        xnl = sbuf(ab, "xnl", [P, KC, N], F32R)
        setup_block(nc, sem, sbuf, psum, xT, ctxT, svec, c_rows, w_mod, w_scaleT, b_mod, gains, lru_p,
                    mod, bm, gain, ones, eps, lrup, decay, xnh, xnl)
        ab.close()
        with ExitStack() as cd:
            yh = sbuf(cd, "yh", [P, KC, T], F32R)
            yl = sbuf(cd, "yl", [P, KC, T], F32R)
            with ExitStack() as rest:
                sbuf(rest, "rest_of_tokens", [P, 2 * KC * C])
                mixer_block(nc, sem, sbuf, psum, w_fm, w_qkv, lru_w, qk_g, rpb, bias_d, consts,
                            eps, lrup, decay, xnh, xnl, yh, yl, yr_d, yn_d, smr_d, smn_d)
            x1 = sbuf(cd, "x1", [P, KC, T])
            sc = sbuf(cd, "sc", [P, D])
            total = sbuf(cd, "total_x1", [P, T])
            merge_block(nc, sem, sbuf, psum, xT, w_mix, c_rows, w_modT, bm, mod, sc, total, x1, yh, yl, yn_d, smr_d, smn_d)
            ffn_block(nc, sem, sbuf, psum, w_ff, ffn_p, w_modT, bm, mod, sc, total, gain, ones, eps, x1, yh, yl, outT)


def setup_block(nc, sem, sbuf, psum, xT, ctxT, svec, c_rows, w_mod, w_scaleT, b_mod, gains, lru_p,
                mod, bm, gain, ones, eps, lrup, decay, xnh, xnl):
    ROWS = 4
    SEGS = ((0, 512), (512, 1024), (1024, N))
    with ExitStack() as st:
        xs = sbuf(st, "xs", [P, KC, N])
        sq = sbuf(st, "sq", [P, 2, N])
        total = sbuf(st, "total", [P, N])
        rs = sbuf(st, "rs", [P, N])
        tmp = sbuf(st, "tmp_norm", [P, N])
        wm = sbuf(st, "wm", [P, KC, KC, P])
        rows = sbuf(st, "rows", [P, ROWS, D])
        product = sbuf(st, "product", [P, D])
        sv = sbuf(st, "sv", [P, KC, 2])
        sr = sbuf(st, "sr", [P, 2, D])
        dots = sbuf(st, "dots", [P, KC, 2])
        gm = sbuf(st, "gm", [P, 2, KC])
        la = sbuf(st, "la", [P, 6, 2, KC])
        ss = psum(st, "ss", [P, 3, HALF])
        mp = psum(st, "mp", [P, KC, 2])

        small_in = sem("a_small_in")
        sr_in = sem("a_sr_in")
        x_in = [sem(f"a_x_in{k}") for k in range(KC)]
        wm_in = [sem(f"a_wm_in{s}") for s in range(KC)]
        rows_in = [sem(f"a_rows_in{s}") for s in range(ROWS)]
        rows_used = sem("a_rows_used")
        memset_done = sem("a_memset")
        silu_done = sem("a_silu")
        sr_done = sem("a_sr_done")
        squared = sem("a_squared")
        summed = sem("a_summed")
        mean_done = sem("a_mean")
        log_done = sem("a_log")
        root_done = sem("a_root")
        half_done = sem("a_half")
        shift_done = sem("a_shift")
        scaled = sem("a_scaled")
        hi_done = sem("a_hi")
        dve_step = sem("a_dve_step")
        lam_abs = sem("a_lam_abs")
        lam_exp = sem("a_lam_exp")
        mean = ss[:, :, :].rearrange("p a b -> p (a b)")[:, 0:N]

        with nc.Block() as block:
            @block.sync
            def _(sp):
                sp.dma_start(sv[:, :, :], svec).then_inc(small_in, 16)
                sp.dma_start(bm[:, :], b_mod).then_inc(small_in, 16)
                sp.dma_start(gain[:, :, :], gains).then_inc(small_in, 16)
                sp.dma_start(lrup[:, :, :], lru_p).then_inc(small_in, 16)
                for b in range(2):
                    sp.dma_start(wm[:, b, :, :], w_mod[b]).then_inc(wm_in[b], 16)
                sp.dma_start(sr[:, :, :], bass.AP(tensor=c_rows.tensor, offset=0, ap=[[0, P], [D, 2], [1, D]]))\
                  .then_inc(sr_in, 16)
                for k in range(KC):
                    sp.dma_start(xs[:, k, 0:C], ctxT[k]).then_inc(x_in[k], 16)
                    sp.dma_start(xs[:, k, C:N], xT[k]).then_inc(x_in[k], 16)
                    if k >= 2:
                        sp.dma_start(wm[:, k, :, :], w_mod[k]).then_inc(wm_in[k], 16)
                    if k >= ROWS:
                        sp.wait_ge(rows_used, k - ROWS + 1)
                    sp.dma_start(rows[:, k % ROWS, :], w_scaleT[k]).then_inc(rows_in[k % ROWS], 16)

            @block.gpsimd
            def _(pool):
                pool.memset(ones[:, :], 1.0).then_inc(memset_done, 1)
                pool.memset(eps[:, :], EPS).then_inc(memset_done, 1)
                pool.memset(total[:, :], 0.0).then_inc(memset_done, 1)
                for k in range(KC):
                    if k == 0:
                        pool.wait_ge(memset_done, 3)
                    else:
                        pool.wait_ge(summed, k)
                    pool.wait_ge(squared, k + 1)
                    pool.tensor_tensor(total[:, :], total[:, :], sq[:, k % 2, :], ALU.add).then_inc(summed, 1)

            @block.tensor
            def _(pe):
                pe.wait_ge(memset_done, 2)
                pe.wait_ge(silu_done, 1)
                for b in range(KC):
                    pe.wait_ge(wm_in[b], 16)
                    for k in range(KC):
                        last = pe.matmul(mp[:, b, :], wm[:, b, k, :], sv[:, k, :],
                                         start=(k == 0), stop=(k == KC - 1))
                last.then_inc(shift_done, 1)
                pe.wait_ge(summed, KC)
                for n, (c0, c1) in enumerate(SEGS):
                    last = pe.matmul(ss[:, n, 0:c1 - c0], ones[:, :], total[:, c0:c1], start=True, stop=True)
                last.then_inc(mean_done, 1)

            @block.scalar
            def _(act):
                act.wait_ge(small_in, 64)
                act.activation(sv[:, :, :], sv[:, :, :], ACT.Silu).then_inc(silu_done, 1)
                act.wait_ge(sr_in, 16)
                act.activation(sr[:, :, :], sr[:, :, :], ACT.Silu).then_inc(sr_done, 1)
                act.wait_ge(lam_abs, 1)
                act.activation(la[:, 1], la[:, 0], ACT.Exp).then_inc(lam_exp, 1)
                for k in range(KC):
                    act.wait_ge(x_in[k], 32)
                    if k >= 2:
                        act.wait_ge(summed, k - 1)
                    act.activation(sq[:, k % 2, :], xs[:, k, :], ACT.Square).then_inc(squared, 1)
                act.wait_ge(mean_done, 1)
                act.activation(rs[:, :], mean, ACT.Ln, bias=eps[:, :], scale=1.0 / D).then_inc(log_done, 1)
                act.wait_ge(log_done, 1)
                act.activation(rs[:, :], rs[:, :], ACT.Exp, scale=-0.5).then_inc(root_done, 1)
                for k in range(KC):
                    act.wait_ge(scaled, k + 1)
                    act.activation(xnh[:, k, 0:C], xs[:, k, 0:C], ACT.Identity, bias=mod[:, k, 1:2])
                    act.activation(xnh[:, k, C:N], xs[:, k, C:N], ACT.Identity, bias=mod[:, k, 0:1])\
                       .then_inc(hi_done, 1)

            @block.vector
            def _(dve):
                steps = [0]

                def then(ins):
                    steps[0] += 1
                    ins.then_inc(dve_step, 1)
                    dve.wait_ge(dve_step, steps[0])

                def scale_dots(k):
                    dve.wait_ge(rows_in[k % ROWS], (k // ROWS + 1) * 16)
                    dve.tensor_tensor_reduce(out=product[:, :], in0=rows[:, k % ROWS, :], in1=sr[:, 0, :], scale=1.0,
                                             scalar=0.0, op0=ALU.mult, op1=ALU.add, accum_out=dots[:, k, 0:1])
                    dve.tensor_tensor_reduce(out=rows[:, k % ROWS, :], in0=rows[:, k % ROWS, :], in1=sr[:, 1, :],
                                             scale=1.0, scalar=0.0, op0=ALU.mult, op1=ALU.add,
                                             accum_out=dots[:, k, 1:2]).then_inc(rows_used, 1)
                    dve.wait_ge(rows_used, k + 1)

                dve.wait_ge(small_in, 64)
                lam = lrup[:, 9:11, :]
                dve.scalar_tensor_tensor(la[:, 0], lam, -1.0, lam, ALU.mult, ALU.min).then_inc(lam_abs, 1)
                dve.wait_ge(lam_exp, 1)
                then(dve.tensor_scalar(la[:, 2], la[:, 1], 2.0, None, ALU.add))
                then(dve.reciprocal(la[:, 2], la[:, 2]))
                then(dve.tensor_tensor(la[:, 2], la[:, 1], la[:, 2], ALU.mult))
                then(dve.tensor_tensor(la[:, 3], la[:, 2], la[:, 2], ALU.mult))
                then(dve.tensor_scalar(la[:, 4], la[:, 3], 1.0 / 15, None, ALU.mult))
                for odd in (13, 11, 9, 7, 5, 3):
                    then(dve.scalar_tensor_tensor(la[:, 4], la[:, 4], 1.0 / odd, la[:, 3], ALU.add, ALU.mult))
                then(dve.scalar_tensor_tensor(la[:, 4], la[:, 4], 1.0, la[:, 2], ALU.add, ALU.mult))
                then(dve.tensor_scalar(la[:, 5], lam, -1.0, 0.0, ALU.mult, ALU.max))
                then(dve.scalar_tensor_tensor(la[:, 5], la[:, 4], 2.0, la[:, 5], ALU.mult, ALU.add))
                then(dve.tensor_scalar(decay[:, 0], la[:, 5], -8.0, None, ALU.mult))
                then(dve.tensor_scalar(decay[:, 1], la[:, 5], 8.0, None, ALU.mult))

                dve.wait_ge(sr_done, 1)
                for k in range(KC):
                    scale_dots(k)
                for w in range(2):
                    then(dve.tensor_tensor(gm[:, w, :], dots[:, :, w], bm[:, KC:2 * KC], ALU.add))
                    then(dve.scalar_tensor_tensor(gm[:, w, :], gm[:, w, :], 1.0, gain[:, 0, :],
                                                  ALU.add, ALU.mult))
                dve.wait_ge(shift_done, 1)
                then(dve.tensor_tensor(mod[:, 0:KC, :], mp[:, :, :],
                                       bm[:, 0:KC].unsqueeze(2).broadcast_to([P, KC, 2]), ALU.add))
                dve.wait_ge(log_done, 1)
                dve.tensor_scalar(tmp[:, :], mean, -0.5 / D, -0.5 * EPS, ALU.mult, ALU.add).then_inc(half_done, 1)
                dve.wait_ge(half_done, 1)
                dve.wait_ge(root_done, 1)
                then(dve.tensor_tensor(tmp[:, :], tmp[:, :], rs[:, :], ALU.mult))
                then(dve.tensor_tensor(tmp[:, :], tmp[:, :], rs[:, :], ALU.mult))
                then(dve.scalar_tensor_tensor(rs[:, :], tmp[:, :], 1.5, rs[:, :], ALU.add, ALU.mult))
                for k in range(KC + 1):
                    if k < KC:
                        dve.scalar_tensor_tensor(xs[:, k, 0:C], xs[:, k, 0:C], gm[:, 1, k:k + 1], rs[:, 0:C],
                                                 ALU.mult, ALU.mult)
                        dve.scalar_tensor_tensor(xs[:, k, C:N], xs[:, k, C:N], gm[:, 0, k:k + 1], rs[:, C:N],
                                                 ALU.mult, ALU.mult).then_inc(scaled, 1)
                    if k >= 1:
                        j = k - 1
                        dve.wait_ge(hi_done, k)
                        dve.scalar_tensor_tensor(xnl[:, j, 0:C], xs[:, j, 0:C], mod[:, j, 1:2],
                                                 xnh[:, j, 0:C].bitcast(F32), ALU.add, ALU.subtract)
                        dve.scalar_tensor_tensor(xnl[:, j, C:N], xs[:, j, C:N], mod[:, j, 0:1],
                                                 xnh[:, j, C:N].bitcast(F32), ALU.add, ALU.subtract)


XR, Q0, Q1, Q2, G, MR, MN = range(7)
RAW_SLOT = [0, 1, 2, 0, 1, 2, 1]
RAW_USE = [(0, 2), (0, 3), (0, 2), (1, 2), (1, 3), (1, 2), (2, 3)]
UNITS = 7
F_USES = 21
Q_TILES = NT + NCT
ATT = 2 * NT


def mixer_block(nc, sem, sbuf, psum, w_fm, w_qkv, lru_w, qk_g, rpb, bias_d, consts,
                eps, lrup, decay, xnh, xnl, yh, yl, yr_d, yn_d, smr_d, smn_d):
    with ExitStack() as st:
        raw = sbuf(st, "raw", [P, 3, 1024])
        fh = sbuf(st, "fh", [P, 2, KC, P], F32R)
        fl = sbuf(st, "fl", [P, 2, KC, P], F32R)
        qkv = sbuf(st, "qkv", [P, Q_TILES, 384])
        stage = sbuf(st, "stage", [P, HALF])
        bias = sbuf(st, "bias", [P, 2, BIAS_ROWS + 2, GW])
        cst = sbuf(st, "cst", [P, P + 3 * GW + 2 * NT * HD])
        gqk = sbuf(st, "gqk", [P, 2, HD])
        sqs = sbuf(st, "sqs", [P, 2, 256])
        ssq = sbuf(st, "ssq", [P, Q_TILES, 4])
        rstd = sbuf(st, "rstd", [P, 2, Q_TILES, 4])
        lw = sbuf(st, "lw", [P, 4, P])
        lp = sbuf(st, "lp", [P, 15])
        stat = sbuf(st, "stat", [P, ATT, 7])
        ysc = sbuf(st, "ysc", [P, ATT, 2])
        ytmp = sbuf(st, "ytmp", [P, 2, HD])
        zero = sbuf(st, "zero", [P, 3])
        one = sbuf(st, "one", [P, 1])
        ytok = sbuf(st, "ytok", [P, 4, P])
        yT = sbuf(st, "yT", [P, HALF])
        ident = cst[:, 0:P]
        colmask = cst[:, P:P + GW]
        edgemask = cst[:, P + GW:P + 3 * GW].rearrange("p (a c) -> p a c", c=GW)
        cosT = cst[:, P + 3 * GW:P + 3 * GW + NT * HD].rearrange("p (t f) -> p t f", f=HD)
        sinT = cst[:, P + 3 * GW + NT * HD:].rearrange("p (t f) -> p t f", f=HD)
        with ExitStack() as rnn:
            qh = sbuf(rnn, "qh", [P, KC, 384], F32R)
            ql = sbuf(rnn, "ql", [P, KC, 384], F32R)
            pad = sbuf(rnn, "pad", [P, 1288])
            xc = sbuf(rnn, "xc", [P, N])
            h0 = sbuf(rnn, "h0", [P, N])
            gD = sbuf(rnn, "gD", [P, N])
            gR = sbuf(rnn, "gR", [P, N])
            gI = sbuf(rnn, "gI", [P, N])
            gA = sbuf(rnn, "gA", [P, N])
            gel = sbuf(rnn, "gel", [P, T])
        att = st.enter_context(ExitStack())
        qpS = sbuf(att, "qpS", [P, 2, T], F32R)
        qrS = sbuf(att, "qrS", [P, 2, T], F32R)
        kS = sbuf(att, "kS", [P, 2, T], F32R)
        kX = sbuf(att, "kX", [P, 2, T], F32R)
        kcS = sbuf(att, "kcS", [P, 2, C], F32R)
        kcX = sbuf(att, "kcX", [P, 2, C], F32R)
        vS = sbuf(att, "vS", [P, Q_TILES, 2, P], F32R)
        with ExitStack() as rot:
            qrot = sbuf(rot, "qrot", [P, T])
            krot = sbuf(rot, "krot", [P, T])
            swp = sbuf(rot, "swp", [P, T])
        probT = [[sbuf(att, f"probT{part}{n}", [P, 7, P], F32R) for n in range(2)] for part in "HL"]
        prob = [sbuf(att, f"prob{n}", [P, 13, GW]) for n in range(3)]

        f_ps = [psum(st, f"f_ps{b}", [P, HALF]) for b in range(2)]
        q_ps = [psum(st, f"q_ps{b}", [P, HALF]) for b in range(2)]
        t_ps = [psum(st, f"t_ps{b}", [P, HALF]) for b in range(2)]
        o_ps = [psum(st, f"o_ps{b}", [P, HALF]) for b in range(2)]
        tr_banks = t_ps + o_ps

        raw_in = [sem(f"b_raw_in{s}") for s in range(3)]
        w_hi = sem("b_w_hi")
        w_lo = sem("b_w_lo")
        f_full = sem("b_f_full")
        f_free = sem("b_f_free")
        q_full = sem("b_q_full")
        q_free = sem("b_q_free")
        sq_used = sem("b_sq_used")
        conv_done = sem("b_conv_done")
        lw_in = sem("b_lw_in")
        decayed = sem("b_decayed")
        one_minus = sem("b_one_minus")
        rooted = sem("b_rooted")
        gates_free = sem("b_gates_free")
        dve_step = sem("b_dve_step")
        rms_root = sem("b_rms_root")
        yr_ready = sem("b_yr_ready")
        yr_out = sem("b_yr_out")
        stage_out = sem("b_stage_out")
        rope_q = sem("b_rope_q")
        rope_k = sem("b_rope_k")
        normed = sem("b_normed")
        tr_full = sem("b_tr_full")
        tr_hi = sem("b_tr_hi")
        tr_lo = sem("b_tr_lo")
        v_hi = sem("b_v_hi")
        v_lo = sem("b_v_lo")
        zeroed = sem("b_zeroed")
        y_in = [sem(f"b_y_in{n}") for n in range(3)]
        y_hi = sem("b_y_hi")
        y_lo = sem("b_y_lo")
        high_exchanged = sem("b_high_exchanged")
        low_exchanged = sem("b_low_exchanged")
        bias_set = sem("b_bias_set")
        bias_in = sem("b_bias_in")
        bias_done = sem("b_bias_done")
        const_in = sem("b_const_in")
        set_done = sem("b_set_done")
        qk_done = sem("b_qk_done")
        bound_done = sem("b_bound_done")
        exp_done = sem("b_exp_done")
        pt_full = sem("b_pt_full")
        pt_hi = sem("b_pt_hi")
        pt_lo = sem("b_pt_lo")
        pv_done = sem("b_pv_done")
        y_done = sem("b_y_done")
        yt_full = sem("b_yt_full")
        yt_ready = sem("b_yt_ready")
        yt_out = sem("b_yt_out")

        def hi_parts(u):
            if u in (Q0, Q1, Q2):
                j = u - Q0
                return (qh[:, :, :].rearrange("p k c -> p (k c)")[:, 1024 * j:1024 * j + 1024],
                        ql[:, :, :].rearrange("p k c -> p (k c)")[:, 1024 * j:1024 * j + 1024])
            s = 0 if u in (XR, MR) else 1
            return (fh[:, s, :, :].rearrange("p k c -> p (k c)"), fl[:, s, :, :].rearrange("p k c -> p (k c)"))

        values = qkv[:, :, 2 * P:3 * P].rearrange("p t (h f) -> p t h f", f=HD)

        def raw_wait(eng, u, i):
            use, uses = RAW_USE[u]
            eng.wait_ge(raw_in[RAW_SLOT[u]], (i * uses + use + 1) * 16)

        SEGS = ((0, C), (C, C + HALF), (C + HALF, N))
        TR_JOBS = ((kcS, 0, 2), (kS, 0, 4), (kS, 4, 4), (qpS, 0, 4), (qpS, 4, 4), (qrS, 0, 4), (qrS, 4, 4))
        GATES_AFTER = {1: (0, (0, 1)), 2: (0, (2, 3)), 3: (0, (4, 5)),
                       7: (1, (0, 1)), 8: (1, (2, 3)), 9: (1, (4, 5))}
        HEAD_ROWS = (slice(0, HD), slice(HD, P))

        with nc.Block() as block:
            @block.sync
            def _(sp):
                sp.dma_start(cst[:, :], consts).then_inc(const_in, 16)
                sp.dma_start(gqk[:, :, :], bass.AP(tensor=qk_g.tensor, offset=0, ap=[[0, P], [HD, 2], [1, HD]]))\
                  .then_inc(const_in, 16)

                def load(u, i):
                    if u in (Q0, Q1, Q2):
                        src = w_qkv[bass.ds(i, 1), :, 1024 * (u - Q0):1024 * (u - Q0) + 1024]
                    else:
                        src = w_fm[bass.ds(i * 4 + (u - 3 if u else 0), 1), :, :]
                    sp.dma_start(raw[:, RAW_SLOT[u], :], src.rearrange("a p c -> (a p) c"))\
                      .then_inc(raw_in[RAW_SLOT[u]], 16)

                for u in (XR, Q0, Q1):
                    load(u, 0)
                sp.wait_ge(w_lo, XR + 1)
                load(Q2, 0)

                def store(dst, i, half, src, done):
                    rows = dst[bass.ds(i, 1), :, :] if half is None else \
                        dst[bass.ds(i, 1), :, HALF * half:HALF * half + HALF]
                    sp.dma_start(rows.rearrange("a p t -> (a p) t"), src).then_inc(done, 16)

                def turn(i, first, last):
                    def load_bias():
                        for r in range(2):
                            sp.dma_start(bias[GW * r:GW * r + GW, :, 0:BIAS_ROWS, :].rearrange("p h e c -> p h (e c)"),
                                         bias_d[:, bass.ds(i * 2, 2), 2 - r:2 - r + BIAS_ROWS, :]
                                         .rearrange("p h e c -> p h (e c)")).then_inc(bias_in, 16)

                    if not first:
                        sp.wait_ge(bound_done, i * ATT)
                        load_bias()
                    if not first:
                        sp.wait_ge(f_full, i * F_USES)
                    sp.dma_start(lw[:, :, :].rearrange("p a b -> p (a b)"),
                                 lru_w[bass.ds(i, 1)].rearrange("a p c -> (a p) c")).then_inc(lw_in, 16)
                    def next_block(u, before, n):
                        sp.wait_ge(w_lo, i * UNITS + before + 1)
                        load(u, n)

                    if not first:
                        sp.wait_ge(yt_ready, i * 2)
                        store(yn_d, i - 1, 1, yT[:, :], yt_out)
                    next_block(G, Q0, i)
                    next_block(MR, Q1, i)
                    next_block(MN, G, i)
                    if not last:
                        next_block(XR, Q2, i + 1)
                    if first:
                        sp.wait_ge(bias_set, 16)
                        load_bias()
                    sp.wait_ge(yr_ready, i + 1)
                    store(yr_d, i, None, gel[:, :], yr_out)
                    for j, dst in enumerate((smr_d, smr_d, smn_d, smn_d)):
                        sp.wait_ge(f_free, i * F_USES + (17 + j + 1))
                        store(dst, i, j % 2, stage[:, :], stage_out)
                        if not last and j in (1, 3):
                            next_block(*((Q0, MN), (Q1, MR))[j // 2], i + 1)
                    if not last:
                        sp.wait_ge(w_lo, i * UNITS + (UNITS + XR + 1))
                        load(Q2, i + 1)
                    if last:
                        sp.wait_ge(yr_out, PAIRS * 16)
                        for k in range(KC - 1):
                            if k >= 3:
                                sp.wait_ge(y_lo, k - 2)
                            sp.dma_start(raw[:, k % 3, :], yr_d[k]).then_inc(y_in[k % 3], 16)
                    sp.wait_ge(yt_ready, i * 2 + 1)
                    store(yn_d, i, 0, yT[:, :], yt_out)
                    if last:
                        sp.wait_ge(y_lo, KC - 3)
                        sp.dma_start(raw[:, (KC - 1) % 3, :], yr_d[KC - 1]).then_inc(y_in[(KC - 1) % 3], 16)

                turn(0, True, False)
                with sp.Fori(1, PAIRS - 1) as i:
                    turn(i, False, False)
                turn(PAIRS - 1, False, True)
                sp.wait_ge(yt_ready, PAIRS * 2)
                store(yn_d, PAIRS - 1, 1, yT[:, :], yt_out)
                sp.wait_ge(yr_out, PAIRS * 16)
                sp.wait_ge(stage_out, PAIRS * 64)
                sp.wait_ge(yt_out, PAIRS * 32)

            @block.gpsimd
            def _(pool):
                pool.memset(ssq[:, :, :], 1.0).then_inc(set_done, 1)
                pool.memset(zero[:, :], 0.0).then_inc(set_done, 1)
                pool.memset(one[:, :], 1.0).then_inc(set_done, 1)
                pool.wait_ge(set_done, 3)
                pool.wait_ge(const_in, 32)

                def turn(i, first):
                    if not first:
                        pool.wait_ge(qk_done, i * ATT)
                    for c0, n in ((0, 2), (2 + C, 3), (261 + T, 3)):
                        pool.tensor_tensor(pad[:, c0:c0 + n], zero[:, 0:n], zero[:, 0:n], ALU.add)\
                            .then_inc(zeroed, 1)
                    pool.wait_ge(bias_in, i * 32 + 32)
                    pool.tensor_tensor(bias[:, :, BIAS_ROWS:, :], bias[:, :, 2:11:8, :],
                                       edgemask.unsqueeze(1).broadcast_to([P, 2, 2, GW]), ALU.add)\
                        .then_inc(bias_done, 1)
                    pool.wait_ge(bias_done, i * 3 + 1)
                    for h in range(2):
                        pool.tensor_tensor(bias[:, h, 0:BIAS_ROWS, :], bias[:, h, 0:BIAS_ROWS, :],
                                           colmask.unsqueeze(1).broadcast_to([P, BIAS_ROWS, GW]), ALU.add)\
                            .then_inc(bias_done, 1)
                    pool.wait_ge(bias_done, i * 3 + 3)
                    copies = 0
                    for n, (src, t0, tiles) in enumerate(TR_JOBS):
                        if src is kS or src is kcS:
                            pool.wait_ge(tr_lo, i * len(TR_JOBS) + n + 1)
                            cols = slice(P * t0, P * (t0 + tiles))
                            for h, rows in enumerate(HEAD_ROWS):
                                if copies:
                                    pool.wait_ge(low_exchanged, i * 6 + copies)
                                copies += 1
                                part = src[HEAD_ROWS[1 - h], h, cols].bitcast(F32)
                                pool.tensor_tensor((kX if src is kS else kcX)[rows, h, cols], part,
                                                   one[HEAD_ROWS[1 - h], :].broadcast_to(part.shape),
                                                   ALU.mult).then_inc(low_exchanged, 1)

                turn(0, True)
                with pool.Fori(1, PAIRS) as i:
                    pool.wait_ge(low_exchanged, i * 6)
                    turn(i, False)

            @block.tensor
            def _(pe):
                def f_bank(i, j):
                    if j >= 2:
                        pe.wait_ge(f_free, i * F_USES + j - 1)
                    return f_ps[j % 2]

                def fm(i, j, u, slot, c0, c1):
                    bank = f_bank(i, j)
                    return three_passes(pe, bank[:, 0:c1 - c0], lambda k: fh[:, slot, k, :],
                                        lambda k: fl[:, slot, k, :], lambda k: xnh[:, k, c0:c1],
                                        lambda k: xnl[:, k, c0:c1], KC).then_inc(f_full, 1)

                def fm_block(i, j, u, segs):
                    pe.wait_ge(w_lo, i * UNITS + u + 1)
                    for n, (c0, c1) in enumerate(segs):
                        fm(i, j + n, u, 0 if u in (XR, MR) else 1, c0, c1)

                def q_tile(i, t):
                    c0 = C + P * t if t < NT else P * (t - NT)
                    w0 = 0 if t < NT else P
                    if t >= 2:
                        pe.wait_ge(q_free, i * Q_TILES + t - 1)
                    last = three_passes(pe, q_ps[t % 2][:, w0:384], lambda k: xnh[:, k, c0:c0 + P],
                                        lambda k: xnl[:, k, c0:c0 + P], lambda k: qh[:, k, w0:384],
                                        lambda k: ql[:, k, w0:384], KC)
                    last.then_inc(q_full, 1)

                def gate_pieces(i, d, pieces):
                    if d == 0 and pieces[0] == 0:
                        pe.wait_ge(lw_in, i * 16 + 16)
                        pe.wait_ge(conv_done, i + 1)
                    for n in pieces:
                        c0, c1 = SEGS[n % 3]
                        bank = f_bank(i, 3 + 6 * d + n)
                        pe.matmul(bank[:, 0:c1 - c0], lw[:, 2 * (n // 3) + d, :], xc[:, c0:c1],
                                  start=True, stop=True).then_inc(f_full, 1)

                def transposes(i, jobs):
                    for n in jobs:
                        dst, t0, tiles = TR_JOBS[n]
                        if n == 0:
                            pe.wait_ge(normed, i * 2 + 2)
                            pe.wait_ge(rope_k, i + 1)
                        if n == 5:
                            pe.wait_ge(rope_q, i + 1)
                        if n >= 4:
                            pe.wait_ge(tr_lo, i * len(TR_JOBS) + n - 3)
                        for t in range(t0, t0 + tiles):
                            src = (qkv[:, t, 0:P] if dst is qpS else qkv[:, NT + t, P:2 * P] if dst is kcS
                                   else (qrot if dst is qrS else krot)[:, P * t:P * t + P])
                            last = pe.transpose(tr_banks[n % 4][:, P * (t - t0):P * (t - t0) + P], src, ident)
                        last.then_inc(tr_full, 1)

                def scores(i, u):
                    t, h = u // 2, u % 2
                    a, b = (q_ps if u % 2 == 0 else f_ps)
                    if u >= 2:
                        pe.wait_ge(exp_done, i * ATT + u - 1)
                    r0 = KEY_ROW0[t]
                    inner = KEY_ROWS[t] == 9
                    k0, n = (r0 + inner) * GW, HALF - GW * inner
                    q = qrS[:, h, P * t:P * t + P]
                    for part, k in enumerate((kS, kX)):
                        pe.matmul(a[:, 0:n], q, k[:, h, k0:k0 + n], start=(part == 0), stop=(part == 1))
                    if inner:
                        for part, k in enumerate((kS, kX)):
                            rows = k[:, h, :].rearrange("p (r c) -> p r c", c=GW)[:, r0:r0 + 9:8, :]
                            pe.matmul(b[:, 0:P], q, rows, start=(part == 0), stop=(part == 1))
                    for part, k in enumerate((kcS, kcX)):
                        last = pe.matmul(b[:, P:P + C], qpS[:, h, P * t:P * t + P], k[:, h, :],
                                         start=(part == 0), stop=(part == 1))
                    last.then_inc(qk_done, 1)

                def prob_transposes(i, u):
                    p = prob[u % 3][:, :, :].rearrange("p r c -> p (r c)")
                    pe.wait_ge(exp_done, i * ATT + u + 1)
                    if u >= 1:
                        pe.wait_ge(pt_lo, i * (2 * ATT) + 2 * u - 1)
                    for b in range(4):
                        last = pe.transpose(t_ps[0][:, P * b:P * b + P], p[:, P * b:P * b + P], ident)
                    last.then_inc(pt_full, 1)
                    if u >= 1:
                        pe.wait_ge(pt_lo, i * (2 * ATT) + 2 * u)
                    for b in range(2):
                        last = pe.transpose(t_ps[1][:, P + P * b:2 * P + P * b],
                                            p[:, 576 + P * b:576 + P * b + P], ident)
                    if KEY_ROWS[u // 2] == 9:
                        last = pe.transpose(t_ps[1][0:GW, 0:P], p[:, HALF:HALF + GW], ident)
                    last.then_inc(pt_full, 1)

                def weighted_values(i, u):
                    t, h = u // 2, u % 2
                    out = o_ps[u % 2][:, 0:P]
                    pe.wait_ge(pt_lo, i * (2 * ATT) + 2 * u + 2)
                    if u == 0:
                        pe.wait_ge(v_lo, i + 1)
                    if u >= 2:
                        pe.wait_ge(y_done, i * ATT + u - 1)
                    if u == 9:
                        pe.wait_ge(yt_ready, i * 2 + 1)
                    blocks = [(b, P, KEY_ROW0[t] // 2 + b) for b in range(4)]
                    if KEY_ROWS[t] == 9:
                        blocks.append((4, GW, KEY_ROW0[t] // 2 + 4))
                    blocks += [(5 + b, P, NT + b) for b in range(2)]
                    for b, keys, tile in blocks:
                        for part in range(2):
                            last = pe.matmul(out, probT[part][u % 2][0:keys, b, :], vS[0:keys, tile, h, :],
                                             start=(b == 0 and part == 0), stop=(b == 6 and part == 1))
                    last.then_inc(pv_done, 1)

                def y_transposes(i, j):
                    pe.wait_ge(y_done, i * ATT + (8 * j + 8))
                    for b in range(4):
                        last = pe.transpose(o_ps[1][:, P * b:P * b + P], ytok[:, b, :], ident)
                    last.then_inc(yt_full, 1)

                def turn(i, first):
                    pe.wait_ge(w_lo, i * UNITS + XR + 1)
                    fm(i, 0, XR, 0, *SEGS[0])
                    if not first:
                        y_transposes(i - 1, 1)
                    fm(i, 1, XR, 0, *SEGS[1])
                    fm(i, 2, XR, 0, *SEGS[2])
                    pe.wait_ge(w_lo, i * UNITS + Q2 + 1)
                    for t in range(Q_TILES):
                        q_tile(i, t)
                        if t in GATES_AFTER:
                            gate_pieces(i, *GATES_AFTER[t])
                    fm_block(i, 15, G, SEGS[1:])
                    pe.wait_ge(w_lo, i * UNITS + MR + 1)
                    fm(i, 17, MR, 0, *SEGS[1])
                    fm(i, 18, MR, 0, *SEGS[2])
                    transposes(i, range(0, 3))
                    pe.wait_ge(w_lo, i * UNITS + MN + 1)
                    fm(i, 19, MN, 1, *SEGS[1])
                    transposes(i, range(3, 7))
                    bank = f_bank(i, 20)
                    c0, c1 = SEGS[2]
                    for k in range(KC):
                        if k == KC - 2:
                            pe.wait_ge(q_free, i * Q_TILES + Q_TILES)
                            pe.wait_ge(tr_lo, i * len(TR_JOBS) + len(TR_JOBS))
                            pe.wait_ge(high_exchanged, i * 6 + 6)
                            pe.wait_ge(low_exchanged, i * 6 + 6)
                            scores(i, 0)
                        for w, x in ((fh, xnh), (fh, xnl), (fl, xnh)):
                            last = pe.matmul(bank[:, :], w[:, 1, k, :], x[:, k, c0:c1],
                                             start=(k == 0 and w is fh and x is xnh),
                                             stop=(k == KC - 1 and w is fl))
                    last.then_inc(f_full, 1)
                    pe.wait_ge(f_free, i * F_USES + F_USES)
                    scores(i, 1)
                    for u in range(ATT):
                        if u + 2 < ATT:
                            scores(i, u + 2)
                        prob_transposes(i, u)
                        if u == 9:
                            y_transposes(i, 0)
                        if u >= 1:
                            weighted_values(i, u - 1)
                    weighted_values(i, ATT - 1)
                    pe.wait_ge(exp_done, i * ATT + ATT)

                pe.wait_ge(const_in, 32)
                turn(0, True)
                with pe.Fori(1, PAIRS) as i:
                    turn(i, False)
                y_transposes(PAIRS - 1, 1)

            @block.scalar
            def _(act):
                def split_hi(u, i):
                    raw_wait(act, u, i)
                    act.copy(hi_parts(u)[0], raw[:, RAW_SLOT[u], :]).then_inc(w_hi, 1)

                def f_evac(i, j, out, func, **kw):
                    act.wait_ge(f_full, i * F_USES + j + 1)
                    return act.activation(out, f_ps[j % 2][:, 0:out.shape[1]], func, **kw).then_inc(f_free, 1)

                def q_evac(i, t):
                    w0 = 0 if t < NT else P
                    act.wait_ge(q_full, i * Q_TILES + t + 1)
                    act.copy(qkv[:, t, w0:384], q_ps[t % 2][:, w0:384])
                    if t >= 2:
                        act.wait_ge(sq_used, i * Q_TILES + t - 1)
                    act.activation(sqs[:, t % 2, w0:256], q_ps[t % 2][:, w0:256], ACT.Square).then_inc(q_free, 1)

                def gate_pieces(i, d, pieces):
                    if d == 1 and pieces[0] == 0:
                        act.wait_ge(gates_free, i + 1)
                    for n in pieces:
                        c0, c1 = SEGS[n % 3]
                        f_evac(i, 3 + 6 * d + n, (gR, gI)[n // 3][:, c0:c1], ACT.Sigmoid,
                               bias=lp[:, 5 + 2 * (n // 3) + d:6 + 2 * (n // 3) + d])

                def decays(i, d):
                    act.wait_ge(f_free, i * F_USES + 9 + 6 * d)
                    act.activation(gA[:, :], gR[:, :], ACT.Exp, scale=lp[:, 11 + d:12 + d])\
                       .then_inc(decayed, 1)
                    act.activation(gR[:, :], gR[:, :], ACT.Tanh, scale=lp[:, 13 + d:14 + d])
                    act.wait_ge(decayed, 4 * i + 2 * d + 1)
                    act.activation(gD[:, :], gA[:, :], ACT.Square).then_inc(decayed, 1)

                def root(i, d):
                    act.wait_ge(one_minus, 2 * i + d + 1)
                    act.activation(gD[:, :], gD[:, :], ACT.Sqrt).then_inc(rooted, 1)

                def tr_high(i, jobs):
                    for n in jobs:
                        dst, t0, tiles = TR_JOBS[n]
                        if dst is kcS:
                            act.wait_ge(yr_ready, i + 1)
                        act.wait_ge(tr_full, i * len(TR_JOBS) + n + 1)
                        for h, rows in enumerate(HEAD_ROWS):
                            last = act.copy(dst[rows, h, P * t0:P * (t0 + tiles)],
                                            tr_banks[n % 4][rows, 0:P * tiles])
                        last.then_inc(tr_hi, 1)
                        if dst is kS or dst is kcS:
                            act.wait_ge(tr_hi, i * len(TR_JOBS) + n + 1)
                            for h, rows in enumerate(HEAD_ROWS):
                                act.copy((kX if dst is kS else kcX)[HEAD_ROWS[1 - h], h, P * t0:P * (t0 + tiles)],
                                         dst[rows, h, P * t0:P * (t0 + tiles)].bitcast(F32))\
                                    .then_inc(high_exchanged, 1)

                def v_high(i):
                    act.wait_ge(yr_ready, i + 1)
                    act.copy(vS[:, :, :, 0:HD], values).then_inc(v_hi, 1)

                def soft(i, u):
                    b = (q_ps if u % 2 == 0 else f_ps)[1]
                    act.wait_ge(bound_done, i * ATT + u + 1)
                    rows = KEY_ROWS[u // 2]
                    act.activation(prob[u % 3][:, 0:rows, :], prob[u % 3][:, 0:rows, :], ACT.Exp,
                                   bias=stat[:, u, 4:5], accum_out=stat[:, u, 5:6])
                    act.activation(prob[u % 3][:, 9:13, :], b[:, P:P + C].rearrange("p (r c) -> p r c", c=GW),
                                   ACT.Exp, bias=stat[:, u, 4:5], accum_out=stat[:, u, 6:7])\
                       .then_inc(exp_done, 1)

                def probT_high(i, u):
                    act.wait_ge(pt_full, i * (2 * ATT) + 2 * u + 1)
                    if u >= 2:
                        act.wait_ge(pv_done, i * ATT + u - 1)
                    act.copy(probT[0][u % 2][:, 0:4, :], t_ps[0][:, :].rearrange("p (a b) -> p a b", b=P))\
                       .then_inc(pt_hi, 1)
                    act.wait_ge(pt_full, i * (2 * ATT) + 2 * u + 2)
                    if KEY_ROWS[u // 2] == 9:
                        act.copy(probT[0][u % 2][0:GW, 4, :], t_ps[1][0:GW, 0:P])
                    act.copy(probT[0][u % 2][:, 5:7, :], t_ps[1][:, P:3 * P].rearrange("p (a b) -> p a b", b=P))\
                       .then_inc(pt_hi, 1)

                def y_evac(i, j):
                    act.wait_ge(yt_full, i * 2 + (j + 1))
                    if not (isinstance(i, int) and i == 0 and j == 0):
                        act.wait_ge(yt_out, i * 32 + j * 16)
                    act.copy(yT[:, :], o_ps[1][:, :]).then_inc(yt_ready, 1)

                def y_high(k):
                    act.wait_ge(y_in[k % 3], (k // 3 + 1) * 16)
                    act.copy(yh[:, k, :], raw[:, k % 3, :]).then_inc(y_hi, 1)

                def branch_gate(i, first, j):
                    if j or not first:
                        act.wait_ge(stage_out, i * 64 + j * 16)
                    f_evac(i, 17 + j, stage[:, :], ACT.Sigmoid)

                act.wait_ge(set_done, 3)
                split_hi(XR, 0)

                def turn(i, first, last):
                    if not first:
                        act.wait_ge(qk_done, i * ATT)
                    for u in (Q0, Q1, Q2):
                        split_hi(u, i)
                    if first:
                        act.dma_start(bias_d.rearrange("p h e c -> (h e) p c"),
                                      bass.AP(tensor=rpb.tensor, offset=GW - 1,
                                              ap=[[P, 2 * PAIRS * 16], [-1, GW], [1, GW]])).then_inc(bias_set, 16)
                    f_evac(i, 0, pad[:, 2:2 + C], ACT.Copy)
                    if not first:
                        y_evac(i - 1, 1)
                    f_evac(i, 1, pad[:, 261:261 + HALF], ACT.Copy)
                    f_evac(i, 2, pad[:, 261 + HALF:261 + T], ACT.Copy)
                    for t in range(Q_TILES):
                        q_evac(i, t)
                        if t in GATES_AFTER:
                            gate_pieces(i, *GATES_AFTER[t])
                        if t == 3:
                            decays(i, 0)
                        if t == 4:
                            root(i, 0)
                        if t == 5:
                            split_hi(G, i)
                        if t == 6:
                            split_hi(MR, i)
                    act.wait_ge(sq_used, i * Q_TILES + Q_TILES)
                    act.activation(rstd[:, 0, :, :], ssq[:, :, :], ACT.Sqrt, bias=eps[:, :], scale=1.0 / HD)\
                       .then_inc(rms_root, 1)
                    decays(i, 1)
                    f_evac(i, 15, gel[:, 0:HALF], ACT.Gelu_apprx_tanh)
                    root(i, 1)
                    f_evac(i, 16, gel[:, HALF:T], ACT.Gelu_apprx_tanh)
                    split_hi(MN, i)
                    branch_gate(i, first, 0)
                    branch_gate(i, first, 1)
                    tr_high(i, range(0, 3))
                    v_high(i)
                    branch_gate(i, first, 2)
                    tr_high(i, range(3, 7))
                    branch_gate(i, first, 3)
                    soft(i, 0)
                    soft(i, 1)
                    for u in range(ATT):
                        probT_high(i, u)
                        if u + 2 < ATT:
                            soft(i, u + 2)
                        if not last and u == ATT - 3:
                            split_hi(XR, i + 1)
                        if u == 9:
                            y_evac(i, 0)
                        if last and u % 2 == 1:
                            y_high(u // 2)

                turn(0, True, False)
                with act.Fori(1, PAIRS - 1) as i:
                    turn(i, False, False)
                turn(PAIRS - 1, False, True)
                y_evac(PAIRS - 1, 1)

            @block.vector
            def _(dve):
                def split_lo(u, i):
                    raw_wait(dve, u, i)
                    dve.wait_ge(w_hi, i * UNITS + u + 1)
                    hi, lo = hi_parts(u)
                    dve.tensor_tensor(lo, raw[:, RAW_SLOT[u], :], hi.bitcast(F32), ALU.subtract).then_inc(w_lo, 1)

                steps = [0]

                def then(ins):
                    steps[0] += 1
                    ins.then_inc(dve_step, 1)
                    dve.wait_ge(dve_step, base[0] + steps[0])

                base = [0]

                def conv(i, first):
                    if not first:
                        dve.wait_ge(decayed, i * 4)
                    dve.tensor_scalar(lp[:, 0:11], lrup[:, :, bass.ds(i, 1)].rearrange("p a b -> p (a b)"),
                                      1.0, None, ALU.mult)
                    then(dve.tensor_scalar(lp[:, 11:15], decay[:, :, :, bass.ds(i, 1)].rearrange("p a b c -> p (a b c)"),
                                           1.0, None, ALU.mult))
                    dve.wait_ge(f_free, i * F_USES + 3)
                    dve.wait_ge(zeroed, i * 3 + 3)
                    for o, p0, n in ((0, 0, C), (C, 259, T)):
                        then(dve.tensor_scalar(xc[:, o:o + n], pad[:, p0:p0 + n], lp[:, 0:1],
                                               lp[:, 4:5], ALU.mult, ALU.add))
                        for k in range(1, 4):
                            last = dve.scalar_tensor_tensor(xc[:, o:o + n], pad[:, p0 + k:p0 + k + n],
                                                            lp[:, k:k + 1], xc[:, o:o + n],
                                                            ALU.mult, ALU.add)
                            if k < 3:
                                then(last)
                    last.then_inc(conv_done, 1)

                def head_squares(i, t):
                    g0 = 0 if t < NT else 2
                    dve.wait_ge(q_free, i * Q_TILES + t + 1)
                    dve.tensor_reduce(ssq[:, t, g0:4], sqs[:, t % 2, HD * g0:256].rearrange("p (g f) -> p g f", f=HD),
                                      AX_X, ALU.add).then_inc(sq_used, 1)

                def gated_input(i, d):
                    dve.wait_ge(f_free, i * F_USES + 9 + 6 * d)
                    then(dve.tensor_tensor(gI[:, :], gI[:, :], xc[:, :], ALU.mult))

                def complement(i, d):
                    dve.wait_ge(decayed, 4 * i + 2 * d + 2)
                    dve.scalar_tensor_tensor(gD[:, :], gD[:, :], 1.0, gR[:, :], ALU.add, ALU.mult)\
                       .then_inc(one_minus, 1)

                def scan(i, d):
                    dve.wait_ge(rooted, 2 * i + d + 1)
                    then(dve.tensor_tensor(gI[:, :], gI[:, :], gD[:, :], ALU.mult))
                    if d == 0:
                        dve.tensor_tensor_scan(h0[:, :], gA[:, :], gI[:, :], 0.0, ALU.mult, ALU.add)\
                           .then_inc(gates_free, 1)
                    else:
                        then(dve.tensor_tensor_scan(gI[:, C - 1::-1], gA[:, C - 1::-1], gI[:, C - 1::-1], 0.0,
                                                    ALU.mult, ALU.add))
                        then(dve.tensor_tensor_scan(gI[:, N - 1:C - 1:-1], gA[:, N - 1:C - 1:-1],
                                                    gI[:, N - 1:C - 1:-1], gI[:, 0:1], ALU.mult, ALU.add))
                        last = dve.tensor_tensor(h0[:, C:N], h0[:, C:N], gI[:, C:N], ALU.add)
                        then(last)

                def rnn_out(i):
                    dve.wait_ge(f_free, i * F_USES + 17)
                    dve.tensor_tensor(gel[:, :], gel[:, :], h0[:, C:N], ALU.mult).then_inc(yr_ready, 1)

                def head_norm(i, col, tiles, g):
                    x = qkv[:, 0:tiles, P * col:P * col + P].rearrange("p t (h f) -> p t h f", f=HD)
                    then(dve.tensor_tensor(x, x, ssq[:, 0:tiles, 2 * col:2 * col + 2].unsqueeze(3)
                                           .broadcast_to([P, tiles, 2, HD]), ALU.mult))
                    gb = g.unsqueeze(1).unsqueeze(1).broadcast_to([P, tiles, 2, HD])
                    dve.tensor_tensor(x, x, gb, ALU.mult).then_inc(normed, 1)

                def rotate(i, col, out, done):
                    o4 = out.rearrange("p (t h f) -> p t h f", h=2, f=HD)
                    s4 = swp[:, :].rearrange("p (t h f) -> p t h f", h=2, f=HD)
                    x = qkv[:, 0:NT, P * col:P * col + P].rearrange("p t (h f) -> p t h f", f=HD)
                    dve.tensor_tensor(o4, x, cosT.unsqueeze(2).broadcast_to([P, NT, 2, HD]), ALU.mult)
                    for h in range(2):
                        for b in range(2):
                            xs = x[:, :, h, :].rearrange("p t (a b f) -> p t a b f", a=2, b=2)[:, :, :, 1 - b, :]
                            sn = sinT.rearrange("p t (a b f) -> p t a b f", a=2, b=2)[:, :, :, b, :]
                            so = s4[:, :, h, :].rearrange("p t (a b f) -> p t a b f", a=2, b=2)[:, :, :, b, :]
                            last = dve.tensor_tensor(so, xs, sn, ALU.mult)
                    then(last)
                    dve.tensor_tensor(out, out, swp[:, :], ALU.add).then_inc(done, 1)

                def tr_low(i, jobs):
                    for n in jobs:
                        dst, t0, tiles = TR_JOBS[n]
                        cols = slice(P * t0, P * (t0 + tiles))
                        dve.wait_ge(tr_hi, i * len(TR_JOBS) + n + 1)
                        for h, rows in enumerate(HEAD_ROWS):
                            last = dve.tensor_tensor(dst[HEAD_ROWS[1 - h], h, cols],
                                                     tr_banks[n % 4][rows, 0:P * tiles],
                                                     dst[rows, h, cols].bitcast(F32), ALU.subtract)
                        last.then_inc(tr_lo, 1)

                def v_low(i):
                    dve.wait_ge(v_hi, i + 1)
                    dve.tensor_tensor(vS[:, :, :, HD:P], values, vS[:, :, :, 0:HD].bitcast(F32), ALU.subtract)\
                       .then_inc(v_lo, 1)

                def y_low(k):
                    dve.wait_ge(y_in[k % 3], (k // 3 + 1) * 16)
                    dve.wait_ge(y_hi, k + 1)
                    dve.tensor_tensor(yl[:, k, :], raw[:, k % 3, :], yh[:, k, :].bitcast(F32), ALU.subtract)\
                       .then_inc(y_lo, 1)

                def mark(ins):
                    steps[0] += 1
                    ins.then_inc(dve_step, 1)
                    return steps[0]

                def needs(step):
                    dve.wait_ge(dve_step, base[0] + step)

                def raw_maxima(i, u):
                    t, h = u // 2, u % 2
                    a, b = (q_ps if u % 2 == 0 else f_ps)
                    inner = KEY_ROWS[t] == 9
                    e = BIAS_ROW0[t] - 1 + inner
                    p = prob[u % 3]
                    dve.wait_ge(qk_done, i * ATT + u + 1)
                    dve.tensor_reduce(stat[:, u, 0:1], b[:, P:P + C], AX_X, ALU.max)
                    last = dve.tensor_tensor_reduce(
                        out=p[:, inner:8, :], in0=a[:, 0:HALF - GW * inner].rearrange("p (r c) -> p r c", c=GW),
                        in1=bias[:, h, e:e + 8 - inner, :], scale=1.0, scalar=-3.0e38, op0=ALU.add, op1=ALU.max,
                        accum_out=stat[:, u, 1:2])
                    if inner:
                        last = dve.tensor_tensor_reduce(
                            out=p[:, 0:9:8, :], in0=b[:, 0:P].rearrange("p (r c) -> p r c", c=GW),
                            in1=bias[:, h, BIAS_ROWS:, :], scale=1.0, scalar=-3.0e38, op0=ALU.add, op1=ALU.max,
                            accum_out=stat[:, u, 2:3])
                    return mark(last)

                def probT_low(i, u, bank):
                    inner = KEY_ROWS[u // 2] == 9
                    hi, lo = probT[0][u % 2], probT[1][u % 2]
                    dve.wait_ge(pt_hi, i * (2 * ATT) + (2 * u + bank + 1))
                    if bank == 0:
                        dve.tensor_tensor(lo[:, 0:4, :], t_ps[0][:, :].rearrange("p (a b) -> p a b", b=P),
                                          hi[:, 0:4, :].bitcast(F32), ALU.subtract).then_inc(pt_lo, 1)
                    else:
                        if inner:
                            dve.tensor_tensor(lo[0:GW, 4, :], t_ps[1][0:GW, 0:P], hi[0:GW, 4, :].bitcast(F32),
                                              ALU.subtract)
                        dve.tensor_tensor(lo[:, 5:7, :], t_ps[1][:, P:3 * P].rearrange("p (a b) -> p a b", b=P),
                                          hi[:, 5:7, :].bitcast(F32), ALU.subtract).then_inc(pt_lo, 1)

                def attention_step(i, low, bound, out):
                    if bound is not None:
                        maxima = raw_maxima(i, bound)
                    if out is not None:
                        dve.wait_ge(exp_done, i * ATT + out + 1)
                        total = mark(dve.tensor_tensor(ysc[:, out, 0:1], stat[:, out, 5:6], stat[:, out, 6:7], ALU.add))
                    if bound is not None:
                        needs(maxima)
                        inner = KEY_ROWS[bound // 2] == 9
                        top = mark(dve.tensor_reduce(stat[:, bound, 3:4], stat[:, bound, 0:2 + inner], AX_X, ALU.max))
                    if out is not None:
                        needs(total)
                        inverse = mark(dve.reciprocal(ysc[:, out, 1:2], ysc[:, out, 0:1]))
                    if bound is not None:
                        needs(top)
                        dve.tensor_scalar(stat[:, bound, 4:5], stat[:, bound, 3:4], -1.0, None, ALU.mult)\
                           .then_inc(bound_done, 1)
                    if low is not None:
                        probT_low(i, low, 0)
                        probT_low(i, low, 1)
                    if out is not None:
                        t, h = out // 2, out % 2
                        needs(inverse)
                        dve.wait_ge(pv_done, i * ATT + out + 1)
                        half = mark(dve.tensor_scalar(ytmp[:, out % 2, :], o_ps[out % 2][:, 0:HD], ysc[:, out, 1:2],
                                                      None, ALU.mult))
                        if out == 8:
                            dve.wait_ge(yt_full, i * 2 + 1)
                        if out == 0 and not (isinstance(i, int) and i == 0):
                            dve.wait_ge(yt_full, i * 2)
                        needs(half)
                        dve.scalar_tensor_tensor(ytok[:, t % 4, HD * h:HD * h + HD], o_ps[out % 2][:, HD:P],
                                                 ysc[:, out, 1:2], ytmp[:, out % 2, :], ALU.mult, ALU.add)\
                           .then_inc(y_done, 1)

                dve.wait_ge(const_in, 32)
                then(dve.tensor_scalar(gqk[:, 0, :], gqk[:, 0, :], HD ** -0.5, None, ALU.mult))
                split_lo(XR, 0)

                def turn(i, first, last):
                    base[0] = 1 + i * STEPS
                    steps[0] = 0
                    for u in (Q0, Q1, Q2):
                        split_lo(u, i)
                    conv(i, first)
                    for t in range(Q_TILES):
                        head_squares(i, t)
                        if t == 3:
                            gated_input(i, 0)
                            complement(i, 0)
                        if t == 4:
                            scan(i, 0)
                        if t == 5:
                            split_lo(G, i)
                        if t == 6:
                            split_lo(MR, i)
                    gated_input(i, 1)
                    dve.wait_ge(rms_root, i + 1)
                    rt, v = rstd[:, 0, :, :], ssq[:, :, :]
                    then(dve.reciprocal(rt, rt))
                    dve.tensor_scalar(v, v, -0.5 / HD, -0.5 * EPS, ALU.mult, ALU.add)
                    then(dve.tensor_tensor(rstd[:, 1, :, :], rt, rt, ALU.mult))
                    then(dve.tensor_tensor(v, v, rstd[:, 1, :, :], ALU.mult))
                    then(dve.scalar_tensor_tensor(v, v, 1.5, rt, ALU.add, ALU.mult))
                    head_norm(i, 1, Q_TILES, gqk[:, 1, :])
                    head_norm(i, 0, NT, gqk[:, 0, :])
                    complement(i, 1)
                    scan(i, 1)
                    dve.wait_ge(normed, i * 2 + 1)
                    rotate(i, 1, krot[:, :], rope_k)
                    rnn_out(i)
                    split_lo(MN, i)
                    dve.wait_ge(normed, i * 2 + 2)
                    dve.wait_ge(rope_k, i + 1)
                    rotate(i, 0, qrot[:, :], rope_q)
                    tr_low(i, range(0, 7))
                    v_low(i)
                    dve.wait_ge(bias_done, 3 * i + 3)
                    dve.wait_ge(yr_out, i * 16 + 16)
                    attention_step(i, None, 0, None)
                    attention_step(i, None, 1, None)
                    for u in range(ATT):
                        attention_step(i, u, u + 2 if u + 2 < ATT else None, u - 1 if u >= 1 else None)
                        if not last and u == ATT - 2:
                            split_lo(XR, i + 1)
                        if last and u % 2 == 1:
                            y_low(u // 2)
                    attention_step(i, None, None, ATT - 1)
                    assert steps[0] == STEPS, steps[0]

                turn(0, True, False)
                with dve.Fori(1, PAIRS - 1) as i:
                    turn(i, False, False)
                turn(PAIRS - 1, False, True)


STEPS = 3 + 1 + 6 + 1 + 1 + 1 + 4 + 1 + 3 + 3 + ATT * 5 - 2


def mod_column(dve, n, b, row, sc, dots, bm, mod, dotted, mod_done, count):
    dve.tensor_tensor_reduce(out=row, in0=row, in1=sc[:, :], scale=1.0, scalar=0.0, op0=ALU.mult, op1=ALU.add,
                             accum_out=dots[:, b:b + 1]).then_inc(dotted, 1)
    dve.wait_ge(dotted, count)
    dve.tensor_tensor(mod[:, bass.ds(n, 1), 0:1].rearrange("p a b -> p (a b)"), dots[:, b:b + 1],
                      bm[:, bass.ds(n, 1)], ALU.add).then_inc(mod_done, 1)


def merge_block(nc, sem, sbuf, psum, xT, w_mix, c_rows, w_modT, bm, mod, sc, total, x1, yh, yl, yn_d, smr_d, smn_d):
    with ExitStack() as st:
        raw = sbuf(st, "raw_c", [P, 2, 1024])
        wh = sbuf(st, "wh_c", [P, 2, KC, P], F32R)
        wl = sbuf(st, "wl_c", [P, 2, KC, P], F32R)
        ah = [yh, sbuf(st, "na_h", [P, KC, T], F32R)]
        al = [yl, sbuf(st, "na_l", [P, KC, T], F32R)]
        aux = sbuf(st, "aux", [P, 2, T])
        ys = sbuf(st, "ys", [P, 2, T])
        rows = sbuf(st, "rows_c", [P, 2, D])
        dots = sbuf(st, "dots_c", [P, 2])
        square = sbuf(st, "square_c", [P, HALF])
        squared, zeroed = sem("c_squared"), sem("c_zeroed")
        ps = psum(st, "ps_c", [P, 4, HALF])
        c_in, c_silu = sem("c_c_in"), sem("c_c_silu")
        rows_in = [sem(f"c_rows_in{s}") for s in range(2)]
        dotted, mod_done = sem("c_dotted"), sem("c_mod_done")
        raw_in = [sem(f"c_raw_in{s}") for s in range(2)]
        aux_in = [sem(f"c_aux_in{s}") for s in range(2)]
        ys_in = [sem(f"c_ys_in{s}") for s in range(2)]
        w_hi, w_lo = sem("c_w_hi"), sem("c_w_lo")
        y_hi, y_lo = sem("c_y_hi"), sem("c_y_lo")
        full, free = sem("c_full"), sem("c_free")
        part = sem("c_part")
        merged_hi, merged_lo = sem("c_merged_hi"), sem("c_merged_lo")
        units = 3 * KC
        flat = lambda a, s: a[:, s, :, :].rearrange("p k c -> p (k c)")

        with nc.Block() as block:
            @block.sync
            def _(sp):
                for n in range(2):
                    sp.dma_start(raw[:, n, :], w_mix[n]).then_inc(raw_in[n], 16)
                sp.dma_start(sc[:, :], bass.AP(tensor=c_rows.tensor, offset=0, ap=[[0, P], [1, D]])).then_inc(c_in, 16)
                for n in range(2):
                    sp.dma_start(rows[:, n, :], w_modT[n]).then_inc(rows_in[n], 16)
                with sp.Fori(0, units // 2 - 1) as r:
                    for b in range(2):
                        sp.wait_ge(w_lo, r * 2 + b + 1)
                        sp.dma_start(raw[:, b, :], w_mix[bass.ds(r * 2 + b + 2, 1)].rearrange("a p c -> (a p) c"))\
                          .then_inc(raw_in[b], 16)
                        sp.wait_ge(mod_done, r * 2 + b + 1)
                        sp.dma_start(rows[:, b, :], w_modT[bass.ds(r * 2 + b + 2, 1)].rearrange("a p c -> (a p) c"))\
                          .then_inc(rows_in[b], 16)

            @block.gpsimd
            def _(pool):
                pool.memset(total[:, :], 0.0).then_inc(zeroed, 1)
                for n in range(2):
                    pool.dma_start(aux[:, n, :], smr_d[n]).then_inc(aux_in[n], 16)
                for n in range(KC):
                    if n >= 2:
                        pool.wait_ge(y_lo, n - 1)
                    pool.dma_start(ys[:, n % 2, :], yn_d[n]).then_inc(ys_in[n % 2], 16)
                    if n >= 2:
                        pool.wait_ge(free, 2 * n - 2)
                        pool.dma_start(aux[:, n % 2, :], smr_d[n]).then_inc(aux_in[n % 2], 16)
                for n in range(KC, units):
                    src = (smr_d, smn_d, xT)[n // KC]
                    pool.wait_ge(free, 2 * n - 2)
                    pool.dma_start(aux[:, n % 2, :], src[n % KC]).then_inc(aux_in[n % 2], 16)

            @block.tensor
            def _(pe):
                for ph in range(3):
                    if ph == 1:
                        pe.wait_ge(y_lo, KC)
                    if ph == 2:
                        pe.wait_ge(merged_lo, 2 * KC - 2)
                    s = ph % 2

                    def block_pair(r):
                        for b in range(2):
                            n = r * 2 + (KC * ph + b)
                            pe.wait_ge(w_lo, n + 1)
                            if ph == 2 and isinstance(r, int) and b == 0:
                                pe.wait_ge(free, n * 2 - 2)
                                for k in range(KC):
                                    if k == KC - 1:
                                        pe.wait_ge(merged_lo, 2 * KC)
                                    for half in range(2):
                                        cols = slice(HALF * half, HALF * half + HALF)
                                        for w, y in ((wh, ah[s]), (wh, al[s]), (wl, ah[s])):
                                            last = pe.matmul(ps[:, half, :], w[:, b, k, :], y[:, k, cols],
                                                             start=(k == 0 and w is wh and y is ah[s]),
                                                             stop=(k == KC - 1 and w is wl))
                                        if k == KC - 1:
                                            last.then_inc(full, 1)
                                continue
                            for half in range(2):
                                if not (isinstance(n, int) and n < 2):
                                    pe.wait_ge(free, n * 2 + half - 3)
                                cols = slice(HALF * half, HALF * half + HALF)
                                three_passes(pe, ps[:, 2 * b + half, :], lambda k: wh[:, b, k, :],
                                             lambda k: wl[:, b, k, :], lambda k: ah[s][:, k, cols],
                                             lambda k: al[s][:, k, cols], KC).then_inc(full, 1)

                    block_pair(0)
                    with pe.Fori(1, KC // 2) as r:
                        block_pair(r)

            @block.scalar
            def _(act):
                def w_split(n, b):
                    act.wait_ge(raw_in[b], (n // 2) * 16 + 16 if isinstance(n, int) else (n - b) * 8 + 16)
                    act.copy(flat(wh, b), raw[:, b, :]).then_inc(w_hi, 1)

                def y_split(n):
                    act.wait_ge(ys_in[n % 2], (n // 2) * 16 + 16)
                    act.copy(ah[1][:, n, :], ys[:, n % 2, :]).then_inc(y_hi, 1)

                w_split(0, 0)
                w_split(1, 1)
                act.wait_ge(c_in, 16)
                act.activation(sc[:, :], sc[:, :], ACT.Silu).then_inc(c_silu, 1)
                for n in range(KC):
                    y_split(n)
                    act.wait_ge(full, 2 * n + 2)
                    w_split(n + 2, n % 2)
                with act.Fori(KC // 2, units // 2 - 1) as r:
                    for b in range(2):
                        act.wait_ge(full, r * 4 + (2 * b + 2))
                        w_split(r * 2 + (b + 2), b)

            @block.vector
            def _(dve):
                def w_split(n, b):
                    dve.wait_ge(w_hi, n + 1)
                    dve.wait_ge(raw_in[b], (n // 2) * 16 + 16 if isinstance(n, int) else (n - b) * 8 + 16)
                    dve.tensor_tensor(flat(wl, b), raw[:, b, :], flat(wh, b).bitcast(F32), ALU.subtract)\
                       .then_inc(w_lo, 1)

                def y_split(n):
                    dve.wait_ge(y_hi, n + 1)
                    dve.wait_ge(ys_in[n % 2], (n // 2) * 16 + 16)
                    dve.tensor_tensor(al[1][:, n, :], ys[:, n % 2, :],
                                      ah[1][:, n, :].bitcast(F32), ALU.subtract).then_inc(y_lo, 1)

                w_split(0, 0)
                w_split(1, 1)
                dve.wait_ge(c_silu, 1)
                dve.wait_ge(zeroed, 1)
                for ph in range(3):
                    if ph == 2:
                        dve.wait_ge(mod_done, KC)

                    def step(n, m, b, more):
                        dve.wait_ge(rows_in[b], (n - b) * 8 + 16)
                        dve.wait_ge(aux_in[b], (n - b) * 8 + 16)
                        for half in range(2):
                            cols = slice(HALF * half, HALF * half + HALF)
                            out = x1[:, bass.ds(m, 1), cols].rearrange("p a c -> p (a c)")
                            dve.wait_ge(full, n * 2 + half + 1)
                            if ph == 0:
                                dve.tensor_tensor(out, ps[:, 2 * b + half, :], aux[:, b, cols], ALU.mult)\
                                   .then_inc(free, 1)
                            elif ph == 1:
                                dve.tensor_tensor(aux[:, b, cols], ps[:, 2 * b + half, :], aux[:, b, cols],
                                                  ALU.mult).then_inc(part, 1)
                                dve.wait_ge(part, m * 2 + half + 1)
                                dve.tensor_tensor(out, out, aux[:, b, cols], ALU.add)\
                                   .then_inc(free, 1)
                                dve.wait_ge(free, n * 2 + half + 1)
                            else:
                                dve.scalar_tensor_tensor(out, ps[:, 2 * b + half, :],
                                                         mod[:, bass.ds(m + 2 * KC, 1), 0:1].rearrange("p a b -> p (a b)"),
                                                         aux[:, b, cols], ALU.mult, ALU.add).then_inc(free, 1)
                                dve.wait_ge(free, n * 2 + half + 1)
                                dve.tensor_tensor(square[:, :], out, out, ALU.mult).then_inc(squared, 1)
                                dve.wait_ge(squared, m * 2 + half + 1)
                                dve.tensor_tensor(total[:, cols], total[:, cols], square[:, :], ALU.add)
                            if half == 0:
                                mod_column(dve, n + 2 * KC, b, rows[:, b, :], sc, dots, bm, mod,
                                           dotted, mod_done, n + 1)
                        if more:
                            w_split(n + 2, b)
                        if ph == 1:
                            for half in range(2):
                                cols = slice(HALF * half, HALF * half + HALF)
                                out = x1[:, bass.ds(m, 1), cols]
                                dve.tensor_scalar(ah[0][:, bass.ds(m, 1), cols], out, 1.0, None, ALU.mult)\
                                   .then_inc(merged_hi, 1)
                                dve.wait_ge(merged_hi, m * 2 + half + 1)
                                dve.tensor_tensor(al[0][:, bass.ds(m, 1), cols], out,
                                                  ah[0][:, bass.ds(m, 1), cols].bitcast(F32), ALU.subtract)\
                                   .then_inc(merged_lo, 1)

                    if ph == 0:
                        for n in range(KC):
                            y_split(n)
                            step(n, n, n % 2, True)
                    else:
                        with dve.Fori(0, KC // 2 - (ph == 2)) as r:
                            for b in range(2):
                                step(r * 2 + (KC * ph + b), r * 2 + b, b, True)
                    if ph == 2:
                        for b in range(2):
                            step(units - 2 + b, KC - 2 + b, b, False)


def ffn_block(nc, sem, sbuf, psum, w_ff, ffn_p, w_modT, bm, mod, sc, total, gain, ones, eps, x1, xh, xl, outT):
    with ExitStack() as st:
        hh = sbuf(st, "hh_d", [P, max(GROUPS), T], F32R)
        hl = sbuf(st, "hl_d", [P, max(GROUPS), T], F32R)
        raw = sbuf(st, "raw_d", [P, 2, 1024])
        wh = sbuf(st, "wh_d", [P, 2, KC, P], F32R)
        wl = sbuf(st, "wl_d", [P, 2, KC, P], F32R)
        ca = sbuf(st, "ca", [P, T])
        cg = sbuf(st, "cg", [P, T])
        fp = sbuf(st, "fp", [P, FC, 8])
        gm = sbuf(st, "gm_d", [P, KC])
        fps = sbuf(st, "fps", [P, 8])
        rows = sbuf(st, "rows_d", [P, D])
        dots = sbuf(st, "dots_d", [P, 1])
        rows_in, dotted, mod_done = sem("d_rows_in"), sem("d_dotted"), sem("d_mod_done")
        pa = psum(st, "pa", [P, T])
        pg = psum(st, "pg", [P, T])
        pd = psum(st, "pd", [P, 4, HALF])
        scaled_chunk = lambda k: pd[:, 2 * (k % 2):2 * (k % 2) + 2, :].rearrange("p a b -> p (a b)")
        fp_in = sem("d_fp_in")
        raw_in = [sem(f"d_raw_in{s}") for s in range(2)]
        mean_done, rstd_done = sem("d_mean"), sem("d_rstd")
        log_done, root_done = sem("d_log"), sem("d_root")
        mean = pd[:, 0:2, :].rearrange("p a b -> p (a b)")
        gm_done, scaled, hi_done, lo_done = sem("d_gm"), sem("d_scaled"), sem("d_hi"), sem("d_lo")
        w_hi, w_lo, used = sem("d_w_hi"), sem("d_w_lo"), sem("d_used")
        centre = sem("d_centre")
        conv_step, conved = sem("d_conv_step"), sem("d_conved")
        silu_done, gated, h_hi, h_lo = sem("d_silu"), sem("d_gated"), sem("d_h_hi"), sem("d_h_lo")
        taps_in = sem("d_taps_in")
        full, free = sem("d_full"), sem("d_free")
        stored = sem("d_stored")
        flat = lambda a, s: a[:, s, :, :].rearrange("p k c -> p (k c)")
        starts = []
        n = 0
        for g, pairs in enumerate(GROUPS):
            starts.append((n, sum(GROUPS[:g]), n + 2 * pairs))
            n += 2 * pairs + KC

        with nc.Block() as block:
            @block.sync
            def _(sp):
                sp.dma_start(fp[:, :, :], ffn_p).then_inc(fp_in, 16)
                for n in range(2):
                    sp.dma_start(raw[:, n, :], w_ff[n]).then_inc(raw_in[n], 16)
                sp.dma_start(rows[:, :], w_modT[3 * KC]).then_inc(rows_in, 16)

                def load_pair(r):
                    for b in range(2):
                        sp.wait_ge(w_lo, r * 2 + b + 1)
                        sp.dma_start(raw[:, b, :], w_ff[bass.ds(r * 2 + b + 2, 1)].rearrange("a p c -> (a p) c"))\
                          .then_inc(raw_in[b], 16)

                with sp.Fori(0, GROUPS[0] - 1) as r:
                    load_pair(r)
                    sp.wait_ge(mod_done, r + 1)
                    sp.dma_start(rows[:, :], w_modT[bass.ds(r + (3 * KC + 1), 1)].rearrange("a p c -> (a p) c"))\
                      .then_inc(rows_in, 16)
                with sp.Fori(GROUPS[0] - 1, FF_UNITS // 2 - 1) as r:
                    load_pair(r)
                with sp.Fori(0, KC) as m:
                    sp.wait_ge(free, m * 2 + (2 * KC * (len(GROUPS) - 1) + 2))
                    sp.dma_start(outT[bass.ds(m, 1)].rearrange("a p t -> (a p) t"),
                                 x1[:, bass.ds(m, 1), :].rearrange("p a t -> p (a t)")).then_inc(stored, 16)
                sp.wait_ge(stored, 16 * KC)

            @block.tensor
            def _(pe):
                for half in range(2):
                    last = pe.matmul(pd[:, half, :], ones[:, :], total[:, HALF * half:HALF * half + HALF],
                                     start=True, stop=True)
                last.then_inc(mean_done, 1)
                for g, pairs in enumerate(GROUPS):
                    u0, j0, d0 = starts[g]
                    def up_pair(j):
                        for b, bank in enumerate((pa, pg)):
                            pe.wait_ge(w_lo, j * 2 + (u0 + b + 1))
                            if not (isinstance(j, int) and j0 == 0):
                                pe.wait_ge(conved, j * 2 + (2 * j0 + b - 1))
                            if isinstance(j, int) and j0 == 0 and b == 0:
                                for k in range(KC):
                                    pe.wait_ge(lo_done, k + 1)
                                    for half in range(2):
                                        cols = slice(HALF * half, HALF * half + HALF)
                                        for w, x in ((wh, xh), (wh, xl), (wl, xh)):
                                            last = pe.matmul(bank[:, cols], w[:, b, k, :], x[:, k, cols],
                                                             start=(k == 0 and w is wh and x is xh),
                                                             stop=(k == KC - 1 and w is wl))
                                last.then_inc(used, 1)
                                continue
                            for half in range(2):
                                cols = slice(HALF * half, HALF * half + HALF)
                                last = three_passes(pe, bank[:, cols], lambda k: wh[:, b, k, :],
                                                    lambda k: wl[:, b, k, :], lambda k: xh[:, k, cols],
                                                    lambda k: xl[:, k, cols], KC)
                            last.then_inc(used, 1)

                    up_pair(0)
                    with pe.Fori(1, pairs) as j:
                        up_pair(j)
                    def down_pair(r):
                        for b in range(2):
                            pe.wait_ge(w_lo, r * 2 + (d0 + b + 1))
                            if isinstance(r, int) and b == 0:
                                pe.wait_ge(h_lo, j0 + pairs - 1)
                                for k in range(pairs):
                                    if k == pairs - 1:
                                        pe.wait_ge(h_lo, j0 + pairs)
                                    for half in range(2):
                                        cols = slice(HALF * half, HALF * half + HALF)
                                        if k == 0 and g > 0:
                                            pe.wait_ge(free, 2 * KC * g + half - 3)
                                        for w, h in ((wh, hh), (wh, hl), (wl, hh)):
                                            last = pe.matmul(pd[:, half, :], w[:, b, k, :], h[:, k, cols],
                                                             start=(k == 0 and w is wh and h is hh),
                                                             stop=(k == pairs - 1 and w is wl))
                                        if k == pairs - 1:
                                            last.then_inc(full, 1)
                                continue
                            for half in range(2):
                                cols = slice(HALF * half, HALF * half + HALF)
                                if not (isinstance(r, int) and g == 0):
                                    pe.wait_ge(free, r * 4 + (2 * KC * g + 2 * b + half - 3))
                                three_passes(pe, pd[:, 2 * b + half, :], lambda k: wh[:, b, k, :],
                                                    lambda k: wl[:, b, k, :], lambda k: hh[:, k, cols],
                                                    lambda k: hl[:, k, cols], pairs).then_inc(full, 1)

                    down_pair(0)
                    with pe.Fori(1, KC // 2) as r:
                        down_pair(r)

            @block.scalar
            def _(act):
                def w_split(n, b):
                    act.wait_ge(raw_in[b], (n // 2) * 16 + 16 if isinstance(n, int) else (n - b) * 8 + 16)
                    act.copy(flat(wh, b), raw[:, b, :]).then_inc(w_hi, 1)

                act.wait_ge(mean_done, 1)
                act.activation(cg[:, :], mean, ACT.Ln, bias=eps[:, :], scale=1.0 / D).then_inc(log_done, 1)
                act.wait_ge(log_done, 1)
                act.activation(cg[:, :], cg[:, :], ACT.Exp, scale=-0.5).then_inc(root_done, 1)
                w_split(0, 0)
                w_split(1, 1)
                for k in range(KC):
                    act.wait_ge(scaled, k + 1)
                    act.activation(xh[:, k, :], scaled_chunk(k), ACT.Identity,
                                   bias=mod[:, 3 * KC + k, 0:1]).then_inc(hi_done, 1)
                act.wait_ge(fp_in, 16)
                for g, pairs in enumerate(GROUPS):
                    u0, j0, d0 = starts[g]
                    def up_pair(j):
                        for b, (bank, out) in enumerate(((pa, ca), (pg, cg))):
                            act.wait_ge(used, j * 2 + (2 * j0 + b + 1))
                            if b == 0 and not (isinstance(j, int) and j0 == 0):
                                act.wait_ge(h_lo, j + j0)
                            if b == 0:
                                act.wait_ge(taps_in, j + (j0 + 1))
                            act.activation(out[:, :], bank[:, :], ACT.Identity, bias=fps[:, 4 * b + 3:4 * b + 4],
                                           scale=fps[:, 4 * b + 1:4 * b + 2]).then_inc(centre, 1)
                            w_split(j * 2 + (u0 + b + 2), b)
                        act.wait_ge(conved, j * 2 + (2 * j0 + 1))
                        act.activation(ca[:, :], ca[:, :], ACT.Silu).then_inc(silu_done, 1)

                    up_pair(0)
                    with act.Fori(1, pairs) as j:
                        up_pair(j)
                    turns = KC // 2 - (g == len(GROUPS) - 1)
                    with act.Fori(0, turns) as r:
                        for b in range(2):
                            act.wait_ge(full, r * 4 + (2 * KC * g + 2 * b + 2))
                            w_split(r * 2 + (d0 + b + 2), b)

            @block.vector
            def _(dve):
                def w_split(n, b):
                    dve.wait_ge(w_hi, n + 1)
                    dve.wait_ge(raw_in[b], (n // 2) * 16 + 16 if isinstance(n, int) else (n - b) * 8 + 16)
                    dve.tensor_tensor(flat(wl, b), raw[:, b, :], flat(wh, b).bitcast(F32), ALU.subtract)\
                       .then_inc(w_lo, 1)

                dve.scalar_tensor_tensor(gm[:, :], mod[:, 4 * KC:5 * KC, 0], 1.0, gain[:, 1, :], ALU.add, ALU.mult)\
                   .then_inc(gm_done, 1)
                dve.wait_ge(gm_done, 1)
                dve.wait_ge(log_done, 1)
                dve.tensor_scalar(ca[:, :], mean, -0.5 / D, -0.5 * EPS, ALU.mult, ALU.add).then_inc(rstd_done, 1)
                dve.wait_ge(rstd_done, 1)
                dve.wait_ge(root_done, 1)
                for n in range(2):
                    dve.tensor_tensor(ca[:, :], ca[:, :], cg[:, :], ALU.mult).then_inc(rstd_done, 1)
                    dve.wait_ge(rstd_done, 2 + n)
                dve.scalar_tensor_tensor(cg[:, :], ca[:, :], 1.5, cg[:, :], ALU.add, ALU.mult).then_inc(rstd_done, 1)
                dve.wait_ge(rstd_done, 4)
                for k in range(KC + 1):
                    if k == 1:
                        w_split(0, 0)
                    if k == 3:
                        w_split(1, 1)
                    if k < KC:
                        if k >= 2:
                            dve.wait_ge(lo_done, k - 1)
                        dve.scalar_tensor_tensor(scaled_chunk(k), x1[:, k, :], gm[:, k:k + 1],
                                                 cg[:, :], ALU.mult, ALU.mult).then_inc(scaled, 1)
                    if k >= 1:
                        j = k - 1
                        dve.wait_ge(hi_done, k)
                        dve.scalar_tensor_tensor(xl[:, j, :], scaled_chunk(j),
                                                 mod[:, 3 * KC + j, 0:1], xh[:, j, :].bitcast(F32),
                                                 ALU.add, ALU.subtract).then_inc(lo_done, 1)
                dve.wait_ge(fp_in, 16)
                for g, pairs in enumerate(GROUPS):
                    u0, j0, d0 = starts[g]
                    def up_pair(j):
                        if not (isinstance(j, int) and j0 == 0):
                            dve.wait_ge(centre, j * 2 + 2 * j0)
                        dve.tensor_scalar(fps[:, :], fp[:, bass.ds(j + j0, 1), :].rearrange("p a b -> p (a b)"),
                                          1.0, None, ALU.mult).then_inc(taps_in, 1)
                        dve.wait_ge(taps_in, j + (j0 + 1))
                        for b, (bank, out) in enumerate(((pa, ca), (pg, cg))):
                            tap = lambda k: fps[:, 4 * b + k:4 * b + k + 1]
                            dve.wait_ge(centre, j * 2 + (2 * j0 + b + 1))
                            dve.scalar_tensor_tensor(out[:, 1:T], bank[:, 0:T - 1], tap(0), out[:, 1:T],
                                                     ALU.mult, ALU.add).then_inc(conv_step, 1)
                            dve.wait_ge(conv_step, j * 2 + (2 * j0 + b + 1))
                            dve.scalar_tensor_tensor(out[:, 0:T - 1], bank[:, 1:T], tap(2), out[:, 0:T - 1],
                                                     ALU.mult, ALU.add).then_inc(conved, 1)
                            if g == 0 and b == 0:
                                dve.wait_ge(rows_in, j * 16 + 16)
                            w_split(j * 2 + (u0 + b + 2), b)
                            if g == 0 and b == 0:
                                mod_column(dve, j + 5 * KC, 0, rows[:, :], sc, dots, bm, mod, dotted, mod_done, j + 1)
                        dve.wait_ge(conved, j * 2 + (2 * j0 + 2))
                        dve.wait_ge(silu_done, j + (j0 + 1))
                        dve.tensor_tensor(ca[:, :], ca[:, :], cg[:, :], ALU.mult).then_inc(gated, 1)
                        dve.wait_ge(gated, j + (j0 + 1))
                        dve.tensor_scalar(hh[:, bass.ds(j, 1), :].rearrange("p a t -> p (a t)"), ca[:, :],
                                          1.0, None, ALU.mult).then_inc(h_hi, 1)
                        dve.wait_ge(h_hi, j + (j0 + 1))
                        dve.tensor_tensor(hl[:, bass.ds(j, 1), :].rearrange("p a t -> p (a t)"), ca[:, :],
                                          hh[:, bass.ds(j, 1), :].rearrange("p a t -> p (a t)").bitcast(F32),
                                          ALU.subtract).then_inc(h_lo, 1)

                    up_pair(0)
                    with dve.Fori(1, pairs) as j:
                        up_pair(j)
                    if g == 0:
                        dve.wait_ge(mod_done, KC)

                    def down(n, m, b, more):
                        for half in range(2):
                            cols = slice(HALF * half, HALF * half + HALF)
                            out = x1[:, bass.ds(m, 1), cols].rearrange("p a c -> p (a c)")
                            dve.wait_ge(full, m * 2 + (2 * KC * g + half + 1))
                            dve.scalar_tensor_tensor(out, pd[:, 2 * b + half, :],
                                                     mod[:, bass.ds(m + 5 * KC, 1), 0:1].rearrange("p a b -> p (a b)"),
                                                     out, ALU.mult, ALU.add).then_inc(free, 1)
                        if more:
                            w_split(n + 2, b)

                    last_group = g == len(GROUPS) - 1
                    with dve.Fori(0, KC // 2 - last_group) as r:
                        for b in range(2):
                            down(r * 2 + (d0 + b), r * 2 + b, b, True)
                    if last_group:
                        for b in range(2):
                            down(d0 + KC - 2 + b, KC - 2 + b, b, False)


def constants():
    col = np.arange(GW)
    start = np.clip(col - 8, 0, GW - 16)
    inside = (col[None, :] >= start[:, None]) & (col[None, :] < start[:, None] + 16)
    mask = np.where(inside, 0.0, NEG).astype(np.float32)
    mask = np.concatenate([mask, mask], 0)
    lower = np.where(np.arange(P) >= GW, NEG, 0.0).astype(np.float32)[:, None]
    edges = np.concatenate([mask + lower, mask + (np.float32(NEG) - lower)], 1)
    n = HD // 4
    freq = (np.float32(10000.0) ** (-np.arange(n, dtype=np.float32) / np.float32(n))).astype(np.float32)
    tok = np.arange(T)
    cos = np.zeros((T, 2, 2, n), np.float32)
    sin = np.zeros((T, 2, 2, n), np.float32)
    for a, pos in enumerate((tok // GW, tok % GW)):
        ang = (pos.astype(np.float32)[:, None] * freq).astype(np.float32)
        for b in range(2):
            cos[:, a, b] = np.cos(ang)
            sin[:, a, b] = np.sin(ang) * (1 if b else -1)
    tiles = lambda a: a.reshape(NT, P, HD).transpose(1, 0, 2).reshape(P, NT * HD)
    table = np.concatenate([np.eye(P, dtype=np.float32), mask, edges, tiles(cos), tiles(sin)], 1)
    return np.ascontiguousarray(table, np.float32)


def kernel(**inputs):
    import concourse.bacc as bacc
    from concourse.bass_utils import run_bass_kernel_spmd

    a = {k: np.asarray(v) for k, v in inputs.items()}
    chunks = lambda m: m.reshape(KC, P, -1)
    cols = lambda v: v.reshape(-1, P).T
    blocks = lambda w: w.reshape(w.shape[0] // P, P, w.shape[1] // P, P).transpose(2, 1, 0, 3)
    w_in = a["w_in"][0].reshape(KC, P, 7, KC, P)
    fm = w_in[:, :, [0, 3, 5, 6]].transpose(3, 2, 1, 0, 4).reshape(4 * KC, P, D)
    qkv = w_in[:, :, [4, 1, 2]].transpose(3, 1, 0, 2, 4).reshape(KC, P, 3 * D)
    lru_w = np.stack([a["lru_wa"][0], a["lru_wx"][0]]).reshape(4, KC, P, P).transpose(1, 2, 0, 3)
    lru_p = np.concatenate([a["lru_conv_w"][0], a["lru_conv_b"], a["lru_ba"][0], a["lru_bx"][0],
                            a["lru_lambda"][0]]).reshape(11, KC, P).transpose(2, 0, 1)
    rpb = np.zeros((16 * 16 + 1, P), np.float32)
    rpb[:-1].reshape(16, 16, P)[:, 1:, 48:79] = a["na_rpb"][0]
    up = blocks(a["w_up"][0]).reshape(2, FC, P, D)
    down = blocks(a["w_down"][0])
    units, j = [], 0
    for n in GROUPS:
        units.append(up[:, j:j + n].transpose(1, 0, 2, 3).reshape(2 * n, P, D))
        d = np.zeros((KC, P, KC, P), np.float32)
        d[:, :, 0:n] = down[:, :, j:j + n]
        units.append(d.reshape(KC, P, D))
        j += n
    conv = np.concatenate([a["ffn_conv_w"][0], a["ffn_conv_b"]]).reshape(4, 2, FC, P).transpose(3, 2, 1, 0)
    arrays = {
        "xT": chunks(a["x"][0].T), "ctxT": chunks(a["ctx"][0].T),
        "svec": np.stack([cols(a["c"][0]), cols(a["c_ctx"])], 2),
        "c_rows": np.stack([a["c"][0], a["c_ctx"]]), "w_mod": blocks(a["w_mod"][0])[0:KC],
        "w_scaleT": a["w_mod"][0][:, D:2 * D].T.reshape(KC, P, D),
        "w_modT": a["w_mod"][0][:, 2 * D:].T.reshape(4 * KC, P, D), "b_mod": cols(a["b_mod"][0]),
        "gains": np.stack([cols(a["norm_mix_g"][0]), cols(a["norm_ffn_g"][0])], 1),
        "w_fm": fm, "w_qkv": qkv, "lru_w": lru_w.reshape(KC, P, 4 * P), "lru_p": lru_p,
        "qk_g": np.stack([a["q_norm_g"][0], a["k_norm_g"][0]]), "rpb": rpb,
        "w_mix": np.concatenate([blocks(a[n][0]).reshape(KC, P, D) for n in ("w_rnn_out", "w_na_out", "w_out")]),
        "w_ff": np.concatenate(units), "ffn_p": conv.reshape(P, FC, 8), "consts": constants(),
    }
    arrays = {k: np.ascontiguousarray(v) for k, v in arrays.items()}
    nc = bacc.Bacc("TRN2", target_bir_lowering=False, num_devices=1, dynamic_dma_scratch_size=4096)
    aps = {k: nc.dram_tensor(k, v.shape, mybir.dt.from_np(v.dtype), kind="ExternalInput").ap()
           for k, v in arrays.items()}
    aps["outT"] = nc.dram_tensor("outT", (KC, P, T), F32, kind="ExternalOutput").ap()
    for k in ("yr_d", "yn_d", "smr_d", "smn_d"):
        aps[k] = nc.dram_tensor(k, (KC, P, T), F32, kind="Internal").ap()
    aps["bias_d"] = nc.dram_tensor("bias_d", (GW, 2 * PAIRS, 16, GW), F32, kind="Internal").ap()
    build(nc, **aps)
    r = run_bass_kernel_spmd(nc, [arrays], core_ids=[0])
    out = np.asarray(r.results[0]["outT"])
    return np.ascontiguousarray(out.reshape(D, T).T)[None]
```
